# Optimizing a Trainium2 kernel written in Bass

```python
import jax, jax.numpy as jnp
from jax import lax
import numpy as np

D_MODEL = 1024
BATCH = 1
SEQ = 1024
DEPTH = 1
DEC_BATCH = 8
DEC_SEQ = 8
PAST_LEN = 512
PAGE_SIZE = 128

HEAD_DIM = 64
N_FOX = 8
N_NSA = 8
N_NSA_KV = 2
NSA_GROUP = N_NSA // N_NSA_KV
D_FOX = N_FOX * HEAD_DIM
D_NSA = N_NSA * HEAD_DIM
D_MIX = D_FOX + D_NSA
D_NSA_KV = N_NSA_KV * HEAD_DIM
D_IN = 3 * D_FOX + N_FOX + D_NSA + 6 * D_NSA_KV + 3 * N_NSA
BLOCK = 64
N_SELECT = 16
WINDOW = 512
Q_BLOCK = 128
SLC_CHUNK = 32
D_FF = 4 * D_MODEL
ROPE_THETA = 500000.0
ROPE_DIM = HEAD_DIM // 4
EPS = 1e-6
SCALE = HEAD_DIM ** -0.5
NEG_INF = -1e30
FORCED_SCORE = 1e4

kernel_name = 'hymba_fox_nsa_adaln_decoder_step'

def _rmsnorm(x, g):
    xf = x.astype(jnp.float32)
    y = xf * lax.rsqrt(jnp.mean(xf * xf, axis=-1, keepdims=True) + EPS)
    return (y * g.astype(jnp.float32)).astype(x.dtype)

def _rope(x, pos):
    half = ROPE_DIM // 2
    inv = ROPE_THETA ** (-jnp.arange(half, dtype=jnp.float32) / half)
    ang = pos.astype(jnp.float32)[:, None] * inv[None, :]
    shape = (1, ang.shape[0]) + (1,) * (x.ndim - 3) + (half,)
    cos = jnp.cos(ang).reshape(shape)
    sin = jnp.sin(ang).reshape(shape)
    xr = x[..., :ROPE_DIM].astype(jnp.float32)
    x1, x2 = xr[..., :half], xr[..., half:]
    rot = jnp.concatenate([x1 * cos - x2 * sin, x2 * cos + x1 * sin], axis=-1).astype(x.dtype)
    return jnp.concatenate([rot, x[..., ROPE_DIM:]], axis=-1)

def _adaln(c, w_ada, b_ada):
    m = jax.nn.silu(c) @ w_ada + b_ada
    return [t[:, None, :] for t in jnp.split(m, 6, axis=-1)]

def _modulate(x, g, shift, scale):
    return _rmsnorm(x, g) * (1.0 + scale) + shift

def _chunks(a, axis, c):
    n = a.shape[axis] // c
    a = a.reshape(a.shape[:axis] + (n, c) + a.shape[axis + 1:])
    return jnp.moveaxis(a, axis, 0)

def _unchunk(a, axis):
    a = jnp.moveaxis(a, 0, axis)
    return a.reshape(a.shape[:axis] + (a.shape[axis] * a.shape[axis + 1],) + a.shape[axis + 2:])

def _pad_rows(a, n):
    return jnp.pad(a, ((0, 0), (0, n - a.shape[1])) + ((0, 0),) * (a.ndim - 2))

def _gather_pages(cache, page_table):
    g = cache[page_table]
    return g.reshape((g.shape[0], g.shape[1] * g.shape[2]) + g.shape[3:])

def _attend(q, k, v, mask, bias=None):
    s = jnp.einsum('btgnd,bkgd->bgntk', q, k, preferred_element_type=jnp.float32) * SCALE
    if bias is not None:
        s = s + bias
    p = jax.nn.softmax(jnp.where(mask, s, NEG_INF), axis=-1)
    return jnp.einsum('bgntk,bkgd->btgnd', p.astype(v.dtype), v, preferred_element_type=jnp.float32).astype(v.dtype)

def _window_mask(qpos, kpos):
    d = qpos[:, None] - kpos[None, :]
    return (d >= 0) & (d < WINDOW) & (kpos[None, :] >= 0)

def _project(h, lw, pos):
    B, T, _ = h.shape
    z = h @ lw['w_in']
    sizes = [D_FOX, D_FOX, D_FOX, N_FOX, D_NSA, 6 * D_NSA_KV, 3 * N_NSA]
    cuts = np.cumsum(sizes)[:-1].tolist()
    q_f, k_f, v_f, f_lin, q_n, kv_n, g_lin = jnp.split(z, cuts, axis=-1)
    q_f = _rmsnorm(q_f.reshape(B, T, N_FOX, HEAD_DIM), lw['g_q_fox'])
    k_f = _rmsnorm(k_f.reshape(B, T, N_FOX, HEAD_DIM), lw['g_k_fox'])
    v_f = v_f.reshape(B, T, N_FOX, HEAD_DIM)
    logf = jax.nn.log_sigmoid((f_lin + lw['b_forget']).astype(jnp.float32))
    q_n = _rope(_rmsnorm(q_n.reshape(B, T, N_NSA, HEAD_DIM), lw['g_q_nsa']), pos)
    kv_n = kv_n.reshape(B, T, 3, 2, N_NSA_KV, HEAD_DIM)
    k_n = _rope(_rmsnorm(kv_n[:, :, :, 0], lw['g_k_nsa'][:, None, :]), pos)
    v_n = kv_n[:, :, :, 1]
    gates = jax.nn.sigmoid(g_lin + lw['b_gate']).reshape(B, T, 3, N_NSA)
    return q_f, k_f, v_f, logf, q_n, k_n, v_n, gates

def _fox_prompt(q, k, v, logf):
    S = q.shape[1]
    C = jnp.cumsum(logf, axis=1)
    Ck = jnp.moveaxis(C, 1, 2)[:, :, None, None, :]
    kpos = jnp.arange(S)

    def blk(args):
        qb, cb, pb = args
        bias = jnp.moveaxis(cb, 1, 2)[:, :, None, :, None] - Ck
        return _attend(qb, k, v, kpos[None, :] <= pb[:, None], bias)

    o = lax.map(blk, (_chunks(q[:, :, :, None, :], 1, Q_BLOCK), _chunks(C, 1, Q_BLOCK), jnp.arange(S).reshape(-1, Q_BLOCK)))
    return _unchunk(o, 1)

def _fox_sample(q, k_past, v_past, k_new, v_new, logf_all, qpos):
    P = k_past.shape[1]
    C = jnp.cumsum(logf_all, axis=1)
    bias = jnp.transpose(C[:, P:], (0, 2, 1))[..., None] - jnp.transpose(C, (0, 2, 1))[:, :, None, :]
    s_past = jnp.einsum('bthd,bshd->bhts', q, k_past, preferred_element_type=jnp.float32)
    s_new = jnp.einsum('bthd,bshd->bhts', q, k_new, preferred_element_type=jnp.float32)
    s = jnp.concatenate([s_past, s_new], axis=-1) * SCALE + bias
    kpos = jnp.arange(C.shape[1])
    p = jax.nn.softmax(jnp.where(kpos[None, :] <= qpos[:, None], s, NEG_INF), axis=-1).astype(v_new.dtype)
    o = jnp.einsum('bhts,bshd->bthd', p[..., :P], v_past, preferred_element_type=jnp.float32)
    o = o + jnp.einsum('bhts,bshd->bthd', p[..., P:], v_new, preferred_element_type=jnp.float32)
    return o.astype(v_new.dtype)

def _compress(k, pe, w):
    B, Lp, G, D = k.shape
    kb = k.reshape(B, Lp // BLOCK, BLOCK, G, D) + pe[:, None, :]
    kb = jnp.transpose(kb, (0, 1, 3, 2, 4)).reshape(B, Lp // BLOCK, G, BLOCK * D)
    return kb @ w

def _blocks_by_group(a, nbs):
    B, _, G, D = a.shape
    return jnp.transpose(a.reshape(B, nbs, BLOCK, G, D), (0, 3, 1, 2, 4))

def _nsa_cmp_slc(qg, qpos, kc, vc, ks, vs, pe_cmp, w_cmp, chunk):
    L = kc.shape[1]
    nb = -(-L // BLOCK)
    nbs = max(nb, N_SELECT)
    k_cmp = _compress(_pad_rows(kc, nb * BLOCK), pe_cmp[0], w_cmp[0])
    v_cmp = _compress(_pad_rows(vc, nb * BLOCK), pe_cmp[1], w_cmp[1])
    blk = jnp.arange(nb)
    complete = (blk[None, :] + 1) * BLOCK <= qpos[:, None] + 1
    s = jnp.einsum('btgnd,bjgd->bgntj', qg, k_cmp, preferred_element_type=jnp.float32) * SCALE
    p = jax.nn.softmax(jnp.where(complete, s, NEG_INF), axis=-1)
    p = p * jnp.any(complete, axis=-1)[:, None]
    o_cmp = jnp.einsum('bgntj,bjgd->btgnd', p.astype(v_cmp.dtype), v_cmp, preferred_element_type=jnp.float32).astype(qg.dtype)
    imp = jnp.pad(jnp.sum(p, axis=2), ((0, 0), (0, 0), (0, 0), (0, nbs - nb)))
    blk_s = jnp.arange(nbs)[None, :]
    cur = (qpos // BLOCK)[:, None]
    imp = jnp.where((blk_s == cur) | (blk_s == 0), FORCED_SCORE, jnp.where(blk_s <= cur, imp, -1.0))
    vals, idx = lax.top_k(imp, N_SELECT)
    valid = vals >= 0.0
    ksT = _blocks_by_group(_pad_rows(ks, nbs * BLOCK), nbs)
    vsT = _blocks_by_group(_pad_rows(vs, nbs * BLOCK), nbs)
    gather = jax.vmap(jax.vmap(lambda a, i: a[i]))

    def sel(args):
        qb, ib, vb, pb = args
        kg = gather(ksT, ib)
        vg = gather(vsT, ib)
        kpos = ib[..., None] * BLOCK + jnp.arange(BLOCK)
        mask = vb[..., None] & (kpos <= pb[None, None, :, None, None])
        Bq, Gq, cq = ib.shape[:3]
        kg = kg.reshape(Bq, Gq, cq, N_SELECT * BLOCK, HEAD_DIM)
        vg = vg.reshape(Bq, Gq, cq, N_SELECT * BLOCK, HEAD_DIM)
        mask = mask.reshape(Bq, Gq, 1, cq, N_SELECT * BLOCK)
        sc = jnp.einsum('bcgnd,bgckd->bgnck', qb, kg, preferred_element_type=jnp.float32) * SCALE
        pr = jax.nn.softmax(jnp.where(mask, sc, NEG_INF), axis=-1)
        return jnp.einsum('bgnck,bgckd->bcgnd', pr.astype(vg.dtype), vg, preferred_element_type=jnp.float32).astype(vg.dtype)

    o_slc = _unchunk(lax.map(sel, (_chunks(qg, 1, chunk), _chunks(idx, 2, chunk), _chunks(valid, 2, chunk), qpos.reshape(-1, chunk))), 1)
    return o_cmp, o_slc

def _window_prompt(qg, kw, vw):
    S = qg.shape[1]
    pad = ((0, 0), (WINDOW, 0), (0, 0), (0, 0))
    kp = jnp.pad(kw, pad)
    vp = jnp.pad(vw, pad)
    span = WINDOW + Q_BLOCK

    def blk(args):
        qb, st = args
        kb = lax.dynamic_slice_in_dim(kp, st, span, axis=1)
        vb = lax.dynamic_slice_in_dim(vp, st, span, axis=1)
        qpos = st + jnp.arange(Q_BLOCK)
        kpos = st - WINDOW + jnp.arange(span)
        return _attend(qb, kb, vb, _window_mask(qpos, kpos))

    return _unchunk(lax.map(blk, (_chunks(qg, 1, Q_BLOCK), jnp.arange(S // Q_BLOCK) * Q_BLOCK)), 1)

def _finish(x, o_fox, gates, o_cmp, o_slc, o_win, gt1, sh2, sc2, gt2, lw):
    B, T, _ = x.shape
    g = gates.reshape(B, T, 3, N_NSA_KV, NSA_GROUP, 1).astype(o_cmp.dtype)
    o_nsa = (g[:, :, 0] * o_cmp + g[:, :, 1] * o_slc + g[:, :, 2] * o_win).reshape(B, T, D_NSA)
    mix = jnp.concatenate([o_fox.reshape(B, T, D_FOX), o_nsa], axis=-1) @ lw['w_out']
    x = x + gt1 * mix
    h = _modulate(x, lw['norm2_g'], sh2, sc2)
    u = jax.nn.relu(h @ lw['w_up'])
    return x + gt2 * ((u * u) @ lw['w_down'])

def _prompt_layer(x, c, lw):
    B, S, _ = x.shape
    pos = jnp.arange(S)
    sh1, sc1, gt1, sh2, sc2, gt2 = _adaln(c, lw['w_ada'], lw['b_ada'])
    h = _modulate(x, lw['norm1_g'], sh1, sc1)
    q_f, k_f, v_f, logf, q_n, k_n, v_n, gates = _project(h, lw, pos)
    o_fox = _fox_prompt(q_f, k_f, v_f, logf)
    qg = q_n.reshape(B, S, N_NSA_KV, NSA_GROUP, HEAD_DIM)
    o_cmp, o_slc = _nsa_cmp_slc(qg, pos, k_n[:, :, 0], v_n[:, :, 0], k_n[:, :, 1], v_n[:, :, 1], lw['pe_cmp'], lw['w_cmp'], SLC_CHUNK)
    o_win = _window_prompt(qg, k_n[:, :, 2], v_n[:, :, 2])
    y = _finish(x, o_fox, gates, o_cmp, o_slc, o_win, gt1, sh2, sc2, gt2, lw)
    wb = min(WINDOW, S)
    fox_kv = jnp.stack([k_f, v_f], axis=2)
    nsa_kv = jnp.stack([k_n[:, :, 0], v_n[:, :, 0], k_n[:, :, 1], v_n[:, :, 1]], axis=2)
    win = jnp.stack([k_n[:, S - wb:, 2], v_n[:, S - wb:, 2]], axis=2)
    return y, fox_kv, logf, nsa_kv, win

def _sample_layer(x, c, fox_kv_cache, fox_logf_cache, nsa_kv_cache, win_buf, page_table, lw):
    B, T, _ = x.shape
    qpos = PAST_LEN + jnp.arange(T)
    sh1, sc1, gt1, sh2, sc2, gt2 = _adaln(c, lw['w_ada'], lw['b_ada'])
    h = _modulate(x, lw['norm1_g'], sh1, sc1)
    q_f, k_f, v_f, logf, q_n, k_n, v_n, gates = _project(h, lw, qpos)
    past_fox = _gather_pages(fox_kv_cache, page_table)
    past_logf = _gather_pages(fox_logf_cache, page_table).astype(jnp.float32)
    o_fox = _fox_sample(q_f, past_fox[:, :, 0], past_fox[:, :, 1], k_f, v_f, jnp.concatenate([past_logf, logf], axis=1), qpos)
    past_nsa = _gather_pages(nsa_kv_cache, page_table)
    kc = jnp.concatenate([past_nsa[:, :, 0], k_n[:, :, 0]], axis=1)
    vc = jnp.concatenate([past_nsa[:, :, 1], v_n[:, :, 0]], axis=1)
    ks = jnp.concatenate([past_nsa[:, :, 2], k_n[:, :, 1]], axis=1)
    vs = jnp.concatenate([past_nsa[:, :, 3], v_n[:, :, 1]], axis=1)
    qg = q_n.reshape(B, T, N_NSA_KV, NSA_GROUP, HEAD_DIM)
    o_cmp, o_slc = _nsa_cmp_slc(qg, qpos, kc, vc, ks, vs, lw['pe_cmp'], lw['w_cmp'], 1)
    wb = win_buf.shape[1]
    kw = jnp.concatenate([win_buf[:, :, 0], k_n[:, :, 2]], axis=1)
    vw = jnp.concatenate([win_buf[:, :, 1], v_n[:, :, 2]], axis=1)
    kpos = PAST_LEN - wb + jnp.arange(wb + T)
    o_win = _attend(qg, kw, vw, _window_mask(qpos, kpos))
    y = _finish(x, o_fox, gates, o_cmp, o_slc, o_win, gt1, sh2, sc2, gt2, lw)
    fox_kv = jnp.stack([k_f, v_f], axis=2)
    nsa_kv = jnp.stack([k_n[:, :, 0], v_n[:, :, 0], k_n[:, :, 1], v_n[:, :, 1]], axis=2)
    win = jnp.stack([kw[:, T:], vw[:, T:]], axis=2)
    return y, fox_kv, logf, nsa_kv, win

def setup_inputs(seed: int = 0) -> dict:
    key = jax.random.key(seed)
    ks = jax.random.split(key, 32)
    n_pages = PAST_LEN // PAGE_SIZE
    n_used = DEC_BATCH * n_pages
    n_pool = (5 * n_used + 3) // 4
    wb_s = min(WINDOW, PAST_LEN)
    nrm = jax.random.normal
    f32 = jnp.float32
    page_table = jax.random.permutation(ks[0], n_pool)[:n_used].reshape(DEC_BATCH, n_pages).astype(jnp.int32)
    return {
        'x_prompt': nrm(ks[1], (BATCH, SEQ, D_MODEL), f32),
        'x_sample': nrm(ks[2], (DEC_BATCH, DEC_SEQ, D_MODEL), f32),
        'c_prompt': nrm(ks[3], (BATCH, D_MODEL), f32),
        'c_sample': nrm(ks[4], (DEC_BATCH, D_MODEL), f32),
        'cache_fox_kv': nrm(ks[5], (DEPTH, n_pool, PAGE_SIZE, 2, N_FOX, HEAD_DIM), f32),
        'cache_fox_logf': jax.nn.log_sigmoid(4.0 + 0.5 * nrm(ks[6], (DEPTH, n_pool, PAGE_SIZE, N_FOX), f32)),
        'cache_nsa_kv': nrm(ks[7], (DEPTH, n_pool, PAGE_SIZE, 4, N_NSA_KV, HEAD_DIM), f32),
        'state_nsa_win': nrm(ks[8], (DEPTH, DEC_BATCH, wb_s, 2, N_NSA_KV, HEAD_DIM), f32),
        'page_table': page_table,
        'w_ada': nrm(ks[9], (DEPTH, D_MODEL, 6 * D_MODEL), f32) * (0.5 * D_MODEL ** -0.5),
        'b_ada': 0.02 * nrm(ks[10], (DEPTH, 6 * D_MODEL), f32),
        'norm1_g': 1.0 + 0.02 * nrm(ks[11], (DEPTH, D_MODEL), f32),
        'norm2_g': 1.0 + 0.02 * nrm(ks[12], (DEPTH, D_MODEL), f32),
        'w_in': nrm(ks[13], (DEPTH, D_MODEL, D_IN), f32) * D_MODEL ** -0.5,
        'b_forget': 4.0 + 0.5 * nrm(ks[14], (DEPTH, N_FOX), f32),
        'b_gate': 0.02 * nrm(ks[15], (DEPTH, 3 * N_NSA), f32),
        'g_q_fox': 1.0 + 0.02 * nrm(ks[16], (DEPTH, HEAD_DIM), f32),
        'g_k_fox': 1.0 + 0.02 * nrm(ks[17], (DEPTH, HEAD_DIM), f32),
        'g_q_nsa': 1.0 + 0.02 * nrm(ks[18], (DEPTH, HEAD_DIM), f32),
        'g_k_nsa': 1.0 + 0.02 * nrm(ks[19], (DEPTH, 3, HEAD_DIM), f32),
        'pe_cmp': 0.1 * nrm(ks[20], (DEPTH, 2, BLOCK, HEAD_DIM), f32),
        'w_cmp': nrm(ks[21], (DEPTH, 2, BLOCK * HEAD_DIM, HEAD_DIM), f32) * (BLOCK * HEAD_DIM) ** -0.5,
        'w_out': nrm(ks[22], (DEPTH, D_MIX, D_MODEL), f32) * D_MIX ** -0.5,
        'w_up': nrm(ks[23], (DEPTH, D_MODEL, D_FF), f32) * D_MODEL ** -0.5,
        'w_down': nrm(ks[24], (DEPTH, D_FF, D_MODEL), f32) * D_FF ** -0.5,
    }

def reference(x_prompt, x_sample, c_prompt, c_sample, cache_fox_kv, cache_fox_logf, cache_nsa_kv, state_nsa_win, page_table, w_ada, b_ada, norm1_g, norm2_g, w_in, b_forget, b_gate, g_q_fox, g_k_fox, g_q_nsa, g_k_nsa, pe_cmp, w_cmp, w_out, w_up, w_down):
    xp, xs = x_prompt, x_sample
    fkv_p, flf_p, nkv_p, win_p = [], [], [], []
    fkv_s, flf_s, nkv_s, win_s = [], [], [], []
    for l in range(DEPTH):
        lw = dict(w_ada=w_ada[l], b_ada=b_ada[l], norm1_g=norm1_g[l], norm2_g=norm2_g[l], w_in=w_in[l], b_forget=b_forget[l], b_gate=b_gate[l], g_q_fox=g_q_fox[l], g_k_fox=g_k_fox[l], g_q_nsa=g_q_nsa[l], g_k_nsa=g_k_nsa[l], pe_cmp=pe_cmp[l], w_cmp=w_cmp[l], w_out=w_out[l], w_up=w_up[l], w_down=w_down[l])
        xp, a, b, cc, d = _prompt_layer(xp, c_prompt, lw)
        fkv_p.append(a); flf_p.append(b); nkv_p.append(cc); win_p.append(d)
        xs, a, b, cc, d = _sample_layer(xs, c_sample, cache_fox_kv[l], cache_fox_logf[l], cache_nsa_kv[l], state_nsa_win[l], page_table, lw)
        fkv_s.append(a); flf_s.append(b); nkv_s.append(cc); win_s.append(d)
    return (xp, xs, jnp.stack(fkv_p), jnp.stack(fkv_s), jnp.stack(flf_p), jnp.stack(flf_s), jnp.stack(nkv_p), jnp.stack(nkv_s), jnp.stack(win_p), jnp.stack(win_s))


_drawn_inputs = setup_inputs


def setup_inputs(seed=0):
    import zlib

    import numpy as np

    out = dict(_drawn_inputs(seed))
    spreads = {}
    factors = {'cache_fox_logf': 115.555,
     'norm1_g': 2.931,
     'norm2_g': 6.443,
     'b_gate': 38.845,
     'g_q_fox': 8.0,
     'g_k_fox': 4.186,
     'g_q_nsa': 8.0,
     'g_k_nsa': 4.112,
     'pe_cmp': 4.757}
    for name, (base, spread) in spreads.items():
        noise = np.random.default_rng([zlib.crc32(name.encode()), seed]).standard_normal(out[name].shape)
        drawn = base * np.exp(spread * noise) if base else spread * noise
        out[name] = __import__('jax').numpy.asarray(drawn.astype(out[name].dtype))
    for name, factor in factors.items():
        out[name] = (out[name] * factor).astype(out[name].dtype)
    return out
```

```python
import numpy as np

import concourse.bass as bass
from concourse import mybir

F32 = mybir.dt.float32
I32 = mybir.dt.int32
ALU = mybir.AluOpType
ACT = mybir.ActivationFunctionType
AX = mybir.AxisListType

P = 128
D = 1024
KC = D // P
NT = 8
T9 = NT + 1
S = NT * P
B, TQ = 8, 8
NS = B * TQ
TOK = S + NS
HD = 64
NH = 8
G = 2
PAST = 512
PAGES = PAST // P
L = PAST + TQ
BLOCK = 64
NBP = S // BLOCK
NBS = PAST // BLOCK
DFF = 4096
FC = DFF // P
EPS = 1e-6
SCALE = HD ** -0.5
NEG = -1e30
CREDIT = 1
EXP_MAX = 88.0

C_QF, C_KF, C_VF, C_F, C_QN, C_KV = 0, 512, 1024, 1536, 1544, 2056
C_WIN = C_KV + 512
N_MISC = 256 + 24
ZB = ["misc", "kf", "vf", "qf", "qn", "cs"]
ZW = {"misc": N_MISC + 8, "kf": 512, "vf": 512, "qf": 512, "qn": 512, "cs": 512}
ZC = {"kf": C_KF, "vf": C_VF, "qf": C_QF, "qn": C_QN, "cs": C_KV}

K_ID, K_U, K_ONE, K_CAUS, K_WIN, K_CMP, K_ANY = 0, 128, 256, 384, 512, 640, 768
K_COS, K_SIN, K_SELP, K_SELS, K_NEW, K_OLD = 769, 913, 1057, 1185, 1249, 1257
K_N = 1265


def constants():
    c = np.zeros((P, K_N), np.float32)
    p = np.arange(P)[:, None]
    f = np.arange(P)[None, :]
    c[:, K_ID:K_ID + P] = p == f
    c[:, K_U:K_U + P] = p <= f
    c[:, K_ONE:K_ONE + P] = 1
    c[:, K_CAUS:K_CAUS + P] = np.where(f <= p, 0, NEG)
    c[:, K_WIN:K_WIN + P] = np.where(f > p, 0, NEG)
    for t in range(NT):
        blk = np.arange(NBP)[None, :]
        c[:, K_CMP + NBP * t:K_CMP + NBP * (t + 1)] = np.where((blk + 1) * BLOCK <= t * P + p + 1, 0, NEG)
    c[:, K_ANY] = (np.arange(P) + 1 >= BLOCK)
    half = 8
    inv = (np.float32(500000.0) ** (-np.arange(half, dtype=np.float32) / np.float32(half))).astype(np.float32)
    for t in range(T9):
        pos = t * P + np.arange(P) if t < NT else PAST + np.arange(P) % TQ
        ang = pos.astype(np.float32)[:, None] * inv[None, :]
        co, si = np.cos(ang), np.sin(ang)
        c[:, K_COS + 16 * t:K_COS + 16 * t + 16] = np.concatenate([co, co], 1)
        c[:, K_SIN + 16 * t:K_SIN + 16 * t + 16] = np.concatenate([-si, si], 1)
    c[0, K_SELP:K_SELP + P] = 1
    for b in range(B):
        c[b + 1, K_SELS + b * TQ:K_SELS + (b + 1) * TQ] = 1
    q, k = (np.arange(HD) % TQ)[:, None], np.arange(TQ)[None, :]
    c[:HD, K_NEW:K_NEW + TQ] = np.where(k <= q, 0, NEG)
    c[:HD, K_OLD:K_OLD + TQ] = np.where(k > q, 0, NEG)
    return c


class Chain:

    def __init__(self, eng, sem):
        self.eng, self.sem = eng, sem
        self.base, self.k, self.reg, self.per = 0, 0, None, 0

    def loop(self, reg, per):
        self.base += self.k
        self.k, self.reg, self.per = 0, reg, per

    def end(self, times):
        assert self.k == self.per, ("steps in the loop", self.k, self.per)
        self.base, self.k, self.reg = self.base + times * self.per, 0, None

    def link(self, ins):
        self.k += 1
        ins.then_inc(self.sem, 1)
        n = self.base + self.k
        self.eng.wait_ge(self.sem, n if self.reg is None else self.reg * self.per + n)


def rows(t):
    return P if t < NT else NS


def attention_units(kinds):
    out = []
    for t in range(NT):
        for kind in kinds:
            if kind == "cmp":
                out.append((kind, t, 0, 1))
            elif kind == "win":
                lo = max(0, t - 4)
                out.append((kind, t, lo, t + 1 - lo))
            else:
                out.append((kind, t, 0, t + 1))
    return out


def layer_kernel(nc, x_prompt, x_sample, c_prompt, c_sample, cache_fox_kv, cache_fox_logf, cache_nsa_kv,
                 state_nsa_win, page_table, w_ada, b_ada, norm1_g, norm2_g, w_in, b_forget, b_gate,
                 g_q_fox, g_k_fox, g_q_nsa, g_k_nsa, pe_cmp, w_cmp, w_out, w_up, w_down, consts,
                 y_p, y_s, fkv_p, fkv_s, flf_p, flf_s, nkv_p, nkv_s, win_p, win_s):
    n_pool = cache_fox_kv.shape[1]
    xp_v = x_prompt.rearrange("a (t p) d -> p (a t) d", p=P)
    xs_v = x_sample.rearrange("b t d -> (b t) d")
    wada_v = w_ada.rearrange("a (k p) n -> p (a k) n", p=P)
    win_v = w_in.rearrange("a (k p) n -> p (a k) n", p=P)
    wout_v = w_out.rearrange("a (k p) n -> p (a k) n", p=P)
    wup_v = w_up.rearrange("a (k p) n -> p (a k) n", p=P)
    wdn_v = w_down.rearrange("a (f p) n -> p (a f) n", p=P)
    cfox_v = cache_fox_kv.rearrange("a n p k h d -> (a n) p (k h d)")
    clf_v = cache_fox_logf.rearrange("a n p h -> (a n) p h")
    cnsa_v = cache_nsa_kv.rearrange("a n p k g d -> (a n) p (k g d)")
    stw_v = state_nsa_win.rearrange("a b (j p) k g d -> (a b) p j (k g d)", p=P)
    stw_rows = state_nsa_win.rearrange("a b s k g d -> (a b) s (k g d)")
    fkvp_v = fkv_p.rearrange("a b (t p) k h d -> (a b t) p k (h d)", p=P)
    fkvs_v = fkv_s.rearrange("a b t k h d -> (a b t) k (h d)")
    fkvs_b = fkv_s.rearrange("a b t k h d -> (a b) t (k h d)")
    nkvp_v = nkv_p.rearrange("a b (t p) k g d -> (a b t) p (k g d)", p=P)
    nkvs_v = nkv_s.rearrange("a b t k g d -> (a b t) (k g d)")
    nkvs_b = nkv_s.rearrange("a b t k g d -> (a b) t (k g d)")
    winp_v = win_p.rearrange("a b (t p) k g d -> (a b t) p (k g d)", p=P)
    wins_v = win_s.rearrange("a b s k g d -> (a b) s (k g d)")
    flfs_b = flf_s.rearrange("a b t h -> (a b) t h")
    yp_v = y_p.rearrange("a (t p) d -> p (a t) d", p=P)
    ys_v = y_s.rearrange("b t d -> (b t) d")
    qt_d = nc.dram_tensor("qt_scratch", [2, NH, HD, S], F32, kind="Internal").ap()
    qs_d = nc.dram_tensor("qs_scratch", [NS, D], F32, kind="Internal").ap()
    gs_d = nc.dram_tensor("gs_scratch", [NS, 24], F32, kind="Internal").ap()
    mixs_d = nc.dram_tensor("mixs_scratch", [NS, D], F32, kind="Internal").ap()
    x1_d = nc.dram_tensor("x1_scratch", [TOK, D], F32, kind="Internal").ap()

    ARENA = 16640

    def at(name, shape, off, dt=F32):
        return nc.alloc_sbuf_tensor_at(name, shape, dt, offset=ARENA + off)

    small = [0]

    def keep(name, shape, dt=F32):
        n = 4
        for s in shape[1:]:
            n *= s
        off = small[0]
        small[0] += (n + 31) // 32 * 32
        return at(name, shape, off, dt)

    cst = keep("cst", [P, K_N])
    modT = keep("modT", [P, 6 * KC, B + 1])
    vecT = keep("vecT", [P, HD])
    gain1 = keep("gain1", [P, KC, B + 1])
    gain2 = keep("gain2", [P, KC, B + 1])
    gates = keep("gates", [P, T9, 24])
    logf = keep("logf", [P, T9, NH])
    ssum = keep("ssum", [P, 16])
    rstd = keep("rstd", [P, 16])
    gate_qk = keep("gate_qk", [P, 2, 4])
    nmax = keep("nmax", [P, 2, 4])
    scT = keep("scT", [P, KC, B + 1])
    ptab = keep("ptab", [1, B * PAGES], I32)
    kcS = keep("kcS", [P, B * NBS])
    kcP = keep("kcP", [HD + 1, G, NBP])
    vcP = keep("vcP", [P, G, HD + 1])
    gateS = keep("gateS", [HD, 3, B])
    SMALL = small[0]
    assert SMALL <= 14336, SMALL
    KV = 14336
    kTf = at("kTf", [HD + 1, NH, S], KV)
    Vf = at("Vf", [P, NT, NH, HD + 1], KV + 32768)
    kTs = at("kTs", [HD + 1, G, S], KV + 49408)
    kTw = at("kTw", [HD + 1, G, S], KV + 57600)
    Vs = at("Vs", [P, NT, G, HD + 1], KV + 65792)
    Vw = at("Vw", [P, NT, G, HD + 1], KV + 69952)
    XC = 88448
    Xc = at("Xc", [P, NBP + B * NBS, 2, BLOCK], XC)
    HT = 96640
    hT = at("hT", [P, KC, TOK], HT)
    WB = 131456
    wbuf = [at(f"wbuf{i}", [P, KC, 512], WB + 16384 * i) for i in range(3)]
    ST = WB + 3 * 16384
    zsb = [at(f"zsb{i}", [P, 512], ST + 2048 * i) for i in range(5)]
    sq = [at(f"sq{i}", [P, 512], ST + 10240 + 2048 * i) for i in range(2)]
    qst = [at(f"qst{i}", [HD, NH, P], ST + 14336 + 4096 * i) for i in range(2)]
    rope = [at(f"rope{i}", [P, NH, 16], ST + 22528 + 512 * i) for i in range(2)]
    EXTRA = ST + 23552
    gvec = at("gvec", [P, 6, HD], EXTRA)
    hv = [at(f"hv{i}", [P, 3, NH], EXTRA + 1536 + 96 * i) for i in range(3)]
    graw = at("graw", [P, T9, 32], EXTRA + 1824)
    gexp = at("gexp", [P, T9, 32], EXTRA + 2976)
    bias32 = at("bias32", [P, 32], EXTRA + 4128)
    peT = at("peT", [P, 2, BLOCK], EXTRA + 4256)
    csum = at("csum", [P, NT, NH], EXTRA + 4768)
    cpre = at("cpre", [P, NT, NH], EXTRA + 5024)
    nCT = at("nCT", [HD, P], EXTRA + 5280)
    lnv = at("lnv", [P, T9, NH], EXTRA + 5792)
    assert ARENA + EXTRA + 6080 <= 229344
    xb = at("xb", [P, T9, D], KV)
    c9 = at("c9", [B + 1, D], KV + 36864)
    c9e = at("c9e", [B + 1, D], KV + 40960)
    vecn = at("vecn", [HD, P], KV + 45056)
    pen = at("pen", [BLOCK, 2, 2, HD], KV + 45568)
    junk = at("junk", [P, D], KV + 46592)
    cpage = [at(f"cpage{i}", [P, PAGES, 256], WB + 4096 * i) for i in range(2)]
    wbd = [at(f"wbd{i}", [P, 2, 8, P], WB + 8192 + 8192 * i) for i in range(2)]
    kvcT = at("kvcT", [P, 2, NBP + B * NBS], WB + 24576)
    vcS = at("vcS", [NBS, B, P], XC + 25088)
    qT = [at(f"qT{i}", [HD + 1, S], XC + 4096 * i) for i in range(2)]
    prob = [at(f"prob{i}", [P, S], XC + 8192 + 4096 * i) for i in range(2)]
    probT = [at(f"probT{i}", [P, NT, P], XC + 16384 + 4096 * i) for i in range(2)]
    mix = at("mix", [P, T9, D], WB)
    fpage = [at(f"fpage{i}", [P, PAGES, D], KV + 16384 * i) for i in range(2)]
    npage = [at(f"npage{i}", [P, PAGES, 256], KV + 32768 + 4096 * i) for i in range(2)]
    wpage = [at(f"wpage{i}", [P, PAGES, 256], KV + 40960 + 4096 * i) for i in range(2)]
    o = KV + 49152
    lpage, fnew, nnew, wnew, qrow, lnew, vcb = [], [], [], [], [], [], []
    for i in range(2):
        fnew.append(at(f"fnew{i}", [TQ, D], o)); o += 4096
        qrow.append(at(f"qrow{i}", [TQ, D], o)); o += 4096
        nnew.append(at(f"nnew{i}", [TQ, 256], o)); o += 1024
        wnew.append(at(f"wnew{i}", [TQ, 256], o)); o += 1024
        lpage.append(at(f"lpage{i}", [P, PAGES, NH], o)); o += 128
        lnew.append(at(f"lnew{i}", [TQ, NH], o)); o += 32
        vcb.append(at(f"vcb{i}", [NBS, P], o)); o += 512
    assert o <= KV + 74112
    KTf = [at(f"KTf{i}", [P, 4, L], XC + 8320 * i) for i in range(2)]
    KTn = [at(f"KTn{i}", [P, 2, L], XC + 16640 + 4160 * i) for i in range(2)]
    o = WB + 36864
    sc, scc, negc, lf64, Qf, Qn, PTb, PTs, ofs, ons, srow, csa = ([] for _ in range(12))
    for i in range(2):
        sc.append(at(f"sc{i}", [HD, 3, L], o)); o += 6240
        scc.append(at(f"scc{i}", [HD, NBS], o)); o += 32
        negc.append(at(f"negc{i}", [HD, L], o)); o += 2080
        lf64.append(at(f"lf64{i}", [P, PAGES + 1, NH, TQ], o)); o += 1280
        Qf.append(at(f"Qf{i}", [P, 320], o)); o += 1280
        Qn.append(at(f"Qn{i}", [P, HD], o)); o += 256
        PTb.append(at(f"PTb{i}", [P, 3, PAGES, HD], o)); o += 3072
        PTs.append(at(f"PTs{i}", [TQ, 4, HD], o)); o += 1024
        ofs.append(at(f"ofs{i}", [TQ, 512], o)); o += 2048
        ons.append(at(f"ons{i}", [32, G, HD], o)); o += 512
        srow.append(at(f"srow{i}", [HD, 4, 4], o)); o += 64
    ones512 = at("ones512", [HD, PAST], o); o += 2048
    assert ARENA + o <= 229344, o
    h2T = at("h2T", [P, KC, TOK], KV)
    wo = at("wo", [P, KC, D], KV + 34816)
    o = KV + 34816 + 32768
    mixT = [at(f"mixT{i}", [P, KC, P], o + 4096 * i) for i in range(2)]; o += 8192
    xt = [at(f"xt{i}", [P, D], o + 4096 * i) for i in range(2)]; o += 8192
    x1 = [at(f"x1{i}", [P, D], o + 4096 * i) for i in range(2)]; o += 8192
    xn = [at(f"xn{i}", [P, D], o + 4096 * i) for i in range(2)]; o += 8192
    junk2 = at("junk2", [P, D], o); o += 4096
    gt1n = at("gt1n", [B + 1, D], o); o += 4096
    gt1b = at("gt1b", [P, 2, D], o); o += 8192
    assert o <= WB
    u2T = at("u2T", [P, FC, TOK], KV + 34816)
    wu = [at(f"wu{i}", [P, KC, 256], KV + 34816 + 139264 + 8192 * i) for i in range(2)]
    wd = [at(f"wd{i}", [P, FC, P], KV + 16384 * i) for i in range(2)]
    o = KV + 34816 + 139264
    yT = [at(f"yT{i}", [P, TOK], o + 4352 * i) for i in range(2)]; o += 8704
    xc = [at(f"xc{i}", [P, T9, P], o + 4608 * i) for i in range(2)]; o += 9216
    assert ARENA + o <= 229344

    bank = nc.alloc_psum_tensor("bank", [P, 8, 512], F32)
    bk = [bank[:, i, :] for i in range(8)]

    def banks(i, n):
        return bank[:, i:i + n, :].rearrange("p a b -> p (a b)")

    sem = nc.alloc_semaphore

    ident = cst[:, K_ID:K_ID + P]

    s_const, s_c, s_vec, s_gvec, s_pe, s_pt = (sem(n) for n in (
        "const_loaded", "c_loaded", "vec_loaded", "gvec_loaded", "pe_loaded", "ptab_loaded"))
    s_x = [sem(f"x_loaded{i}") for i in range(3)]
    w_ld = [sem(f"w_loaded{i}") for i in range(3)]
    c_neg, c_exp, c_silu, t0_ready, sc_ready = (sem(n) for n in (
        "c_negated", "c_exp_done", "c_silu_done", "small_transposed", "small_copied"))
    ln_sq, ln_var, ln_root, xn_done, ln_t, ln_ea, ln_ed = (sem(n) for n in (
        "ln_squares", "ln_variance", "ln_root", "xn_ready", "ln_transposed", "ln_copied_act", "ln_copied_dve"))
    ada_ready, ada_ev, mod_ready, mod_a, mod_d = (sem(n) for n in (
        "ada_ready", "ada_stored", "gain_ready", "h_act", "h_dve"))
    z_ready, z_ev, z_var, z_root, z_scaled, pool_done, tz_ready, tz_a, tz_d = (sem(n) for n in (
        "z_ready", "z_copied", "z_variance", "z_root", "z_scaled", "z_normed", "z_transposed",
        "zt_copied_act", "zt_copied_dve"))
    z_st = [sem(f"z_stored{i}") for i in range(5)]
    q_st = [sem(f"qt_stored{i}") for i in range(2)]
    misc_set, kv_set, g_arg, g_exp, g_one, g_ln, g_done = (sem(n) for n in (
        "misc_cleared", "kv_ones_set", "gate_args", "gate_exps", "gate_ones", "gate_logs", "gates_done"))
    c_ready, c_neg2, ct_ready, ct_copied, ct_moved = (sem(n) for n in (
        "csum_ready", "csum_negated", "csum_transposed", "csum_copied", "csum_moved"))
    misc_st, copy_st = sem("logf_stored"), sem("window_copied")
    dve_a, pool_a = sem("dve_step_a"), sem("pool_step_a")
    phase1_sems = [s_const, s_c, s_vec, s_gvec, s_pe, *s_x, *w_ld, c_neg, c_exp, c_silu, t0_ready, sc_ready, ln_sq, ln_var,
                   ln_root, xn_done, ln_t, ln_ea, ln_ed, ada_ready, ada_ev, mod_ready, mod_a, mod_d, z_ready, z_ev, z_var,
                   z_root, z_scaled, pool_done, tz_ready, tz_a, tz_d, *z_st, *q_st, misc_set, kv_set, g_arg, g_exp, g_one,
                   g_ln, g_done, c_ready, c_neg2, ct_ready, ct_copied, ct_moved, misc_st, copy_st, dve_a, pool_a]

    jobs = [(b, t) for b in range(len(ZB)) for t in range(T9)]
    NJ = len(jobs)
    LAG = 2
    tz_index, tz_eng = {}, []
    for J, (b, t) in enumerate(jobs):
        if t < NT and ZB[b] != "vf":
            tz_index[J] = len(tz_eng)
            tz_eng.append("d" if ZB[b] == "cs" else "a")
    tz_order = [tz_eng[:i + 1].count(e) for i, e in enumerate(tz_eng)]
    q_index = {J: i for i, J in enumerate(J for J in tz_index if ZB[jobs[J][0]] in ("qf", "qn"))}
    normed = [J for J, (b, t) in enumerate(jobs) if ZB[b] != "vf"]
    n_index = {J: i for i, J in enumerate(normed)}
    pool_jobs = [J for J, (b, t) in enumerate(jobs) if not (ZB[b] == "vf" and t == NT)]
    pool_count = [sum(j <= J for j in pool_jobs) for J in range(NJ)]
    ada1 = 4
    ada_after = [4, 13, 22, 26, 31, 35, 40, 49]
    csum_after = 12
    loads01 = {0: [1, 1, 2, 1, 1], 1: [1, 1, 1, 1, 1]}

    def loaded(buf, item):
        return 16 * sum(loads01[buf][:item + 1])

    def z_stores(J):
        b, t = jobs[J]
        name, z, r = ZB[b], zsb[J % 5], rows(t)
        if name == "misc":
            if t == NT:
                return [(wins_v[q, PAST - TQ:PAST, :], z[q * TQ:(q + 1) * TQ, 0:256]) for q in range(B)]
            return [(winp_v[t - 4, :, :], z[:, 0:256])] if t >= 4 else []
        if name in ("kf", "vf"):
            i = int(name == "vf")
            return [(fkvs_v[:, i, :] if t == NT else fkvp_v[t, :, i, :], z[0:r, :])]
        if name in ("qf", "qn"):
            i = int(name == "qn")
            return [(qs_d[:, 512 * i:512 * (i + 1)], z[0:NS, :])] if t == NT else []
        return [(nkvs_v if t == NT else nkvp_v[t, :, :], z[0:r, :])]

    def stored(J):
        return 16 * sum(len(z_stores(j)) for j in range(J + 1) if j % 5 == J % 5)

    def k_heads(name, z, r, w):
        if name == "cs":
            return z[0:r, :].rearrange("p (a k h d) -> p a k h d", a=2, k=2, h=G)[:, :, 0, :, 0:w]
        n = G if name == "misc" else NH
        return z[0:r, 0:n * HD].rearrange("p (h d) -> p h d", d=HD)[:, :, 0:w]

    with nc.Block() as block:

        @block.sync
        def _(sp):
            sp.dma_start(c9[0:1, :], c_prompt).then_inc(s_c, 16)
            sp.dma_start(c9[1:B + 1, :], c_sample).then_inc(s_c, 16)
            sp.dma_start(vecn[0:48, :], b_ada.rearrange("a (n p) -> (a n) p", p=P)).then_inc(s_vec, 16)
            sp.dma_start(vecn[48:56, :], norm1_g.rearrange("a (n p) -> (a n) p", p=P)).then_inc(s_vec, 16)
            sp.dma_start(vecn[56:64, :], norm2_g.rearrange("a (n p) -> (a n) p", p=P)).then_inc(s_vec, 16)
            sp.dma_start(cst[:, :], consts).then_inc(s_const, 16)
            sp.dma_start(xb[:, 0:4, :], xp_v[:, 0:4, :]).then_inc(s_x[0], 16)
            sp.dma_start(wbuf[0][:, :, :], wada_v[:, :, 0:512]).then_inc(w_ld[0], 16)
            sp.dma_start(xb[:, 4:8, :], xp_v[:, 4:8, :]).then_inc(s_x[1], 16)
            sp.dma_start(xb[0:NS, NT, :], xs_v).then_inc(s_x[2], 16)
            for i in range(2):
                sp.dma_start(pen[:, :, i, :], pe_cmp.rearrange("a k p d -> p (a k) d")).then_inc(s_pe, 16)
            sp.dma_start(wbuf[1][:, :, :], wada_v[:, :, 512:1024]).then_inc(w_ld[1], 16)
            for i, g in enumerate((g_q_fox, g_k_fox, g_q_nsa)):
                sp.dma_start(gvec[:, i, :], g[0, :].partition_broadcast(P)).then_inc(s_gvec, 16)
            sp.dma_start(gvec[:, 3:6, :], g_k_nsa[0, :, :].partition_broadcast(P)).then_inc(s_gvec, 16)
            sp.dma_start(bias32[:, 0:24], b_gate[0, :].partition_broadcast(P)).then_inc(s_gvec, 16)
            sp.dma_start(bias32[:, 24:32], b_forget[0, :].partition_broadcast(P)).then_inc(s_gvec, 16)
            sp.dma_start(ptab[:, :], page_table.rearrange("b (o j) -> o (b j)", o=1)).then_inc(s_pt, 16)
            for n in (2, 3):
                sp.wait_ge(ada_ready, n - 1)
                sp.dma_start(wbuf[n % 2][:, :, :], wada_v[:, :, 512 * n:512 * (n + 1)]).then_inc(w_ld[n % 2], 16)

            def load_z(b):
                if b == 0:
                    sp.wait_ge(ada_ready, 3)
                    sp.dma_start(wbuf[0][:, :, 0:N_MISC], win_v[:, :, C_WIN:C_WIN + N_MISC]).then_inc(w_ld[0], 16)
                    sp.dma_start(wbuf[0][:, :, N_MISC:N_MISC + 8], win_v[:, :, C_F:C_F + 8]).then_inc(w_ld[0], 16)
                    return
                if b == 1:
                    sp.wait_ge(ada_ready, 4)
                else:
                    sp.wait_ge(z_ready, T9 * (b - 1))
                c = ZC[ZB[b]]
                sp.dma_start(wbuf[b % 2][:, :, :], win_v[:, :, c:c + 512]).then_inc(w_ld[b % 2], 16)

            def load_ada(i):
                if i:
                    sp.wait_ge(ada_ready, ada1 + i)
                n = ada1 + i
                sp.dma_start(wbuf[2][:, :, :], wada_v[:, :, 512 * n:512 * (n + 1)]).then_inc(w_ld[2], 16)

            load_z(0)
            load_ada(0)
            for J in range(NJ + LAG):
                if J < NJ and jobs[J][1] == 0 and jobs[J][0] + 1 < len(ZB):
                    load_z(jobs[J][0] + 1)
                if J - 2 in ada_after and ada_after.index(J - 2) + 1 < len(ada_after):
                    load_ada(ada_after.index(J - 2) + 1)
                K = J - LAG
                if K < 0:
                    continue
                if z_stores(K):
                    if K in pool_jobs:
                        sp.wait_ge(pool_done, pool_count[K])
                    else:
                        sp.wait_ge(z_ev, K + 1)
                    for dst, src in z_stores(K):
                        sp.dma_start(dst, src).then_inc(z_st[K % 5], 16)
                if K in q_index:
                    i, t = q_index[K], jobs[K][1]
                    sp.wait_ge(tz_a, tz_order[tz_index[K]])
                    sp.dma_start(qt_d[i // NT, :, :, t * P:(t + 1) * P].rearrange("h d t -> d h t"),
                                 qst[i % 2][:, :, :]).then_inc(q_st[i % 2], 16)
                if K == csum_after + 3:
                    sp.wait_ge(g_done, 1)
                    sp.dma_start(flf_p.rearrange("a b (t p) h -> p (a b t) h", p=P), logf[:, 0:NT, :]).then_inc(misc_st, 16)
                    sp.dma_start(flf_s.rearrange("a b t h -> (a b t) h"), logf[0:NS, NT, :]).then_inc(misc_st, 16)
                    sp.dma_start(gs_d, gates[0:NS, NT, :]).then_inc(misc_st, 16)
                    sp.wait_ge(ct_copied, 1)
                    for t in range(NT):
                        sp.dma_start(kTf[HD:HD + 1, :, t * P:(t + 1) * P], nCT[t * NH:(t + 1) * NH, :]).then_inc(ct_moved, 16)
                if K == 20:
                    sp.dma_start(wins_v[:, 0:PAST - TQ, :], stw_rows[:, TQ:PAST, :]).then_inc(copy_st, 16)
            for i in range(5):
                last = max(J for J in range(NJ) if J % 5 == i)
                sp.wait_ge(z_st[i], stored(last))
            for i in range(2):
                sp.wait_ge(q_st[i], 16 * NT)
            sp.wait_ge(ct_moved, 16 * NT)
            sp.wait_ge(misc_st, 48)
            sp.wait_ge(copy_st, 16)

        @block.gpsimd
        def _(pool):
            ch = Chain(pool, pool_a)
            nc.gpsimd.memset(graw[:, :, :], 0.0).then_inc(misc_set, 1)
            pool.wait_ge(ln_t, 2 * T9)
            pool.wait_ge(sc_ready, 1)
            ch.link(nc.gpsimd.memset(Vf[:, :, :, HD:HD + 1], 1.0))
            ch.link(nc.gpsimd.memset(Vs[:, :, :, HD:HD + 1], 1.0))
            ch.link(nc.gpsimd.memset(kTs[HD:HD + 1, :, :], 0.0))
            ch.link(nc.gpsimd.memset(kTw[HD:HD + 1, :, :], 0.0))
            nc.gpsimd.memset(Vw[:, :, :, HD:HD + 1], 1.0).then_inc(kv_set, 1)
            pool.wait_ge(s_gvec, 96)
            ch.link(nc.gpsimd.tensor_scalar(gvec[:, 0, :], gvec[:, 0, :], SCALE, None, ALU.mult))
            ch.link(nc.gpsimd.tensor_scalar(gvec[:, 2, :], gvec[:, 2, :], SCALE, None, ALU.mult))
            for J in pool_jobs:
                b, t = jobs[J]
                name, z, r = ZB[b], zsb[J % 5], rows(t)
                if name == "vf":
                    pool.wait_ge(z_ev, J + 1)
                    nc.gpsimd.tensor_copy(Vf[:, t, :, 0:HD], z[:, :].rearrange("p (h d) -> p h d", d=HD)).then_inc(pool_done, 1)
                    continue
                pool.wait_ge(z_scaled, n_index[J] + 1)
                x = k_heads(name, z, r, HD)
                if name == "cs":
                    g = gvec[0:r, 3:5, :].unsqueeze(2).to_broadcast([r, 2, G, HD])
                else:
                    i = {"misc": 5, "kf": 1, "qf": 0, "qn": 2}[name]
                    g = gvec[0:r, i:i + 1, :].to_broadcast([r, G if name == "misc" else NH, HD])
                ins = nc.gpsimd.tensor_tensor(x, x, g, ALU.mult)
                if name in ("kf", "qf"):
                    ins.then_inc(pool_done, 1)
                    continue
                ch.link(ins)
                x = k_heads(name, z, r, 16)
                n = NH if name == "qn" else G
                if name == "cs":
                    a = rope[0][0:r, 0:4, :].rearrange("p (a h) d -> p a h d", a=2)
                    c = rope[1][0:r, 0:4, :].rearrange("p (a h) d -> p a h d", a=2)
                    lo, hi = c[:, :, :, 0:8], c[:, :, :, 8:16]
                    x_lo, x_hi = x[:, :, :, 0:8], x[:, :, :, 8:16]
                else:
                    a, c = rope[0][0:r, 0:n, :], rope[1][0:r, 0:n, :]
                    lo, hi = c[:, :, 0:8], c[:, :, 8:16]
                    x_lo, x_hi = x[:, :, 0:8], x[:, :, 8:16]

                def table(col, w):
                    v = cst[0:r, col + 16 * t:col + 16 * t + w].unsqueeze(1)
                    return v.unsqueeze(1).to_broadcast([r, 2, G, w]) if name == "cs" else v.to_broadcast([r, n, w])

                ch.link(nc.gpsimd.tensor_tensor(a, x, table(K_COS, 16), ALU.mult))
                ch.link(nc.gpsimd.tensor_tensor(lo, x_hi, table(K_SIN, 8), ALU.mult))
                ch.link(nc.gpsimd.tensor_tensor(hi, x_lo, table(K_SIN + 8, 8), ALU.mult))
                last = nc.gpsimd.tensor_tensor(x, a, c, ALU.add)
                if t < NT and name == "misc":
                    last = nc.gpsimd.tensor_copy(Vw[:, t, :, 0:HD], z[:, 128:256].rearrange("p (h d) -> p h d", d=HD))
                if t < NT and name == "cs":
                    last = nc.gpsimd.tensor_copy(Vs[:, t, :, 0:HD], z[:, 384:512].rearrange("p (h d) -> p h d", d=HD))
                last.then_inc(pool_done, 1)

        @block.scalar
        def _(act):
            act.wait_ge(c_neg, 1)
            nc.scalar.activation(c9e[:, :], c9e[:, :], ACT.Exp).then_inc(c_exp, 1)
            for g, (lo, hi) in enumerate(((0, 4), (4, 8), (8, 9))):
                act.wait_ge(s_x[g], 16)
                for t in range(lo, hi):
                    if t:
                        act.wait_ge(ln_sq, t)
                    nc.scalar.activation(junk[0:rows(t), :], xb[0:rows(t), t, :], ACT.Square,
                                         accum_out=ssum[0:rows(t), t:t + 1]).then_inc(ln_sq, 1)
                act.wait_ge(ln_var, g + 1)
                r = rows(lo)
                nc.scalar.activation(rstd[0:r, lo:hi], ssum[0:r, lo:hi], ACT.Sqrt).then_inc(ln_root, 1)
            for t in range(T9):
                act.wait_ge(ln_t, 2 * t + 1)
                r = rows(t)
                nc.scalar.activation(hT[:, 0:4, t * P:t * P + r],
                                     bk[2 * (t % 3)].rearrange("p (k n) -> p k n", k=4)[:, :, 0:r], ACT.Copy).then_inc(ln_ea, 1)
            act.wait_ge(mod_ready, 1)
            act.wait_ge(ln_ea, T9)
            for k in range(4):
                nc.scalar.activation(hT[:, k, 0:S], hT[:, k, 0:S], ACT.Identity, bias=modT[:, k, 0:1],
                                     scale=gain1[:, k, 0:1]).then_inc(mod_a, 1)

            def copy_t(K):
                b, t = jobs[K]
                i = tz_index[K]
                act.wait_ge(tz_ready, i + 1)
                src = bk[3 + i % 3].rearrange("p (j n) -> p j n", n=P)
                cols = slice(t * P, (t + 1) * P)
                if ZB[b] == "misc":
                    nc.scalar.activation(kTw[0:HD, 0, cols], src[0:HD, 0, :], ACT.Copy)
                    nc.scalar.activation(kTw[0:HD, 1, cols], src[HD:P, 0, :], ACT.Copy).then_inc(tz_a, 1)
                    return
                if ZB[b] == "kf":
                    dst = kTf[0:HD, :, cols].rearrange("p (j e) n -> p j e n", e=2)
                else:
                    q = q_index[K]
                    if q >= 2:
                        act.wait_ge(q_st[q % 2], 16 * (q // 2))
                    dst = qst[q % 2][:, :, :].rearrange("p (j e) n -> p j e n", e=2)
                nc.scalar.activation(dst[:, :, 0, :], src[0:HD, :, :], ACT.Copy)
                nc.scalar.activation(dst[:, :, 1, :], src[HD:P, :, :], ACT.Copy).then_inc(tz_a, 1)

            for J in range(NJ + LAG):
                if J < NJ:
                    b, t = jobs[J]
                    name, r, w = ZB[b], rows(t), ZW[ZB[b]]
                    act.wait_ge(z_ready, J + 1)
                    if J >= 5:
                        act.wait_ge(pool_done, pool_count[J - 5])
                        if J - 5 in tz_index:
                            act.wait_ge(tz_ready, tz_index[J - 5] + 1)
                        if stored(J - 5):
                            act.wait_ge(z_st[J % 5], stored(J - 5))
                    ins = nc.scalar.activation(zsb[J % 5][0:r, 0:w], bk[J % 3][0:r, 0:w], ACT.Copy)
                    if name != "vf":
                        before = sum(j <= J - 2 for j in normed)
                        if before:
                            act.wait_ge(z_var, before)
                        n = 128 if name == "misc" else 512
                        ins = nc.scalar.activation(sq[J % 2][0:r, 0:n], bk[J % 3][0:r, 0:n], ACT.Square)
                    ins.then_inc(z_ev, 1)
                    if name != "vf":
                        act.wait_ge(z_var, n_index[J] + 1)
                        h = hv[J % 3]
                        nc.scalar.activation(h[0:r, 1, :], h[0:r, 0, :], ACT.Sqrt).then_inc(z_root, 1)
                    if J == NT:
                        act.wait_ge(g_arg, 1)
                        nc.scalar.activation(gexp[:, :, :], gexp[:, :, :], ACT.Exp).then_inc(g_exp, 1)
                        act.wait_ge(g_one, 1)
                        nc.scalar.activation(lnv[:, :, :], gexp[:, :, 24:32], ACT.Ln).then_inc(g_ln, 1)
                K = J - LAG
                if K in tz_index and tz_eng[tz_index[K]] == "a":
                    copy_t(K)

        @block.vector
        def _(dve):
            ch = Chain(dve, dve_a)
            nc.vector.nop().then_inc(ada_ev, CREDIT)
            dve.wait_ge(s_c, 32)
            nc.vector.tensor_scalar(c9e[:, :], c9[:, :], -1.0, EXP_MAX, ALU.mult, ALU.min).then_inc(c_neg, 1)
            dve.wait_ge(c_exp, 1)
            ch.link(nc.vector.tensor_scalar(c9e[:, :], c9e[:, :], 1.0, None, ALU.add))
            ch.link(nc.vector.reciprocal(c9e[:, :], c9e[:, :]))
            nc.vector.tensor_tensor(c9e[:, :], c9[:, :], c9e[:, :], ALU.mult).then_inc(c_silu, 1)
            for g, (lo, hi) in enumerate(((0, 4), (4, 8), (8, 9))):
                r = rows(lo)
                dve.wait_ge(ln_sq, hi)
                nc.vector.tensor_scalar(ssum[0:r, lo:hi], ssum[0:r, lo:hi], 1.0 / D, EPS, ALU.mult, ALU.add).then_inc(ln_var, 1)
                dve.wait_ge(ln_root, g + 1)
                ch.link(nc.vector.reciprocal(rstd[0:r, lo:hi], rstd[0:r, lo:hi]))
                for t in range(lo, hi):
                    nc.vector.tensor_scalar(xb[0:r, t, :], xb[0:r, t, :], rstd[0:r, t:t + 1], None, ALU.mult).then_inc(xn_done, 1)
                if g == 0:
                    dve.wait_ge(t0_ready, 1)
                    nc.vector.tensor_copy(scT[:, :, :], bk[7][:, 0:72].rearrange("p (k n) -> p k n", k=KC))
                    nc.vector.tensor_copy(vecT[:, :], bk[7][:, 128:192])
                    nc.vector.tensor_copy(peT[:, :, :], bk[7][:, 256:384].rearrange("p (k n) -> p k n", k=2)).then_inc(sc_ready, 1)
            for t in range(T9):
                dve.wait_ge(ln_t, 2 * t + 2)
                r = rows(t)
                nc.vector.tensor_copy(hT[:, 4:8, t * P:t * P + r],
                                      bk[2 * (t % 3) + 1].rearrange("p (k n) -> p k n", k=4)[:, :, 0:r]).then_inc(ln_ed, 1)
            dve.wait_ge(sc_ready, 1)

            def store_ada(n, src):
                out, bias = modT[:, bass.ds(4 * n, 4), :], vecT[:, bass.ds(4 * n, 4)]
                nc.vector.tensor_tensor(out, src[:, 0:36].rearrange("p (k n) -> p k n", k=4),
                                        bias.unsqueeze(2).to_broadcast([P, 4, B + 1]), ALU.add).then_inc(ada_ev, 1)

            with dve.Fori(0, ada1 // 2) as it:
                for s in range(2):
                    dve.wait_ge(ada_ready, 2 * it + s + 1)
                    store_ada(2 * it + s, bk[6 + s])
            dve.wait_ge(ada_ev, CREDIT + ada1)
            nc.vector.scalar_tensor_tensor(gain1[:, :, :], modT[:, 8:16, :], 1.0,
                                           vecT[:, 48:56].unsqueeze(2).to_broadcast([P, KC, B + 1]),
                                           ALU.add, ALU.mult).then_inc(mod_ready, 1)
            dve.wait_ge(mod_ready, 1)
            dve.wait_ge(ln_ed, T9)
            for k in range(4, 8):
                nc.vector.tensor_scalar(hT[:, k, 0:S], hT[:, k, 0:S], gain1[:, k, 0:1], modT[:, k, 0:1],
                                        ALU.mult, ALU.add).then_inc(mod_d, 1)
            dve.wait_ge(ln_ea, T9)
            hs = hT[:, :, S:TOK].rearrange("p k (b t) -> p k b t", b=B)
            ch.link(nc.vector.tensor_tensor(hs, hs, gain1[:, :, 1:B + 1].unsqueeze(3).to_broadcast([P, KC, B, TQ]), ALU.mult))
            nc.vector.tensor_tensor(hs, hs, modT[:, 0:KC, 1:B + 1].unsqueeze(3).to_broadcast([P, KC, B, TQ]), ALU.add).then_inc(mod_d, 1)
            dve.wait_ge(misc_set, 1)
            dve.wait_ge(s_gvec, 96)

            def copy_t(K):
                t, i = jobs[K][1], tz_index[K]
                dve.wait_ge(tz_ready, i + 1)
                src = bk[3 + i % 3]
                for kv in range(2):
                    nc.vector.tensor_tensor(Xc[:, 2 * t:2 * t + 2, kv, :],
                                            src[:, P * kv:P * (kv + 1)].rearrange("p (n d) -> p n d", n=2),
                                            peT[:, kv:kv + 1, :].to_broadcast([P, 2, BLOCK]), ALU.add)
                nc.vector.tensor_copy(kTs[0:HD, 0, t * P:(t + 1) * P], src[0:HD, 256:384])
                nc.vector.tensor_copy(kTs[0:HD, 1, t * P:(t + 1) * P], src[HD:P, 256:384]).then_inc(tz_d, 1)

            for J in range(NJ + LAG):
                if J < NJ:
                    b, t = jobs[J]
                    name, z, r, h = ZB[b], zsb[J % 5], rows(t), hv[J % 3]
                    if name != "vf":
                        n = G if name == "misc" else NH
                        dve.wait_ge(z_ev, J + 1)
                        ch.link(nc.vector.tensor_reduce(h[0:r, 0, 0:n], sq[J % 2][0:r, 0:n * HD].rearrange("p (h d) -> p h d", d=HD),
                                                        AX.X, ALU.add))
                        if name == "misc":
                            ch.link(nc.vector.memset(h[0:r, 0, n:NH], 1.0))
                        nc.vector.tensor_scalar(h[0:r, 0, :], h[0:r, 0, :], 1.0 / HD, EPS, ALU.mult, ALU.add).then_inc(z_var, 1)
                        if name == "misc":
                            nc.vector.tensor_tensor(graw[0:r, t, :], z[0:r, 256:288], bias32[0:r, :], ALU.add)
                        dve.wait_ge(z_root, n_index[J] + 1)
                        ch.link(nc.vector.reciprocal(h[0:r, 2, :], h[0:r, 1, :]))
                        x = k_heads(name, z, r, HD)
                        if name == "cs":
                            s = h[0:r, 2, :].rearrange("p (a k h) -> p a k h", a=2, k=2)[:, :, 0, :].unsqueeze(3).to_broadcast([r, 2, G, HD])
                        else:
                            s = h[0:r, 2, 0:n].unsqueeze(2).to_broadcast([r, n, HD])
                        nc.vector.tensor_tensor(x, x, s, ALU.mult).then_inc(z_scaled, 1)
                    if J == NT:
                        dve.wait_ge(z_scaled, n_index[J] + 1)
                        ch.link(nc.vector.tensor_scalar(gexp[:, :, 0:24], graw[:, :, 0:24], -1.0, EXP_MAX, ALU.mult, ALU.min))
                        ch.link(nc.vector.tensor_scalar(gexp[:, :, 24:32], graw[:, :, 24:32], -1.0, None, ALU.mult))
                        nc.vector.tensor_tensor(gexp[:, :, 24:32], gexp[:, :, 24:32], graw[:, :, 24:32], ALU.min).then_inc(g_arg, 1)
                        dve.wait_ge(g_exp, 1)
                        nc.vector.tensor_scalar(gexp[:, :, :], gexp[:, :, :], 1.0, None, ALU.add).then_inc(g_one, 1)
                        dve.wait_ge(g_one, 1)
                        ch.link(nc.vector.reciprocal(gates[:, :, :], gexp[:, :, 0:24]))
                        ch.link(nc.vector.tensor_scalar(gates[:, 0, 0:NH], gates[:, 0, 0:NH], cst[:, K_ANY:K_ANY + 1], None, ALU.mult))
                        dve.wait_ge(g_ln, 1)
                        nc.vector.scalar_tensor_tensor(logf[:, :, :], graw[:, :, 24:32], 0.0, lnv[:, :, :],
                                                       ALU.min, ALU.subtract).then_inc(g_done, 1)
                    if J in ada_after:
                        i = ada_after.index(J)
                        dve.wait_ge(ada_ready, ada1 + i + 1)
                        store_ada(ada1 + i, bk[6])
                    if J == csum_after:
                        dve.wait_ge(c_ready, 1)
                        tot = bk[7][:, 64:128].rearrange("p (t h) -> p t h", h=NH)
                        ch.link(nc.vector.memset(cpre[:, 0, :], 0.0))
                        for t2 in range(1, NT):
                            ch.link(nc.vector.tensor_tensor(cpre[:, t2, :], cpre[:, t2 - 1, :], tot[:, t2 - 1, :], ALU.add))
                        nc.vector.scalar_tensor_tensor(csum[:, :, :], bk[7][:, 0:64].rearrange("p (t h) -> p t h", h=NH), -1.0,
                                                       cpre[:, :, :], ALU.mult, ALU.subtract).then_inc(c_neg2, 1)
                    if J == csum_after + 2:
                        dve.wait_ge(ct_ready, 1)
                        nc.vector.tensor_copy(nCT[:, :], bk[7][0:HD, 128:256]).then_inc(ct_copied, 1)
                K = J - LAG
                if K in tz_index and tz_eng[tz_index[K]] == "d":
                    copy_t(K)

        @block.tensor
        def _(pe):
            pe.wait_ge(s_const, 16)
            pe.wait_ge(s_vec, 48)
            pe.wait_ge(c_silu, 1)
            pe.wait_ge(s_pe, 32)
            for k in range(KC):
                nc.tensor.transpose(bk[7][:, 9 * k:9 * k + 9], c9e[:, k * P:(k + 1) * P], ident[0:B + 1, 0:B + 1])
            nc.tensor.transpose(bk[7][:, 128:192], vecn[:, :], ident[0:HD, 0:HD])
            for kv in range(2):
                last = nc.tensor.transpose(bk[7][:, 256 + 64 * kv:320 + 64 * kv],
                                           pen[:, kv, :, :].rearrange("p a d -> p (a d)"), ident[0:HD, 0:HD])
            last.then_inc(t0_ready, 1)
            for t in range(T9):
                r = rows(t)
                pe.wait_ge(xn_done, t + 1)
                if t >= 3:
                    pe.wait_ge(ln_ea, t - 2)
                    pe.wait_ge(ln_ed, t - 2)
                for k in range(KC):
                    dst = bk[2 * (t % 3) + k // 4][:, P * (k % 4):P * (k % 4) + r]
                    ins = nc.tensor.transpose(dst, xb[0:r, t, k * P:(k + 1) * P], ident[0:r, 0:r])
                    if k % 4 == 3:
                        ins.then_inc(ln_t, 1)
            pe.wait_ge(sc_ready, 1)

            def ada(buf, dst):
                for j in range(4):
                    for k in range(KC):
                        last = nc.tensor.matmul(dst[:, 9 * j:9 * j + 9], buf[:, k, j * P:(j + 1) * P], scT[:, k, :],
                                                start=(k == 0), stop=(k == KC - 1))
                last.then_inc(ada_ready, 1)

            with pe.Fori(0, ada1 // 2) as it:
                pe.wait_ge(ada_ev, 2 * it + CREDIT)
                for s in range(2):
                    pe.wait_ge(w_ld[s], 16 * it + 16)
                    ada(wbuf[s], bk[6 + s])
            pe.wait_ge(mod_a, 4)
            pe.wait_ge(mod_d, 5)
            for J in range(NJ + LAG):
                if J < NJ:
                    b, t = jobs[J]
                    r, w = rows(t), ZW[ZB[b]]
                    if t == 0:
                        pe.wait_ge(w_ld[b % 2], loaded(b % 2, 2 + b // 2))
                    if J >= 3:
                        pe.wait_ge(z_ev, J - 2)
                    for k in range(KC):
                        last = nc.tensor.matmul(bk[J % 3][0:r, 0:w], hT[:, k, t * P:t * P + r], wbuf[b % 2][:, k, 0:w],
                                                start=(k == 0), stop=(k == KC - 1))
                    last.then_inc(z_ready, 1)
                K = J - LAG
                if K in tz_index:
                    i = tz_index[K]
                    pe.wait_ge(pool_done, pool_count[K])
                    if i >= 3:
                        pe.wait_ge(tz_a if tz_eng[i - 3] == "a" else tz_d, tz_order[i - 3])
                    n = {"misc": 1, "cs": 3}.get(ZB[jobs[K][0]], 4)
                    for j in range(n):
                        last = nc.tensor.transpose(bk[3 + i % 3][:, j * P:(j + 1) * P], zsb[K % 5][:, j * P:(j + 1) * P], ident)
                    last.then_inc(tz_ready, 1)
                if J == csum_after:
                    pe.wait_ge(g_done, 1)
                    lf = logf[:, 0:NT, :].rearrange("p t h -> p (t h)")
                    nc.tensor.matmul(bk[7][:, 0:64], cst[:, K_U:K_U + P], lf, start=True, stop=True)
                    nc.tensor.matmul(bk[7][:, 64:128], cst[:, K_ONE:K_ONE + P], lf, start=True, stop=True).then_inc(c_ready, 1)
                if J == csum_after + 2:
                    pe.wait_ge(c_neg2, 1)
                    nc.tensor.transpose(bk[7][0:HD, 128:256], csum[:, :, :].rearrange("p t h -> p (t h)"), ident).then_inc(ct_ready, 1)
                if J in ada_after:
                    i = ada_after.index(J)
                    pe.wait_ge(w_ld[2], 16 * (i + 1))
                    pe.wait_ge(ada_ev, CREDIT + ada1 + i)
                    ada(wbuf[2], bk[6])

    cp_ld = [sem(f"cpage_loaded{i}") for i in range(2)]
    wc_ld = [sem(f"wcmp_loaded{i}") for i in range(2)]
    wc_set, cb_ready, xc_ev, wc_used, kvc_done, vt_ready, vc_done, vcp_set = (sem(n) for n in (
        "wcmp_cleared", "cpage_transposed", "cinput_stored", "wcmp_used", "kvc_copied",
        "vc_transposed", "vc_copied", "vcp_ones_set"))
    wcmp_v = w_cmp.rearrange("a k (p d) e -> (a k) d p e", d=HD)
    CW = 8
    NCW = BLOCK // CW

    with nc.Block() as block:

        @block.sync
        def _(sp):
            sp.wait_ge(s_pt, 16)
            sp.wait_ge(wc_set, 1)

            def load_w(c):
                for kv in range(2):
                    for i in range(2):
                        sp.dma_start(wbd[c % 2][HD * i:HD * (i + 1), kv, :, HD * i:HD * (i + 1)],
                                     wcmp_v[kv, :, CW * c:CW * (c + 1), :]).then_inc(wc_ld[c % 2], 16)

            def load_pages(b, s):
                for j in range(PAGES):
                    page = sp.value_load(ptab[0:1, bass.ds(b * PAGES + j, 1)], min_val=0, max_val=n_pool - 1)
                    sp.dma_start(cpage[s][:, j, :], cnsa_v[page, :, 0:256]).then_inc(cp_ld[s], 16)

            for s in range(2):
                load_pages(s, s)
            for c in range(2):
                load_w(c)
            with sp.Fori(0, B // 2 - 1) as it:
                for s in range(2):
                    sp.wait_ge(cb_ready, 2 * it + s + 1)
                    load_pages(2 * it + s + 2, s)
            for c in range(2, NCW):
                sp.wait_ge(wc_used, c - 1)
                load_w(c)

        @block.gpsimd
        def _(pool):
            nc.gpsimd.memset(kcP[HD:HD + 1, :, :], 0.0).then_inc(vcp_set, 1)
            pool.wait_ge(vcp_set, 1)
            nc.gpsimd.memset(vcP[:, :, :], 0.0).then_inc(vcp_set, 1)
            nc.gpsimd.memset(wbd[0][:, :, :, :], 0.0)
            nc.gpsimd.memset(wbd[1][:, :, :, :], 0.0).then_inc(wc_set, 1)

        @block.vector
        def _(dve):
            nc.vector.nop().then_inc(xc_ev, CREDIT)
            with dve.Fori(0, B // 2) as it:
                for s in range(2):
                    dve.wait_ge(cb_ready, 2 * it + s + 1)
                    for kv in range(2):
                        ins = nc.vector.tensor_tensor(
                            Xc[:, bass.ds(it * (2 * NBS) + (NBP + NBS * s), NBS), kv, :],
                            bk[2 * s + kv].rearrange("p (n d) -> p n d", d=BLOCK),
                            peT[:, kv:kv + 1, :].to_broadcast([P, NBS, BLOCK]), ALU.add)
                    ins.then_inc(xc_ev, 1)
            dve.wait_ge(vcp_set, 2)
            dve.wait_ge(vt_ready, 1)
            nc.vector.memset(vcP[0:NBP, :, HD:HD + 1], 1.0)
            nc.vector.tensor_copy(vcP[0:NBP, :, 0:HD], bk[6][0:NBP, 0:P].rearrange("p (g d) -> p g d", g=G))
            nc.vector.tensor_copy(vcS[:, 0:4, :], bk[7][0:NBS, :].rearrange("p (b d) -> p b d", b=4))
            nc.vector.tensor_copy(vcS[:, 4:8, :], bk[0][0:NBS, :].rearrange("p (b d) -> p b d", b=4)).then_inc(vc_done, 1)

        @block.scalar
        def _(act):
            act.wait_ge(wc_used, NCW)
            nc.scalar.activation(kvcT[:, 1, :], bk[5][:, 0:NBP + B * NBS], ACT.Copy).then_inc(kvc_done, 1)
            nc.scalar.activation(kcS[:, :], bk[4][:, NBP:NBP + B * NBS], ACT.Copy)
            nc.scalar.activation(kcP[0:HD, 0, :], bk[4][0:HD, 0:NBP], ACT.Copy)
            nc.scalar.activation(kcP[0:HD, 1, :], bk[4][HD:P, 0:NBP], ACT.Copy).then_inc(kvc_done, 1)

        @block.tensor
        def _(pe):
            with pe.Fori(0, B // 2) as it:
                pe.wait_ge(xc_ev, 2 * it + CREDIT)
                for s in range(2):
                    pe.wait_ge(cp_ld[s], it * (16 * PAGES) + 16 * PAGES)
                    for kv in range(2):
                        for j in range(PAGES):
                            last = nc.tensor.transpose(bk[2 * s + kv][:, j * P:(j + 1) * P], cpage[s][:, j, P * kv:P * (kv + 1)], ident)
                    last.then_inc(cb_ready, 1)
            pe.wait_ge(xc_ev, B + CREDIT)
            for c in range(NCW):
                pe.wait_ge(wc_ld[c % 2], 64 * (c // 2 + 1))
                for p in range(CW):
                    for kv in range(2):
                        last = nc.tensor.matmul(bk[4 + kv][:, 0:NBP + B * NBS], wbd[c % 2][:, kv, p, :], Xc[:, :, kv, CW * c + p],
                                                start=(c == 0 and p == 0), stop=(c == NCW - 1 and p == CW - 1))
                last.then_inc(wc_used, 1)
            pe.wait_ge(kvc_done, 1)
            nc.tensor.transpose(bk[6][0:NBP, 0:P], kvcT[:, 1, 0:NBP], ident)
            for b in range(B):
                last = nc.tensor.transpose((bk[7] if b < 4 else bk[0])[0:NBS, P * (b % 4):P * (b % 4 + 1)],
                                           kvcT[:, 1, NBP + NBS * b:NBP + NBS * (b + 1)], ident)
            last.then_inc(vt_ready, 1)

    q_one = sem("q_ones_set")

    def prompt_attention(tag, source, kinds):
        q_ld = [sem(f"{tag}_q_loaded{i}") for i in range(2)]
        scores_ready, max_ready, prob_ready, pt_ready, pt_act, pt_dve, o_ready, o_norm = (sem(f"{tag}_{n}") for n in (
            "scores_ready", "max_ready", "prob_ready", "pt_ready", "pt_copied_act", "pt_copied_dve", "o_ready", "o_stored"))
        dve_s = sem(f"{tag}_dve_step")
        fox = kinds == ("fox",)
        units = [(s, u) for s in range(2) for u in attention_units(kinds)]
        n = len(units)
        nk = [u[3] for _, u in units]
        halves = [(k + 3) // 4 for k in nk]
        h0 = [sum(halves[:i]) for i in range(n + 1)]
        d0 = [sum(h == 2 for h in halves[:i]) for i in range(n + 1)]
        owner = [(i, j) for i in range(n) for j in range(halves[i])]
        steps = sum((2 if u[0] == "win" and u[3] == 5 else 1) + (1 if fox else 2) for _, u in units)
        TURNS = NH // 2
        K = HD + 1

        with nc.Block() as block:

            @block.sync
            def _(sp):
                for s in range(2):
                    sp.dma_start(qT[s][0:HD, :], qt_d[source, s, :, :]).then_inc(q_ld[s], 16)
                with sp.Fori(0, TURNS - 1) as it:
                    for s in range(2):
                        sp.wait_ge(o_ready, it * n + (s + 1) * (n // 2))
                        sp.dma_start(qT[s][0:HD, :], qt_d[source, 2 * it + (s + 2), :, :]).then_inc(q_ld[s], 16)

            if fox:
                @block.gpsimd
                def _(pool):
                    nc.gpsimd.memset(probT[0][:, 0, :], 0.0)
                    nc.gpsimd.memset(probT[1][:, 0, :], 0.0).then_inc(q_one, 1)
                    pool.wait_ge(q_one, 1)
                    nc.gpsimd.memset(qT[0][HD:HD + 1, :], 1.0)
                    nc.gpsimd.memset(qT[1][HD:HD + 1, :], 1.0).then_inc(q_one, 1)

            @block.tensor
            def _(pe):
                if fox:
                    pe.wait_ge(q_one, 2)
                with pe.Fori(0, TURNS) as it:

                    def scores(i):
                        s, (kind, t, lo, k) = units[i]
                        if i % (n // 2) == 0:
                            pe.wait_ge(q_ld[s], it * 16 + 16)
                        if i >= 2:
                            pe.wait_ge(prob_ready, it * n + (i - 1))
                        dst = banks(2 * (i % 2), 2)
                        lhsT = qT[s][0:K, t * P:(t + 1) * P]
                        if kind == "cmp":
                            last = nc.tensor.matmul(dst[:, 0:NBP], lhsT, kcP[:, it // 2, :], start=True, stop=True)
                        for c in range(0, 0 if kind == "cmp" else k * P, 512):
                            w = min(512, k * P - c)
                            a, z = lo * P + c, lo * P + c + w
                            rhs = (kTf[0:K, 2 * it + s, a:z] if kind == "fox" else
                                   kTs[:, it // 2, a:z] if kind == "slc" else kTw[:, it // 2, a:z])
                            last = nc.tensor.matmul(dst[:, c:c + w], lhsT, rhs, start=True, stop=True)
                        last.then_inc(scores_ready, 1)

                    def transposes(i):
                        kind, _, _, k = units[i][1]
                        pe.wait_ge(prob_ready, it * n + (i + 1))
                        for hh in range(halves[i]):
                            g = h0[i] + hh
                            if g >= 2:
                                j, jj = owner[g - 2]
                                if jj == 0:
                                    pe.wait_ge(pt_act, it * n + (j + 1))
                                else:
                                    pe.wait_ge(pt_dve, it * d0[n] + d0[j + 1])
                            for j in range(4 * hh, min(k, 4 * hh + 4)):
                                w = NBP if kind == "cmp" else P
                                last = nc.tensor.transpose(bk[4 + g % 2][0:w, P * (j % 4):P * (j % 4 + 1)],
                                                           prob[i % 2][:, j * P:j * P + w], ident)
                            last.then_inc(pt_ready, 1)

                    def values(i):
                        s, (kind, t, lo, k) = units[i]
                        pe.wait_ge(pt_act, it * n + (i + 1))
                        if halves[i] == 2:
                            pe.wait_ge(pt_dve, it * d0[n] + d0[i + 1])
                        pe.wait_ge(o_norm, it * n + (max(i - 1, 0) + CREDIT))
                        dst = bk[6 + i % 2][:, 0:HD + 1]
                        for j in range(k):
                            v = (vcP[:, it // 2, :] if kind == "cmp" else Vf[:, lo + j, 2 * it + s, :] if kind == "fox" else
                                 Vs[:, lo + j, it // 2, :] if kind == "slc" else Vw[:, lo + j, it // 2, :])
                            last = nc.tensor.matmul(dst, probT[i % 2][:, j, :], v, start=(j == 0), stop=(j == k - 1))
                        last.then_inc(o_ready, 1)

                    scores(0)
                    for i in range(n):
                        if i + 1 < n:
                            scores(i + 1)
                        transposes(i)
                        if i:
                            values(i - 1)
                    values(n - 1)

            @block.scalar
            def _(act):
                if fox:
                    act.wait_ge(q_one, 1)
                with act.Fori(0, TURNS) as it:
                    for i, (s, (kind, t, lo, k)) in enumerate(units):
                        w = NBP if kind == "cmp" else k * P
                        act.wait_ge(max_ready, it * n + (i + 1))
                        nc.scalar.activation(prob[i % 2][:, 0:w], banks(2 * (i % 2), 2)[:, 0:w], ACT.Exp,
                                             bias=nmax[:, i % 2, 0:1]).then_inc(prob_ready, 1)
                        act.wait_ge(pt_ready, it * h0[n] + (h0[i] + 1))
                        m, r = min(k, 4), NBP if kind == "cmp" else P
                        nc.scalar.activation(probT[i % 2][0:r, 0:m, :],
                                             bk[4 + h0[i] % 2][0:r, 0:m * P].rearrange("p (j n) -> p j n", n=P),
                                             ACT.Copy).then_inc(pt_act, 1)

            @block.vector
            def _(dve):
                ch = Chain(dve, dve_s)
                nc.vector.nop().then_inc(o_norm, CREDIT)
                if fox:
                    dve.wait_ge(q_one, 1)
                with dve.Fori(0, TURNS) as it:
                    ch.loop(it, steps)

                    def maximum(i):
                        s, (kind, t, lo, k) = units[i]
                        src = banks(2 * (i % 2), 2)
                        dve.wait_ge(scores_ready, it * n + (i + 1))
                        if kind == "cmp":
                            w = NBP
                            ch.link(nc.vector.tensor_tensor(src[:, 0:w], src[:, 0:w], cst[:, K_CMP + NBP * t:K_CMP + NBP * (t + 1)], ALU.add))
                        else:
                            w = k * P
                            d = src[:, w - P:w]
                            ch.link(nc.vector.tensor_tensor(d, d, cst[:, K_CAUS:K_CAUS + P], ALU.add))
                            if kind == "win" and k == 5:
                                d = src[:, 0:P]
                                ch.link(nc.vector.tensor_tensor(d, d, cst[:, K_WIN:K_WIN + P], ALU.add))
                        nc.vector.tensor_reduce(nmax[:, i % 2, 0:1], src[:, 0:w], AX.X, ALU.max, negate=True).then_inc(max_ready, 1)

                    def second_half(i):
                        k = nk[i]
                        if halves[i] == 2:
                            dve.wait_ge(pt_ready, it * h0[n] + (h0[i] + 2))
                            nc.vector.tensor_copy(probT[i % 2][:, 4:k, :],
                                                  bk[4 + (h0[i] + 1) % 2][:, 0:(k - 4) * P].rearrange("p (j n) -> p j n", n=P)).then_inc(pt_dve, 1)

                    def output(i):
                        s, (kind, t, lo, k) = units[i]
                        dve.wait_ge(o_ready, it * n + (i + 1))
                        src, f = bk[6 + i % 2], gate_qk[:, i % 2, :]
                        ch.link(nc.vector.reciprocal(f[:, 0:1], src[:, HD:HD + 1]))
                        if kind == "fox":
                            nc.vector.tensor_scalar(mix[:, t, bass.ds(it * (2 * HD) + s * HD, HD)], src[:, 0:HD], f[:, 0:1], None, ALU.mult).then_inc(o_norm, 1)
                            return
                        br = {"cmp": 0, "slc": 1, "win": 2}[kind]
                        ch.link(nc.vector.tensor_tensor(f[:, 1:2], f[:, 0:1], gates[:, t, bass.ds(it * 2 + (br * NH + s), 1)], ALU.mult))
                        m = mix[:, t, bass.ds(it * (2 * HD) + (512 + s * HD), HD)]
                        if kind == "cmp":
                            nc.vector.tensor_scalar(m, src[:, 0:HD], f[:, 1:2], None, ALU.mult).then_inc(o_norm, 1)
                        else:
                            dve.wait_ge(o_norm, it * n + (i + CREDIT))
                            nc.vector.scalar_tensor_tensor(m, src[:, 0:HD], f[:, 1:2], m, ALU.mult, ALU.add).then_inc(o_norm, 1)

                    maximum(0)
                    for i in range(n):
                        if i + 1 < n:
                            maximum(i + 1)
                        second_half(i)
                        if i:
                            output(i - 1)
                    output(n - 1)
                    ch.end(TURNS)

    prompt_attention("fox", 0, ("fox",))
    prompt_attention("nsa", 1, ("cmp", "slc", "win"))

    in_ld = [sem(f"sample_loaded{i}") for i in range(2)]
    g_ld = sem("sample_gates_loaded")
    (e_set, lf_ready, p1_ready, q_bd, negc_done, kt_ready, kt_act, kt_dve, ks_ready, ks_done, sc_done, sc_act, m_ready,
     e_ready, p_ready, pt2_ready, pt2_act, pt2_dve, o2_ready, o2_done) = (sem(f"sample_{n}") for n in (
        "cleared", "logf_spread", "queries_transposed", "queries_placed", "bias_ready", "keys_transposed", "keys_act",
        "keys_dve", "new_keys_transposed", "new_keys_stored", "scores", "scores_act", "maxima", "exps", "probs",
        "probs_transposed", "probs_act", "probs_dve", "outputs", "outputs_copied"))
    os_st = [sem(f"sample_stored{i}") for i in range(2)]
    dve_e, pool_e = sem("dve_step_e"), sem("pool_step_e")
    nc.clear_and_free_semaphores(phase1_sems)
    N_LD = 20
    N_OS = 5
    TURNS2 = B // 2
    SAMPLE_STEPS = 2 * (3 + 2 + 3)

    with nc.Block() as block:

        @block.sync
        def _(sp):
            def load(b, s):
                q0 = b * TQ
                for j in range(PAGES):
                    page = sp.value_load(ptab[0:1, bass.ds(b * PAGES + j, 1)], min_val=0, max_val=n_pool - 1)
                    sp.dma_start(fpage[s][:, j, :], cfox_v[page, :, :]).then_inc(in_ld[s], 16)
                    sp.dma_start(npage[s][:, j, :], cnsa_v[page, :, 256:512]).then_inc(in_ld[s], 16)
                    sp.dma_start(lpage[s][:, j, :], clf_v[page, :, :]).then_inc(in_ld[s], 16)
                sp.dma_start(wpage[s][:, :, :], stw_v[b, :, :, :]).then_inc(in_ld[s], 16)
                sp.dma_start(fnew[s][:, :].rearrange("q (k x) -> q k x", k=2), fkvs_v[bass.ds(q0, TQ), :, :]).then_inc(in_ld[s], 16)
                sp.dma_start(nnew[s][:, :], nkvs_v[bass.ds(q0, TQ), 256:512]).then_inc(in_ld[s], 16)
                sp.dma_start(wnew[s][:, :], wins_v[b, PAST - TQ:PAST, :]).then_inc(in_ld[s], 16)
                sp.dma_start(lnew[s][:, :], flfs_b[b, :, :]).then_inc(in_ld[s], 16)
                sp.dma_start(qrow[s][:, 0:512], qs_d[bass.ds(q0, TQ), 0:512]).then_inc(in_ld[s], 16)
                for g in range(G):
                    sp.dma_start(qrow[s][:, 512:1024].rearrange("q (n g d) -> q n g d", g=G, d=HD)[:, :, g, :],
                                 qs_d[bass.ds(q0, TQ), 512 + 256 * g:768 + 256 * g].rearrange("q (n d) -> q n d", d=HD)).then_inc(in_ld[s], 16)

            def store(b, s):
                rows8 = bass.ds(b * TQ, TQ)
                sp.dma_start(mixs_d[rows8, 0:512], ofs[s][:, :]).then_inc(os_st[s], 16)
                for h in range(4):
                    dst = mixs_d[rows8, 512:1024].rearrange("q (g n d) -> q n g d", g=G, n=4)[:, h, :, :]
                    sp.dma_start(dst, ons[s][TQ * h:TQ * (h + 1), :, :]).then_inc(os_st[s], 16)

            for s in range(2):
                sp.nop().then_inc(os_st[s], CREDIT)
                load(s, s)
            with nc.allow_non_contiguous_dma(reason="gates of 64 tokens, once"):
                for h in range(NH):
                    for r in range(3):
                        sp.dma_start(gateS[h * TQ:(h + 1) * TQ, r, :],
                                     gs_d.rearrange("(b q) (r h) -> h r q b", q=TQ, h=NH)[h, r, :, :]).then_inc(g_ld, 16)
            with sp.Fori(0, TURNS2 - 1) as it:
                for s in range(2):
                    sp.wait_ge(o2_ready, 2 * it + (s + 1))
                    load(2 * it + (s + 2), s)
                for s in range(2):
                    sp.wait_ge(o2_done, 2 * it + (s + 1 + CREDIT))
                    store(2 * it + s, s)
            for s in range(2):
                sp.wait_ge(o2_done, B - 1 + s + CREDIT)
                store(B - 2 + s, s)
            for s in range(2):
                sp.wait_ge(os_st[s], 16 * N_OS * TURNS2 + CREDIT)

        @block.gpsimd
        def _(pool):
            ch = Chain(pool, pool_e)
            for s in range(2):
                ch.link(nc.gpsimd.memset(Qf[s][:, :], 0.0))
                ch.link(nc.gpsimd.memset(Qn[s][:, :], 0.0))
            nc.gpsimd.memset(ones512[:, :], 1.0).then_inc(e_set, 1)

        @block.tensor
        def _(pe):
            def pages(dst, src):
                for j in range(PAGES):
                    last = nc.tensor.transpose(dst[:, j * P:(j + 1) * P], src(j), ident)
                return last

            def flip(dst, src, eye, after_wait):
                if after_wait:
                    nc.tensor.matmul(dst, src, eye, start=True, stop=True)
                else:
                    nc.tensor.transpose(dst, src, eye)

            with pe.Fori(0, TURNS2) as it:
                for s in range(2):
                    b0, b1, b2, b3 = bk[4 * s:4 * s + 4]
                    pe.wait_ge(in_ld[s], it * (16 * N_LD) + 16 * N_LD)
                    pe.wait_ge(lf_ready, 2 * it + (s + 1))
                    pe.wait_ge(o2_done, 2 * it + CREDIT)
                    for j in range(8):
                        flip(b0[:, 8 * j:8 * j + 8], qrow[s][:, j * P:(j + 1) * P], ident[0:TQ, 0:TQ], j == 0)
                    for j in range(PAGES):
                        nc.tensor.transpose(b1[0:HD, j * P:(j + 1) * P], lf64[s][:, j, :, :].rearrange("p h q -> p (h q)"), ident)
                    nc.tensor.transpose(b0[0:HD, 64:72], lf64[s][0:TQ, PAGES, :, :].rearrange("p h q -> p (h q)"),
                                        ident[0:TQ, 0:TQ]).then_inc(p1_ready, 1)
                for s in range(2):
                    b0, b1, b2, b3 = bk[4 * s:4 * s + 4]
                    for k in range(6):
                        if k == 2:
                            pe.wait_ge(negc_done, 2 * it + (s + 1))
                        if k == 3:
                            pe.wait_ge(kt_act, it * 6 + (3 * s + 1))
                        if k == 4:
                            pe.wait_ge(kt_dve, it * 6 + (3 * s + 1))
                        if k == 5:
                            pe.wait_ge(kt_act, it * 6 + (3 * s + 2))
                        src = (lambda j: fpage[s][:, j, k * P:(k + 1) * P]) if k < 4 else \
                              (lambda j: (npage if k == 4 else wpage)[s][:, j, 0:P])
                        pages((b2, b3, b1)[k % 3], src).then_inc(kt_ready, 1)
                    for j in range(4):
                        nc.tensor.transpose(b0[:, 128 + 8 * j:136 + 8 * j], fnew[s][:, j * P:(j + 1) * P], ident[0:TQ, 0:TQ])
                    nc.tensor.transpose(b0[:, 160:168], nnew[s][:, 0:P], ident[0:TQ, 0:TQ])
                    nc.tensor.transpose(b0[:, 168:176], wnew[s][:, 0:P], ident[0:TQ, 0:TQ]).then_inc(ks_ready, 1)
                for s in range(2):
                    b0, b1, b2, b3 = bk[4 * s:4 * s + 4]
                    pe.wait_ge(q_bd, 2 * it + (s + 1))
                    pe.wait_ge(kt_act, it * 6 + (3 * s + 3))
                    pe.wait_ge(kt_dve, it * 6 + (3 * s + 3))
                    pe.wait_ge(ks_done, 2 * it + (s + 1))
                    for dst, cols in ((b1[0:HD, 0:PAST], slice(0, PAST)), (b0[0:HD, 192:200], slice(PAST, L))):
                        for j in range(4):
                            nc.tensor.matmul(dst, Qf[s][:, HD * j:HD * (j + 1)], KTf[s][:, j, cols], start=(j == 0), stop=(j == 3))
                    for i, dst in enumerate((b2, b3)):
                        nc.tensor.matmul(dst[0:HD, 0:PAST], Qn[s][:, :], KTn[s][:, i, 0:PAST], start=True, stop=True)
                        nc.tensor.matmul(b0[0:HD, 200 + 8 * i:208 + 8 * i], Qn[s][:, :], KTn[s][:, i, PAST:L], start=True, stop=True)
                    nc.tensor.matmul(b0[0:HD, 216:224], Qn[s][:, :], kcS[:, bass.ds(it * (2 * NBS) + NBS * s, NBS)],
                                     start=True, stop=True).then_inc(sc_done, 1)
                for s in range(2):
                    b0, b1, b2, b3 = bk[4 * s:4 * s + 4]
                    pe.wait_ge(p_ready, 2 * it + (s + 1))
                    for br, dst in enumerate((b1, b2, b3)):
                        for j in range(PAGES):
                            flip(dst[:, HD * j:HD * (j + 1)], sc[s][:, br, j * P:(j + 1) * P], ident[0:HD, 0:HD], br == 0 and j == 0)
                        nc.tensor.transpose(b0[0:TQ, 256 + HD * br:320 + HD * br], sc[s][:, br, PAST:L], ident[0:HD, 0:HD])
                    nc.tensor.transpose(b0[0:NBS, 448:512], scc[s][:, :], ident[0:HD, 0:HD]).then_inc(pt2_ready, 1)
                for s in range(2):
                    b0, b1, b2, b3 = bk[4 * s:4 * s + 4]
                    pe.wait_ge(pt2_act, 2 * it + (s + 1))
                    pe.wait_ge(pt2_dve, 2 * it + (s + 1))
                    for h in range(NH):
                        dst, a, v = b1[0:TQ, HD * h:HD * (h + 1)], slice(TQ * h, TQ * (h + 1)), slice(512 + HD * h, 576 + HD * h)
                        for j in range(PAGES):
                            nc.tensor.matmul(dst, PTb[s][:, 0, j, a], fpage[s][:, j, v], start=(j == 0), stop=False)
                        nc.tensor.matmul(dst, PTs[s][:, 0, a], fnew[s][:, v], start=False, stop=True)
                    for g in range(G):
                        dst, a, v = b2[0:32, HD * g:HD * (g + 1)], slice(32 * g, 32 * g + 32), slice(P + HD * g, P + HD * (g + 1))
                        nc.tensor.matmul(dst, PTs[s][:, 3, a], vcb[s][:, HD * g:HD * (g + 1)], start=True, stop=False)
                        for br, page, new in ((1, npage, nnew), (2, wpage, wnew)):
                            for j in range(PAGES):
                                nc.tensor.matmul(dst, PTb[s][:, br, j, a], page[s][:, j, v], start=False, stop=False)
                            last = nc.tensor.matmul(dst, PTs[s][:, br, a], new[s][:, v], start=False, stop=(br == 2))
                    last.then_inc(o2_ready, 1)

        @block.scalar
        def _(act):
            nc.scalar.nop().then_inc(o2_done, CREDIT)
            with act.Fori(0, TURNS2) as it:
                for s in range(2):
                    b0, b1, b2, b3 = bk[4 * s:4 * s + 4]
                    for k in (0, 2, 4):
                        act.wait_ge(kt_ready, it * 12 + (6 * s + k + 1))
                        dst = KTf[s][:, k, 0:PAST] if k < 4 else KTn[s][:, 0, 0:PAST]
                        nc.scalar.activation(dst, (b2, b3, b1)[k % 3], ACT.Copy).then_inc(kt_act, 1)
                    act.wait_ge(ks_ready, 2 * it + (s + 1))
                    nc.scalar.activation(KTf[s][:, :, PAST:L], b0[:, 128:160].rearrange("p (j n) -> p j n", j=4), ACT.Copy)
                    nc.scalar.activation(KTn[s][:, :, PAST:L], b0[:, 160:176].rearrange("p (j n) -> p j n", j=2), ACT.Copy).then_inc(ks_done, 1)
                for s in range(2):
                    b0, b1, b2, b3 = bk[4 * s:4 * s + 4]
                    act.wait_ge(sc_done, 2 * it + (s + 1))
                    nc.scalar.activation(sc[s][:, 1, 0:PAST], b2[0:HD, :], ACT.Copy)
                    nc.scalar.activation(sc[s][:, 2, 0:PAST], b3[0:HD, :], ACT.Copy).then_inc(sc_act, 1)
                for s in range(2):
                    act.wait_ge(m_ready, 2 * it + (s + 1))
                    for br in range(4):
                        x = sc[s][:, br, :] if br < 3 else scc[s][:, :]
                        ins = nc.scalar.activation(x, x, ACT.Exp, bias=srow[s][:, 0, br:br + 1], accum_out=srow[s][:, 1, br:br + 1])
                    ins.then_inc(e_ready, 1)
                for s in range(2):
                    b0, b1, b2, b3 = bk[4 * s:4 * s + 4]
                    act.wait_ge(pt2_ready, 2 * it + (s + 1))
                    nc.scalar.activation(PTb[s][:, 1, :, :], b2[:, 0:256].rearrange("p (j n) -> p j n", n=HD), ACT.Copy)
                    nc.scalar.activation(PTb[s][:, 2, :, :], b3[:, 0:256].rearrange("p (j n) -> p j n", n=HD), ACT.Copy).then_inc(pt2_act, 1)
                for s in range(2):
                    b0, b1, b2, b3 = bk[4 * s:4 * s + 4]
                    act.wait_ge(o2_ready, 2 * it + (s + 1))
                    act.wait_ge(os_st[s], it * (16 * N_OS) + CREDIT)
                    nc.scalar.activation(ofs[s][:, :], b1[0:TQ, :], ACT.Copy)
                    nc.scalar.activation(ons[s][:, :, :], b2[0:32, 0:P].rearrange("p (g d) -> p g d", g=G), ACT.Copy).then_inc(o2_done, 1)

        @block.vector
        def _(dve):
            ch = Chain(dve, dve_e)
            dve.wait_ge(e_set, 1)
            dve.wait_ge(g_ld, 16 * NH * 3)
            with dve.Fori(0, TURNS2) as it:
                ch.loop(it, SAMPLE_STEPS)
                for s in range(2):
                    dve.wait_ge(in_ld[s], it * (16 * N_LD) + 16 * N_LD)
                    nc.vector.tensor_copy(vcb[s][:, :], vcS[:, it * 2 + s, :])
                    nc.vector.tensor_copy(lf64[s][:, 0:PAGES, :, :].rearrange("p j h q -> p (j h) q"),
                                          lpage[s][:, :, :].rearrange("p j h -> p (j h)").unsqueeze(2).to_broadcast([P, PAGES * NH, TQ]))
                    nc.vector.tensor_copy(lf64[s][0:TQ, PAGES, :, :], lnew[s][:, :].unsqueeze(2).to_broadcast([TQ, NH, TQ])).then_inc(lf_ready, 1)
                for s in range(2):
                    b0, b1, b2, b3 = bk[4 * s:4 * s + 4]
                    dve.wait_ge(p1_ready, 2 * it + (s + 1))
                    q4 = Qf[s][:, :].rearrange("p (j c) -> p j c", c=80)
                    f4 = b0[:, 0:32].rearrange("p (j q) -> p j q", j=4)
                    nc.vector.tensor_copy(q4[0:HD, :, 0:8], f4[0:HD, :, :])
                    nc.vector.tensor_copy(q4[HD:P, :, 8:16], f4[HD:P, :, :])
                    nc.vector.tensor_copy(Qn[s][0:HD, 0:32], b0[0:HD, 32:64])
                    nc.vector.tensor_copy(Qn[s][HD:P, 32:64], b0[HD:P, 32:64]).then_inc(q_bd, 1)
                    ch.link(nc.vector.tensor_tensor_scan(negc[s][:, 0:PAST], ones512[:, :], b1[0:HD, :], 0.0, ALU.mult, ALU.add))
                    ch.link(nc.vector.tensor_tensor_scan(negc[s][:, PAST:L], ones512[:, 0:TQ], b0[0:HD, 64:72],
                                                         negc[s][:, PAST - 1:PAST], ALU.mult, ALU.add))
                    ch.link(nc.vector.tensor_scalar(negc[s][:, :], negc[s][:, :], -1.0, None, ALU.mult))
                    nc.vector.tensor_tensor(negc[s][:, PAST:L], negc[s][:, PAST:L], cst[0:HD, K_NEW:K_NEW + TQ], ALU.add).then_inc(negc_done, 1)
                for s in range(2):
                    b0, b1, b2, b3 = bk[4 * s:4 * s + 4]
                    for k in (1, 3, 5):
                        dve.wait_ge(kt_ready, it * 12 + (6 * s + k + 1))
                        dst = KTf[s][:, k, 0:PAST] if k < 4 else KTn[s][:, 1, 0:PAST]
                        nc.vector.tensor_copy(dst, (b2, b3, b1)[k % 3]).then_inc(kt_dve, 1)
                for s in range(2):
                    b0, b1, b2, b3 = bk[4 * s:4 * s + 4]
                    dve.wait_ge(sc_done, 2 * it + (s + 1))
                    dve.wait_ge(negc_done, 2 * it + (s + 1))
                    new = cst[0:HD, K_NEW:K_NEW + TQ].unsqueeze(1).to_broadcast([HD, 2, TQ])
                    nc.vector.tensor_tensor(sc[s][:, 0, 0:PAST], b1[0:HD, :], negc[s][:, 0:PAST], ALU.add)
                    nc.vector.tensor_tensor(sc[s][:, 0, PAST:L], b0[0:HD, 192:200], negc[s][:, PAST:L], ALU.add)
                    nc.vector.tensor_tensor(sc[s][:, 1:3, PAST:L], b0[0:HD, 200:216].rearrange("p (i n) -> p i n", i=2), new, ALU.add)
                    ch.link(nc.vector.tensor_copy(scc[s][:, :], b0[0:HD, 216:224]))
                    dve.wait_ge(sc_act, 2 * it + (s + 1))
                    ch.link(nc.vector.tensor_tensor(sc[s][:, 2, 0:TQ], sc[s][:, 2, 0:TQ], cst[0:HD, K_OLD:K_OLD + TQ], ALU.add))
                    nc.vector.tensor_reduce(srow[s][:, 0, 0:3], sc[s][:, :, :], AX.X, ALU.max, negate=True)
                    nc.vector.tensor_reduce(srow[s][:, 0, 3:4], scc[s][:, :], AX.X, ALU.max, negate=True).then_inc(m_ready, 1)
                for s in range(2):
                    dve.wait_ge(e_ready, 2 * it + (s + 1))
                    ch.link(nc.vector.reciprocal(srow[s][:, 2, :], srow[s][:, 1, :]))
                    w, g = srow[s][:, 2, :], gateS[:, :, bass.ds(it * 2 + s, 1)].rearrange("p r o -> p (r o)")
                    ch.link(nc.vector.tensor_tensor(w[:, 1:3], w[:, 1:3], g[:, 1:3], ALU.mult))
                    ch.link(nc.vector.tensor_tensor(w[:, 3:4], w[:, 3:4], g[:, 0:1], ALU.mult))
                    for br in range(4):
                        x = sc[s][:, br, :] if br < 3 else scc[s][:, :]
                        ins = nc.vector.tensor_scalar(x, x, w[:, br:br + 1], None, ALU.mult)
                    ins.then_inc(p_ready, 1)
                for s in range(2):
                    b0, b1, b2, b3 = bk[4 * s:4 * s + 4]
                    dve.wait_ge(pt2_ready, 2 * it + (s + 1))
                    nc.vector.tensor_copy(PTb[s][:, 0, :, :], b1[:, 0:256].rearrange("p (j n) -> p j n", n=HD))
                    nc.vector.tensor_copy(PTs[s][:, :, :], b0[0:TQ, 256:512].rearrange("p (j n) -> p j n", n=HD)).then_inc(pt2_dve, 1)
                ch.end(TURNS2)

    wo_ld, mx_ld, f_misc, gt_ready, gt_done, gb_ready, gb_done = (sem(n) for n in (
        "wout_loaded", "sample_mix_loaded", "gain2_ready", "gt1_transposed", "gt1_copied", "gt1_spread", "gt1b_ready"))
    x_ld = [sem(f"x_tile_loaded{i}") for i in range(2)]
    x1_st = [sem(f"x1_stored{i}") for i in range(2)]
    wu_ld = [sem(f"wup_loaded{i}") for i in range(2)]
    (mt_ready, mt_act, mt_dve, out_ready, x1_ready, sq2, var2, root2, rstd2, xn2, xt_ready, h2_act, h2_dve) = (sem(f"f_{n}") for n in (
        "mix_transposed", "mix_act", "mix_dve", "projected", "x1_ready", "squares", "variance", "root", "rstd", "xn_ready",
        "xn_transposed", "h_act", "h_dve"))
    dve_f = sem("dve_step_f")
    x1_tiles = [(x1_d[t * P:t * P + rows(t), :]) for t in range(T9)]

    with nc.Block() as block:

        @block.sync
        def _(sp):
            sp.dma_start(mix[0:NS, NT, :], mixs_d).then_inc(mx_ld, 16)
            for k in range(2):
                sp.dma_start(wo[:, 4 * k:4 * k + 4, :], wout_v[:, 4 * k:4 * k + 4, :]).then_inc(wo_ld, 16)
            for i in range(2):
                sp.dma_start(wu[i][:, :, :], wup_v[:, :, 256 * i:256 * (i + 1)]).then_inc(wu_ld[i], 16)
            for t in range(T9 + 1):
                if t < T9:
                    if t >= 2:
                        sp.wait_ge(x1_ready, t - 1)
                    src = xs_v if t == NT else xp_v[:, t, :]
                    sp.dma_start(xt[t % 2][0:rows(t), :], src).then_inc(x_ld[t % 2], 16)
                if t:
                    sp.wait_ge(x1_ready, t)
                    sp.dma_start(x1_tiles[t - 1], x1[(t - 1) % 2][0:rows(t - 1), :]).then_inc(x1_st[(t - 1) % 2], 16)
            sp.wait_ge(x1_st[0], 16 * 5)
            sp.wait_ge(x1_st[1], 16 * 4)

        @block.tensor
        def _(pe):
            for k in range(KC):
                last = nc.tensor.transpose(bk[k // 4][0:B + 1, P * (k % 4):P * (k % 4 + 1)], modT[:, 16 + k, :], ident)
            last.then_inc(gt_ready, 1)
            pe.wait_ge(gt_done, 1)
            for i, (col, r) in enumerate(((K_SELP, P), (K_SELS, NS))):
                for c in range(2):
                    last = nc.tensor.matmul(bk[2 + 2 * i + c][0:r, :], cst[0:B + 1, col:col + r], gt1n[:, 512 * c:512 * (c + 1)],
                                            start=True, stop=True)
            last.then_inc(gb_ready, 1)

            def mix_t(t):
                r = rows(t)
                if t:
                    pe.wait_ge(mt_act, t)
                    pe.wait_ge(mt_dve, t)
                if t == NT:
                    pe.wait_ge(mx_ld, 16)
                for k in range(KC):
                    last = nc.tensor.transpose(bk[k // 4][:, P * (k % 4):P * (k % 4) + r], mix[0:r, t, k * P:(k + 1) * P], ident[0:r, 0:r])
                last.then_inc(mt_ready, 1)

            def xn_t(t):
                r = rows(t)
                pe.wait_ge(xn2, t + 1)
                if t:
                    pe.wait_ge(h2_act, t)
                    pe.wait_ge(h2_dve, t)
                for k in range(KC):
                    last = nc.tensor.transpose(bk[6 + k // 4][:, P * (k % 4):P * (k % 4) + r], xn[t % 2][0:r, k * P:(k + 1) * P], ident[0:r, 0:r])
                last.then_inc(xt_ready, 1)

            mix_t(0)
            pe.wait_ge(gb_done, 1)
            pe.wait_ge(wo_ld, 32)
            for t in range(T9):
                r = rows(t)
                if t + 1 < T9:
                    mix_t(t + 1)
                else:
                    pe.wait_ge(mt_act, T9)
                    pe.wait_ge(mt_dve, T9)
                if t >= 2:
                    pe.wait_ge(x1_ready, t - 1)
                for c in range(2):
                    for k in range(KC):
                        last = nc.tensor.matmul(bk[2 + 2 * (t % 2) + c][0:r, :], mixT[t % 2][:, k, 0:r], wo[:, k, 512 * c:512 * (c + 1)],
                                                start=(k == 0), stop=(k == KC - 1))
                last.then_inc(out_ready, 1)
                if t:
                    xn_t(t - 1)
            xn_t(T9 - 1)

        @block.scalar
        def _(act):
            def mix_copy(t):
                r = rows(t)
                act.wait_ge(mt_ready, t + 1)
                nc.scalar.activation(mixT[t % 2][:, 0:4, 0:r], bk[0].rearrange("p (k n) -> p k n", k=4)[:, :, 0:r], ACT.Copy).then_inc(mt_act, 1)

            def h_copy(t):
                act.wait_ge(xt_ready, t + 1)
                act.wait_ge(f_misc, 1)
                for k in range(4):
                    last = nc.scalar.activation(h2T[:, k, t * P:(t + 1) * P], bk[6][:, P * k:P * (k + 1)], ACT.Identity,
                                                bias=modT[:, 24 + k, 0:1], scale=gain2[:, k, 0:1])
                last.then_inc(h2_act, 1)

            mix_copy(0)
            for t in range(T9):
                r = rows(t)
                if t + 1 < T9:
                    mix_copy(t + 1)
                act.wait_ge(x1_ready, t + 1)
                if t:
                    act.wait_ge(sq2, t)
                nc.scalar.activation(junk2[0:r, :], x1[t % 2][0:r, :], ACT.Square, accum_out=ssum[0:r, t:t + 1]).then_inc(sq2, 1)
                act.wait_ge(var2, t + 1)
                nc.scalar.activation(rstd[0:r, t:t + 1], ssum[0:r, t:t + 1], ACT.Sqrt).then_inc(root2, 1)
                act.wait_ge(rstd2, t + 1)
                if t >= 2:
                    act.wait_ge(xt_ready, t - 1)
                nc.scalar.activation(xn[t % 2][0:r, :], x1[t % 2][0:r, :], ACT.Copy, scale=rstd[0:r, t:t + 1]).then_inc(xn2, 1)
                if t:
                    h_copy(t - 1)

        @block.vector
        def _(dve):
            ch = Chain(dve, dve_f)
            nc.vector.scalar_tensor_tensor(gain2[:, :, :], modT[:, 32:40, :], 1.0,
                                           vecT[:, 56:64].unsqueeze(2).to_broadcast([P, KC, B + 1]), ALU.add, ALU.mult).then_inc(f_misc, 1)
            dve.wait_ge(gt_ready, 1)
            nc.vector.tensor_copy(gt1n[:, :], banks(0, 2)[0:B + 1, :]).then_inc(gt_done, 1)
            dve.wait_ge(gb_ready, 1)
            nc.vector.tensor_copy(gt1b[:, 0, :], banks(2, 2))
            ch.link(nc.vector.tensor_copy(gt1b[0:NS, 1, :], banks(4, 2)[0:NS, :]))
            nc.vector.nop().then_inc(gb_done, 1)

            def mix_copy(t):
                r = rows(t)
                dve.wait_ge(mt_ready, t + 1)
                nc.vector.tensor_copy(mixT[t % 2][:, 4:8, 0:r], bk[1].rearrange("p (k n) -> p k n", k=4)[:, :, 0:r]).then_inc(mt_dve, 1)

            def h_copy(t):
                dve.wait_ge(xt_ready, t + 1)
                dve.wait_ge(f_misc, 1)
                if t < NT:
                    for k in range(4, 8):
                        last = nc.vector.tensor_scalar(h2T[:, k, t * P:(t + 1) * P], bk[7][:, P * (k - 4):P * (k - 3)],
                                                       gain2[:, k, 0:1], modT[:, 24 + k, 0:1], ALU.mult, ALU.add)
                    last.then_inc(h2_dve, 1)
                    return
                hs = h2T[:, :, S:TOK].rearrange("p k (b t) -> p k b t", b=B)
                src = banks(6, 2).rearrange("p (k n) -> p k n", n=P)[:, :, 0:NS].rearrange("p k (b t) -> p k b t", b=B)
                ch.link(nc.vector.tensor_tensor(hs, src, gain2[:, :, 1:B + 1].unsqueeze(3).to_broadcast([P, KC, B, TQ]), ALU.mult))
                nc.vector.tensor_tensor(hs, hs, modT[:, 24:32, 1:B + 1].unsqueeze(3).to_broadcast([P, KC, B, TQ]), ALU.add).then_inc(h2_dve, 1)

            mix_copy(0)
            for t in range(T9):
                r = rows(t)
                if t + 1 < T9:
                    mix_copy(t + 1)
                dve.wait_ge(out_ready, t + 1)
                dve.wait_ge(x_ld[t % 2], 16 * (t // 2 + 1))
                if t >= 2:
                    dve.wait_ge(x1_st[t % 2], 16 * (t // 2))
                    dve.wait_ge(xn2, t - 1)
                ch.link(nc.vector.tensor_tensor(x1[t % 2][0:r, :], banks(2 + 2 * (t % 2), 2)[0:r, :], gt1b[0:r, int(t == NT), :], ALU.mult))
                nc.vector.tensor_tensor(x1[t % 2][0:r, :], x1[t % 2][0:r, :], xt[t % 2][0:r, :], ALU.add).then_inc(x1_ready, 1)
                dve.wait_ge(sq2, t + 1)
                nc.vector.tensor_scalar(ssum[0:r, t:t + 1], ssum[0:r, t:t + 1], 1.0 / D, EPS, ALU.mult, ALU.add).then_inc(var2, 1)
                dve.wait_ge(root2, t + 1)
                nc.vector.reciprocal(rstd[0:r, t:t + 1], rstd[0:r, t:t + 1]).then_inc(rstd2, 1)
                if t:
                    h_copy(t - 1)
            h_copy(T9 - 1)

    up_ready, up_ev, up_sq = sem("up_ready"), sem("up_copied"), sem("up_squared")
    NB2 = DFF // 256
    GROUPS = ((0, 512), (512, 1024), (1024, TOK))

    with nc.Block() as block:

        @block.sync
        def _(sp):
            with sp.Fori(0, NB2 // 2 - 1) as it:
                for s in range(2):
                    sp.wait_ge(up_ready, 4 * it + (2 * s + 2))
                    sp.dma_start(wu[s][:, :, :], wup_v[:, :, bass.ds(it * 512 + (256 * s + 512), 256)]).then_inc(wu_ld[s], 16)

        @block.tensor
        def _(pe):
            with pe.Fori(0, NB2 // 2) as it:
                for j in range(4):
                    s, c = j // 2, j % 2
                    if c == 0:
                        pe.wait_ge(wu_ld[s], it * 16 + 16)
                    pe.wait_ge(up_ev, it * 4 + (j - 1 + 2 * CREDIT))
                    for k in range(KC):
                        for i, (a, z) in enumerate(GROUPS):
                            last = nc.tensor.matmul(bk[3 * c + i][:, 0:z - a], wu[s][:, k, P * c:P * (c + 1)], h2T[:, k, a:z],
                                                    start=(k == 0), stop=(k == KC - 1))
                    last.then_inc(up_ready, 1)

        @block.scalar
        def _(act):
            nc.scalar.nop().then_inc(up_ev, 2 * CREDIT)
            with act.Fori(0, NB2 // 2) as it:
                for j in range(4):
                    c = j % 2
                    act.wait_ge(up_ready, it * 4 + (j + 1))
                    nc.scalar.activation(u2T[:, it * 4 + j, 0:1024], banks(3 * c, 2), ACT.Relu)
                    nc.scalar.activation(u2T[:, it * 4 + j, 1024:TOK], bk[3 * c + 2][:, 0:NS], ACT.Relu).then_inc(up_ev, 1)

        @block.vector
        def _(dve):
            with dve.Fori(0, NB2 // 2) as it:
                for j in range(4):
                    dve.wait_ge(up_ev, it * 4 + (j + 1 + 2 * CREDIT))
                    u = u2T[:, it * 4 + j, :]
                    nc.vector.tensor_tensor(u, u, u, ALU.mult).then_inc(up_sq, 1)

    PIECES = 4
    FP = FC // PIECES
    wd_ld = [[sem(f"wdown_loaded{i}_{j}") for j in range(PIECES)] for i in range(2)]
    xc_ld = [sem(f"x1_columns_loaded{i}") for i in range(2)]
    yc_st = [sem(f"y_columns_stored{i}") for i in range(2)]
    y_ready, y_act, y_dve, yt_ready, yo_ready = (sem(n) for n in ("y_ready", "y_act", "y_dve", "y_transposed", "y_added"))

    with nc.Block() as block:

        @block.sync
        def _(sp):
            def load_w(m, s):
                for j in range(PIECES):
                    sp.dma_start(wd[s][:, FP * j:FP * (j + 1), :], wdn_v[:, FP * j:FP * (j + 1), bass.ds(m * P, P)]).then_inc(wd_ld[s][j], 16)

            def load_x(m, s):
                sp.dma_start(xc[s][:, 0:NT, :], x1_d[0:S, bass.ds(m * P, P)].rearrange("(t p) n -> p t n", p=P)).then_inc(xc_ld[s], 16)
                sp.dma_start(xc[s][0:NS, NT, :], x1_d[S:TOK, bass.ds(m * P, P)]).then_inc(xc_ld[s], 16)

            def store(m, s):
                sp.dma_start(yp_v[:, :, bass.ds(m * P, P)], xc[s][:, 0:NT, :]).then_inc(yc_st[s], 16)
                sp.dma_start(ys_v[:, bass.ds(m * P, P)], xc[s][0:NS, NT, :]).then_inc(yc_st[s], 16)

            for s in range(2):
                load_w(s, s)
                load_x(s, s)
            with sp.Fori(0, KC // 2 - 1) as it:
                for s in range(2):
                    sp.wait_ge(y_ready, 2 * it + (s + 1))
                    load_w(2 * it + (s + 2), s)
                for s in range(2):
                    sp.wait_ge(yo_ready, 2 * it + (s + 1 + 2 * CREDIT))
                    store(2 * it + s, s)
                    sp.wait_ge(yc_st[s], it * 32 + 32)
                    load_x(2 * it + (s + 2), s)
            for s in range(2):
                sp.wait_ge(yo_ready, KC - 1 + s + 2 * CREDIT)
                store(KC - 2 + s, s)
            for s in range(2):
                sp.wait_ge(yc_st[s], 32 * (KC // 2))

        @block.tensor
        def _(pe):
            with pe.Fori(0, KC // 2) as it:
                for s in range(2):
                    pe.wait_ge(y_act, 2 * it + CREDIT)
                    pe.wait_ge(y_dve, 2 * it + CREDIT)
                    pe.wait_ge(yo_ready, 2 * it + (s - 1 + 2 * CREDIT))
                    for f in range(FC):
                        if f % FP == 0:
                            pe.wait_ge(wd_ld[s][f // FP], it * 16 + 16)
                        for i, (a, z) in enumerate(GROUPS):
                            last = nc.tensor.matmul(bk[3 * s + i][:, 0:z - a], wd[s][:, f, :], u2T[:, f, a:z],
                                                    start=(f == 0), stop=(f == FC - 1))
                    last.then_inc(y_ready, 1)
                for s in range(2):
                    pe.wait_ge(y_act, 2 * it + (s + 1 + CREDIT))
                    pe.wait_ge(y_dve, 2 * it + (s + 1 + CREDIT))
                    pe.wait_ge(yo_ready, 2 * it + (s + 2 * CREDIT))
                    for t in range(NT):
                        nc.tensor.transpose(bk[6 + t // 4][:, P * (t % 4):P * (t % 4 + 1)], yT[s][:, t * P:(t + 1) * P], ident)
                    nc.tensor.transpose(bk[3 * s + 2][0:NS, P:2 * P], yT[s][:, S:TOK], ident).then_inc(yt_ready, 1)

        @block.scalar
        def _(act):
            nc.scalar.nop().then_inc(y_act, CREDIT)
            with act.Fori(0, KC // 2) as it:
                for s in range(2):
                    act.wait_ge(y_ready, 2 * it + (s + 1))
                    nc.scalar.activation(yT[s][:, 0:1024], banks(3 * s, 2), ACT.Copy,
                                         scale=modT[:, 40 + (2 * it + s), 0:1]).then_inc(y_act, 1)

        @block.vector
        def _(dve):
            nc.vector.nop().then_inc(y_dve, CREDIT)
            nc.vector.nop().then_inc(yo_ready, 2 * CREDIT)
            with dve.Fori(0, KC // 2) as it:
                for s in range(2):
                    dve.wait_ge(y_ready, 2 * it + (s + 1))
                    g = modT[:, 40 + (2 * it + s), 1:B + 1].unsqueeze(2).to_broadcast([P, B, TQ])
                    nc.vector.tensor_tensor(yT[s][:, S:TOK].rearrange("p (b t) -> p b t", b=B),
                                            bk[3 * s + 2][:, 0:NS].rearrange("p (b t) -> p b t", b=B), g, ALU.mult).then_inc(y_dve, 1)
                for s in range(2):
                    dve.wait_ge(yt_ready, 2 * it + (s + 1))
                    dve.wait_ge(xc_ld[s], it * 32 + 32)
                    nc.vector.tensor_tensor(xc[s][:, 0:NT, :], banks(6, 2).rearrange("p (t n) -> p t n", n=P), xc[s][:, 0:NT, :], ALU.add)
                    nc.vector.tensor_tensor(xc[s][0:NS, NT, :], bk[3 * s + 2][0:NS, P:2 * P], xc[s][0:NS, NT, :], ALU.add).then_inc(yo_ready, 1)


_INS = ['x_prompt', 'x_sample', 'c_prompt', 'c_sample', 'cache_fox_kv', 'cache_fox_logf', 'cache_nsa_kv',
        'state_nsa_win', 'page_table', 'w_ada', 'b_ada', 'norm1_g', 'norm2_g', 'w_in', 'b_forget', 'b_gate',
        'g_q_fox', 'g_k_fox', 'g_q_nsa', 'g_k_nsa', 'pe_cmp', 'w_cmp', 'w_out', 'w_up', 'w_down']
_OUTS = [((1, S, D), 'float32'), ((B, TQ, D), 'float32'),
         ((1, 1, S, 2, NH, HD), 'float32'), ((1, B, TQ, 2, NH, HD), 'float32'),
         ((1, 1, S, NH), 'float32'), ((1, B, TQ, NH), 'float32'),
         ((1, 1, S, 4, G, HD), 'float32'), ((1, B, TQ, 4, G, HD), 'float32'),
         ((1, 1, 512, 2, G, HD), 'float32'), ((1, B, PAST, 2, G, HD), 'float32')]


def kernel(**inputs):
    import numpy as _np
    import concourse.bacc as _bacc
    from concourse import mybir as _mybir
    from concourse.bass_utils import run_bass_kernel_spmd as _run

    nc = _bacc.Bacc("TRN2", target_bir_lowering=False, num_devices=1)
    arrays, args = {}, []
    for name in _INS + ['constants']:
        a = constants() if name == 'constants' else _np.ascontiguousarray(inputs[name])
        arrays[f"in_{name}_dram"] = a
        args.append(nc.dram_tensor(f"in_{name}_dram", a.shape, _mybir.dt.from_np(a.dtype), kind="ExternalInput").ap())
    for i, (shape, dtype) in enumerate(_OUTS):
        dt = _mybir.dt.from_np(_np.dtype(dtype))
        args.append(nc.dram_tensor(f"out_{i}_dram", shape, dt, kind="ExternalOutput").ap())
    layer_kernel(nc, *args)
    r = _run(nc, [arrays], core_ids=[0])
    return tuple(r.results[0][f"out_{i}_dram"] for i in range(len(_OUTS)))
```

```python
import numpy as np

import concourse.bass as bass
from concourse import mybir

F32 = mybir.dt.float32
F32R = mybir.dt.float32r
I32 = mybir.dt.int32
ALU = mybir.AluOpType
ACT = mybir.ActivationFunctionType
AX = mybir.AxisListType

P = 128
D = 1024
KC = D // P
NT = 8
T9 = NT + 1
S = NT * P
B, TQ = 8, 8
NS = B * TQ
TOK = S + NS
HD = 64
NH = 8
G = 2
PAST = 512
PAGES = PAST // P
L = PAST + TQ
BLOCK = 64
NBP = S // BLOCK
NBS = PAST // BLOCK
DFF = 4096
FC = DFF // P
EPS = 1e-6
SCALE = HD ** -0.5
NEG = -1e30
CREDIT = 1
EXP_MAX = 88.0

C_QF, C_KF, C_VF, C_F, C_QN, C_KV = 0, 512, 1024, 1536, 1544, 2056
C_WIN = C_KV + 512
N_MISC = 256 + 24
ZB = ["misc", "kf", "vf", "qf", "qn", "cs"]
ZW = {"misc": N_MISC + 8, "kf": 512, "vf": 512, "qf": 512, "qn": 512, "cs": 512}
ZC = {"kf": C_KF, "vf": C_VF, "qf": C_QF, "qn": C_QN, "cs": C_KV}

K_ID, K_U, K_ONE, K_CAUS, K_WIN, K_CMP, K_ANY = 0, 128, 256, 384, 512, 640, 768
K_COS, K_SIN, K_SELP, K_SELS, K_NEW, K_OLD = 769, 913, 1057, 1185, 1249, 1257
K_N = 1265


def constants():
    c = np.zeros((P, K_N), np.float32)
    p = np.arange(P)[:, None]
    f = np.arange(P)[None, :]
    c[:, K_ID:K_ID + P] = p == f
    c[:, K_U:K_U + P] = p <= f
    c[:, K_ONE:K_ONE + P] = 1
    c[:, K_CAUS:K_CAUS + P] = np.where(f <= p, 0, NEG)
    c[:, K_WIN:K_WIN + P] = np.where(f > p, 0, NEG)
    for t in range(NT):
        blk = np.arange(NBP)[None, :]
        c[:, K_CMP + NBP * t:K_CMP + NBP * (t + 1)] = np.where((blk + 1) * BLOCK <= t * P + p + 1, 0, NEG)
    c[:, K_ANY] = (np.arange(P) + 1 >= BLOCK)
    half = 8
    inv = (np.float32(500000.0) ** (-np.arange(half, dtype=np.float32) / np.float32(half))).astype(np.float32)
    for t in range(T9):
        pos = t * P + np.arange(P) if t < NT else PAST + np.arange(P) % TQ
        ang = pos.astype(np.float32)[:, None] * inv[None, :]
        co, si = np.cos(ang), np.sin(ang)
        c[:, K_COS + 16 * t:K_COS + 16 * t + 16] = np.concatenate([co, co], 1)
        c[:, K_SIN + 16 * t:K_SIN + 16 * t + 16] = np.concatenate([-si, si], 1)
    c[0, K_SELP:K_SELP + P] = 1
    for b in range(B):
        c[b + 1, K_SELS + b * TQ:K_SELS + (b + 1) * TQ] = 1
    q, k = (np.arange(HD) % TQ)[:, None], np.arange(TQ)[None, :]
    c[:HD, K_NEW:K_NEW + TQ] = np.where(k <= q, 0, NEG)
    c[:HD, K_OLD:K_OLD + TQ] = np.where(k > q, 0, NEG)
    return c


class Chain:

    def __init__(self, eng, sem):
        self.eng, self.sem = eng, sem
        self.base, self.k, self.reg, self.per = 0, 0, None, 0

    def loop(self, reg, per):
        self.base += self.k
        self.k, self.reg, self.per = 0, reg, per

    def end(self, times):
        assert self.k == self.per, ("steps in the loop", self.k, self.per)
        self.base, self.k, self.reg = self.base + times * self.per, 0, None

    def link(self, ins):
        self.k += 1
        ins.then_inc(self.sem, 1)
        n = self.base + self.k
        self.eng.wait_ge(self.sem, n if self.reg is None else self.reg * self.per + n)


def rows(t):
    return P if t < NT else NS


def attention_units(kinds):
    out = []
    for t in range(NT):
        for kind in kinds:
            if kind == "cmp":
                out.append((kind, t, 0, 1))
            elif kind == "win":
                lo = max(0, t - 4)
                out.append((kind, t, lo, t + 1 - lo))
            else:
                out.append((kind, t, 0, t + 1))
    return out


def layer_kernel(nc, x_prompt, x_sample, c_prompt, c_sample, cache_fox_kv, cache_fox_logf, cache_nsa_kv,
                 state_nsa_win, page_table, w_ada, b_ada, norm1_g, norm2_g, w_in, b_forget, b_gate,
                 g_q_fox, g_k_fox, g_q_nsa, g_k_nsa, pe_cmp, w_cmp, w_out, w_up, w_down, consts,
                 y_p, y_s, fkv_p, fkv_s, flf_p, flf_s, nkv_p, nkv_s, win_p, win_s):
    n_pool = cache_fox_kv.shape[1]
    xp_v = x_prompt.rearrange("a (t p) d -> p (a t) d", p=P)
    xs_v = x_sample.rearrange("b t d -> (b t) d")
    wada_v = w_ada.rearrange("a (k p) n -> p (a k) n", p=P)
    win_v = w_in.rearrange("a (k p) n -> p (a k) n", p=P)
    wout_v = w_out.rearrange("a (k p) n -> p (a k) n", p=P)
    wup_v = w_up.rearrange("a (k p) n -> p (a k) n", p=P)
    wdn_v = w_down.rearrange("a (f p) n -> p (a f) n", p=P)
    cfox_v = cache_fox_kv.rearrange("a n p k h d -> (a n) p (k h d)")
    clf_v = cache_fox_logf.rearrange("a n p h -> (a n) p h")
    cnsa_v = cache_nsa_kv.rearrange("a n p k g d -> (a n) p (k g d)")
    stw_v = state_nsa_win.rearrange("a b (j p) k g d -> (a b) p j (k g d)", p=P)
    stw_rows = state_nsa_win.rearrange("a b s k g d -> (a b) s (k g d)")
    fkvp_v = fkv_p.rearrange("a b (t p) k h d -> (a b t) p k (h d)", p=P)
    fkvs_v = fkv_s.rearrange("a b t k h d -> (a b t) k (h d)")
    fkvs_b = fkv_s.rearrange("a b t k h d -> (a b) t (k h d)")
    nkvp_v = nkv_p.rearrange("a b (t p) k g d -> (a b t) p (k g d)", p=P)
    nkvs_v = nkv_s.rearrange("a b t k g d -> (a b t) (k g d)")
    nkvs_b = nkv_s.rearrange("a b t k g d -> (a b) t (k g d)")
    winp_v = win_p.rearrange("a b (t p) k g d -> (a b t) p (k g d)", p=P)
    wins_v = win_s.rearrange("a b s k g d -> (a b) s (k g d)")
    flfs_b = flf_s.rearrange("a b t h -> (a b) t h")
    yp_v = y_p.rearrange("a (t p) d -> p (a t) d", p=P)
    ys_v = y_s.rearrange("b t d -> (b t) d")
    qt_d = nc.dram_tensor("qt_scratch", [2, NH, HD, S], F32, kind="Internal").ap()
    qs_d = nc.dram_tensor("qs_scratch", [NS, D], F32, kind="Internal").ap()
    gs_d = nc.dram_tensor("gs_scratch", [NS, 24], F32, kind="Internal").ap()
    mixs_d = nc.dram_tensor("mixs_scratch", [NS, D], F32, kind="Internal").ap()
    x1_d = nc.dram_tensor("x1_scratch", [TOK, D], F32, kind="Internal").ap()

    ARENA = 16640

    def at(name, shape, off, dt=F32):
        return nc.alloc_sbuf_tensor_at(name, shape, dt, offset=ARENA + off)

    small = [0]

    def keep(name, shape, dt=F32):
        n = 4
        for s in shape[1:]:
            n *= s
        off = small[0]
        small[0] += (n + 31) // 32 * 32
        return at(name, shape, off, dt)

    cst = keep("cst", [P, K_N])
    modT = keep("modT", [P, 6 * KC, B + 1])
    vecT = keep("vecT", [P, HD])
    gain1 = keep("gain1", [P, KC, B + 1])
    gain2 = keep("gain2", [P, KC, B + 1])
    gates = keep("gates", [P, T9, 24])
    logf = keep("logf", [P, T9, NH])
    ssum = keep("ssum", [P, 16])
    rstd = keep("rstd", [P, 16])
    gate_qk = keep("gate_qk", [P, 2, 4])
    nmax = keep("nmax", [P, 2, 4])
    scT = keep("scT", [P, KC, B + 1])
    ptab = keep("ptab", [1, B * PAGES], I32)
    kcS = keep("kcS", [P, B * NBS])
    kcP = keep("kcP", [HD + 1, G, NBP])
    vcP = keep("vcP", [P, G, HD + 1])
    gateS = keep("gateS", [HD, 3, B])
    SMALL = small[0]
    assert SMALL <= 14336, SMALL
    KV = 14336
    kTf = at("kTf", [HD + 1, NH, S], KV)
    Vf = at("Vf", [P, NT, NH, HD + 1], KV + 32768)
    kTs = at("kTs", [HD, G, S], KV + 49408)
    kTw = at("kTw", [HD, G, S], KV + 57600)
    Vs = at("Vs", [P, NT, G, HD + 1], KV + 65792)
    Vw = at("Vw", [P, NT, G, HD + 1], KV + 69952)
    XC = 88448
    Xc = at("Xc", [P, NBP + B * NBS, 2, BLOCK], XC)
    HT = 96640
    hT = at("hT", [P, KC, TOK], HT)
    WB = 131456
    wbuf = [at(f"wbuf{i}", [P, KC, 512], WB + 16384 * i) for i in range(3)]
    ST = WB + 3 * 16384
    zsb = [at(f"zsb{i}", [P, 512], ST + 2048 * i) for i in range(5)]
    sq = [at(f"sq{i}", [P, 512], ST + 10240 + 2048 * i) for i in range(2)]
    qst = [at(f"qst{i}", [HD, NH, P], ST + 14336 + 4096 * i) for i in range(2)]
    rope = [at(f"rope{i}", [P, NH, 16], ST + 22528 + 512 * i) for i in range(2)]
    EXTRA = ST + 23552
    gvec = at("gvec", [P, 6, HD], EXTRA)
    hv = [at(f"hv{i}", [P, 3, NH], EXTRA + 1536 + 96 * i) for i in range(3)]
    graw = at("graw", [P, T9, 32], EXTRA + 1824)
    gexp = at("gexp", [P, T9, 32], EXTRA + 2976)
    bias32 = at("bias32", [P, 32], EXTRA + 4128)
    peT = at("peT", [P, 2, BLOCK], EXTRA + 4256)
    csum = at("csum", [P, NT, NH], EXTRA + 4768)
    cpre = at("cpre", [P, NT, NH], EXTRA + 5024)
    nCT = at("nCT", [HD, P], EXTRA + 5280)
    lnv = at("lnv", [P, T9, NH], EXTRA + 5792)
    assert ARENA + EXTRA + 6080 <= 229344
    xb = at("xb", [P, T9, D], KV)
    c9 = at("c9", [B + 1, D], KV + 36864)
    c9e = at("c9e", [B + 1, D], KV + 40960)
    vecn = at("vecn", [HD, P], KV + 45056)
    pen = at("pen", [BLOCK, 2, 2, HD], KV + 45568)
    junk = at("junk", [P, D], KV + 46592)
    cpage = [at(f"cpage{i}", [P, PAGES, 256], WB + 4096 * i) for i in range(2)]
    wbd = [at(f"wbd{i}", [P, 2, 8, P], WB + 8192 + 8192 * i) for i in range(2)]
    kvcT = at("kvcT", [P, 2, NBP + B * NBS], WB + 24576)
    vcS = at("vcS", [NBS, B, P], WB + 77120)
    qT = [at(f"qT{i}", [HD + 1, S], XC + 4096 * i) for i in range(2)]
    prob = [at(f"prob{i}", [P, S], XC + 8192 + 4096 * i) for i in range(2)]
    probT = [at(f"probT{i}", [P, NT, P], XC + 16384 + 4096 * i) for i in range(2)]
    mix = at("mix", [P, T9, D], WB)
    k2 = [at(f"k2_{i}", [P, S], XC + 24576 + 4096 * i, F32R) for i in range(2)]
    k3 = [at(f"k3_{i}", [P, S], XC + 32768 + 4096 * i, F32R) for i in range(2)]
    q2 = [at(f"q2_{i}", [P, S], WB + 36864 + 4096 * i, F32R) for i in range(2)]
    q3 = [at(f"q3_{i}", [P, S], WB + 45056 + 4096 * i, F32R) for i in range(2)]
    ks2 = at("ks2", [P, G, S], WB + 53248, F32R)
    kw2 = at("kw2", [P, G, S], WB + 61440, F32R)
    assert XC + 40960 <= WB
    fpage = [at(f"fpage{i}", [P, PAGES, D], KV + 16384 * i) for i in range(2)]
    npage = [at(f"npage{i}", [P, PAGES, 256], KV + 32768 + 4096 * i) for i in range(2)]
    wpage = [at(f"wpage{i}", [P, PAGES, 256], KV + 40960 + 4096 * i) for i in range(2)]
    o = KV + 49152
    lpage, fnew, nnew, wnew, qrow, lnew, vcb = [], [], [], [], [], [], []
    for i in range(2):
        fnew.append(at(f"fnew{i}", [TQ, D], o)); o += 4096
        qrow.append(at(f"qrow{i}", [TQ, D], o)); o += 4096
        nnew.append(at(f"nnew{i}", [TQ, 256], o)); o += 1024
        wnew.append(at(f"wnew{i}", [TQ, 256], o)); o += 1024
        lpage.append(at(f"lpage{i}", [P, PAGES, NH], o)); o += 128
        lnew.append(at(f"lnew{i}", [TQ, NH], o)); o += 32
        vcb.append(at(f"vcb{i}", [NBS, P], o)); o += 512
    assert o <= KV + 74112
    KTf = [at(f"KTf{i}", [P, 4, L], XC + 8320 * i) for i in range(2)]
    KTn = [at(f"KTn{i}", [P, 2, L], XC + 16640 + 4160 * i) for i in range(2)]
    o = WB + 36864
    sc, scc, negc, lf64, Qf, Qn, PTb, PTs, ofs, ons, srow, csa = ([] for _ in range(12))
    for i in range(2):
        sc.append(at(f"sc{i}", [HD, 3, L], o)); o += 6240
        scc.append(at(f"scc{i}", [HD, NBS], o)); o += 32
        negc.append(at(f"negc{i}", [HD, L], o)); o += 2080
        lf64.append(at(f"lf64{i}", [P, PAGES + 1, NH, TQ], o)); o += 1280
        Qf.append(at(f"Qf{i}", [P, 320], o)); o += 1280
        Qn.append(at(f"Qn{i}", [P, HD], o)); o += 256
        PTb.append(at(f"PTb{i}", [P, 3, PAGES, HD], o)); o += 3072
        PTs.append(at(f"PTs{i}", [TQ, 4, HD], o)); o += 1024
        ofs.append(at(f"ofs{i}", [TQ, 512], o)); o += 2048
        ons.append(at(f"ons{i}", [32, G, HD], o)); o += 512
        srow.append(at(f"srow{i}", [HD, 4, 4], o)); o += 64
    ones512 = at("ones512", [HD, PAST], o); o += 2048
    assert ARENA + o <= 229344, o
    TP = 3 * 364
    h2hi = at("h2hi", [P, KC, TP], KV, F32R)
    h2lo = at("h2lo", [P, KC, TP], KV + 34944, F32R)
    wo = at("wo", [P, KC, D], KV + 69888)
    gt1b = at("gt1b", [P, 2, D], KV + 69888 + 32768)
    gt1n = at("gt1n", [B + 1, D], KV + 69888 + 40960)
    h2s = [at("h2s0", [P, KC, P], KV + 69888 + 40960)]
    assert KV + 69888 + 45056 <= WB
    o = WB + 36864
    mixT = [at(f"mixT{i}", [P, KC, P], o + 4096 * i) for i in range(2)]; o += 8192
    xt = [at(f"xt{i}", [P, D], o + 4096 * i) for i in range(2)]; o += 8192
    x1 = [at(f"x1{i}", [P, D], o + 4096 * i) for i in range(2)]; o += 8192
    xn = [at(f"xn{i}", [P, D], o + 4096 * i) for i in range(2)]; o += 8192
    junk2 = at("junk2", [P, D], o); o += 4096
    h2s.append(at("h2s1", [P, KC, P], o)); o += 4096
    assert ARENA + o <= 229344
    UC = 4
    o = KV + 69888
    u2hi = at("u2hi", [P, UC, TP], o, F32R); o += UC * TP * 4
    u2lo = at("u2lo", [P, UC, TP], o, F32R); o += UC * TP * 4
    yT = at("yT", [P, KC, TP], o); o += KC * TP * 4
    us = [at(f"us{i}", [P, TP], o + 4384 * i) for i in range(2)]; o += 8768
    whi = [at(f"whi{i}", [P, D], o + 4096 * i, F32R) for i in range(2)]; o += 8192
    wlo = [at(f"wlo{i}", [P, D], o + 4096 * i, F32R) for i in range(2)]; o += 8192
    wraw = [at(f"wraw{i}", [P, D], o + 4096 * i) for i in range(2)]; o += 8192
    xo = [at(f"xo{i}", [P, D], o + 4096 * i) for i in range(3)]; o += 12288
    assert ARENA + o <= 229344

    bank = nc.alloc_psum_tensor("bank", [P, 8, 512], F32)
    bk = [bank[:, i, :] for i in range(8)]

    def banks(i, n):
        return bank[:, i:i + n, :].rearrange("p a b -> p (a b)")

    sem = nc.alloc_semaphore

    ident = cst[:, K_ID:K_ID + P]

    s_const, s_c, s_vec, s_gvec, s_pe, s_pt = (sem(n) for n in (
        "const_loaded", "c_loaded", "vec_loaded", "gvec_loaded", "pe_loaded", "ptab_loaded"))
    s_x = [sem(f"x_loaded{i}") for i in range(3)]
    w_ld = [sem(f"w_loaded{i}") for i in range(3)]
    c_neg, c_exp, c_silu, t0_ready, sc_ready = (sem(n) for n in (
        "c_negated", "c_exp_done", "c_silu_done", "small_transposed", "small_copied"))
    ln_sq, ln_var, ln_root, xn_done, ln_t, ln_ea, ln_ed = (sem(n) for n in (
        "ln_squares", "ln_variance", "ln_root", "xn_ready", "ln_transposed", "ln_copied_act", "ln_copied_dve"))
    ada_ready, ada_ev, mod_ready, mod_a, mod_d = (sem(n) for n in (
        "ada_ready", "ada_stored", "gain_ready", "h_act", "h_dve"))
    z_ready, z_ev, z_var, z_root, z_scaled, pool_done, tz_ready, tz_a, tz_d = (sem(n) for n in (
        "z_ready", "z_copied", "z_variance", "z_root", "z_scaled", "z_normed", "z_transposed",
        "zt_copied_act", "zt_copied_dve"))
    z_st = [sem(f"z_stored{i}") for i in range(5)]
    q_st = [sem(f"qt_stored{i}") for i in range(2)]
    misc_set, kv_set, g_arg, g_exp, g_one, g_ln, g_done = (sem(n) for n in (
        "misc_cleared", "kv_ones_set", "gate_args", "gate_exps", "gate_ones", "gate_logs", "gates_done"))
    c_ready, c_neg2, ct_ready, ct_copied, ct_moved = (sem(n) for n in (
        "csum_ready", "csum_negated", "csum_transposed", "csum_copied", "csum_moved"))
    misc_st, copy_st = sem("logf_stored"), sem("window_copied")
    dve_a, pool_a = sem("dve_step_a"), sem("pool_step_a")
    phase1_sems = [s_const, s_c, s_vec, s_gvec, s_pe, *s_x, *w_ld, c_neg, c_exp, c_silu, t0_ready, sc_ready, ln_sq, ln_var,
                   ln_root, xn_done, ln_t, ln_ea, ln_ed, ada_ready, ada_ev, mod_ready, mod_a, mod_d, z_ready, z_ev, z_var,
                   z_root, z_scaled, pool_done, tz_ready, tz_a, tz_d, *z_st, *q_st, misc_set, kv_set, g_arg, g_exp, g_one,
                   g_ln, g_done, c_ready, c_neg2, ct_ready, ct_copied, ct_moved, misc_st, copy_st, dve_a, pool_a]

    jobs = [(b, t) for b in range(len(ZB)) for t in range(T9)]
    NJ = len(jobs)
    LAG = 2
    tz_index, tz_eng = {}, []
    for J, (b, t) in enumerate(jobs):
        if t < NT and ZB[b] != "vf":
            tz_index[J] = len(tz_eng)
            tz_eng.append("d" if ZB[b] == "cs" else "a")
    tz_order = [tz_eng[:i + 1].count(e) for i, e in enumerate(tz_eng)]
    q_index = {J: i for i, J in enumerate(J for J in tz_index if ZB[jobs[J][0]] in ("qf", "qn"))}
    normed = [J for J, (b, t) in enumerate(jobs) if ZB[b] != "vf"]
    n_index = {J: i for i, J in enumerate(normed)}
    pool_jobs = [J for J, (b, t) in enumerate(jobs) if not (ZB[b] == "vf" and t == NT)]
    pool_count = [sum(j <= J for j in pool_jobs) for J in range(NJ)]
    ada1 = 4
    ada_after = [4, 13, 22, 26, 31, 35, 40, 49]
    csum_after = 12
    loads01 = {0: [1, 1, 2, 1, 1], 1: [1, 1, 1, 1, 1]}

    def loaded(buf, item):
        return 16 * sum(loads01[buf][:item + 1])

    def z_stores(J):
        b, t = jobs[J]
        name, z, r = ZB[b], zsb[J % 5], rows(t)
        if name == "misc":
            if t == NT:
                return [(wins_v[q, PAST - TQ:PAST, :], z[q * TQ:(q + 1) * TQ, 0:256]) for q in range(B)]
            return [(winp_v[t - 4, :, :], z[:, 0:256])] if t >= 4 else []
        if name in ("kf", "vf"):
            i = int(name == "vf")
            return [(fkvs_v[:, i, :] if t == NT else fkvp_v[t, :, i, :], z[0:r, :])]
        if name in ("qf", "qn"):
            i = int(name == "qn")
            return [(qs_d[:, 512 * i:512 * (i + 1)], z[0:NS, :])] if t == NT else []
        return [(nkvs_v if t == NT else nkvp_v[t, :, :], z[0:r, :])]

    def stored(J):
        return 16 * sum(len(z_stores(j)) for j in range(J + 1) if j % 5 == J % 5)

    def k_heads(name, z, r, w):
        if name == "cs":
            return z[0:r, :].rearrange("p (a k h d) -> p a k h d", a=2, k=2, h=G)[:, :, 0, :, 0:w]
        n = G if name == "misc" else NH
        return z[0:r, 0:n * HD].rearrange("p (h d) -> p h d", d=HD)[:, :, 0:w]

    with nc.Block() as block:

        @block.sync
        def _(sp):
            sp.dma_start(c9[0:1, :], c_prompt).then_inc(s_c, 16)
            sp.dma_start(c9[1:B + 1, :], c_sample).then_inc(s_c, 16)
            sp.dma_start(vecn[0:48, :], b_ada.rearrange("a (n p) -> (a n) p", p=P)).then_inc(s_vec, 16)
            sp.dma_start(vecn[48:56, :], norm1_g.rearrange("a (n p) -> (a n) p", p=P)).then_inc(s_vec, 16)
            sp.dma_start(vecn[56:64, :], norm2_g.rearrange("a (n p) -> (a n) p", p=P)).then_inc(s_vec, 16)
            sp.dma_start(cst[:, :], consts).then_inc(s_const, 16)
            sp.dma_start(xb[:, 0:4, :], xp_v[:, 0:4, :]).then_inc(s_x[0], 16)
            sp.dma_start(wbuf[0][:, :, :], wada_v[:, :, 0:512]).then_inc(w_ld[0], 16)
            sp.dma_start(xb[:, 4:8, :], xp_v[:, 4:8, :]).then_inc(s_x[1], 16)
            sp.dma_start(xb[0:NS, NT, :], xs_v).then_inc(s_x[2], 16)
            for i in range(2):
                sp.dma_start(pen[:, :, i, :], pe_cmp.rearrange("a k p d -> p (a k) d")).then_inc(s_pe, 16)
            sp.dma_start(wbuf[1][:, :, :], wada_v[:, :, 512:1024]).then_inc(w_ld[1], 16)
            for i, g in enumerate((g_q_fox, g_k_fox, g_q_nsa)):
                sp.dma_start(gvec[:, i, :], g[0, :].partition_broadcast(P)).then_inc(s_gvec, 16)
            sp.dma_start(gvec[:, 3:6, :], g_k_nsa[0, :, :].partition_broadcast(P)).then_inc(s_gvec, 16)
            sp.dma_start(bias32[:, 0:24], b_gate[0, :].partition_broadcast(P)).then_inc(s_gvec, 16)
            sp.dma_start(bias32[:, 24:32], b_forget[0, :].partition_broadcast(P)).then_inc(s_gvec, 16)
            sp.dma_start(ptab[:, :], page_table.rearrange("b (o j) -> o (b j)", o=1)).then_inc(s_pt, 16)
            for n in (2, 3):
                sp.wait_ge(ada_ready, n - 1)
                sp.dma_start(wbuf[n % 2][:, :, :], wada_v[:, :, 512 * n:512 * (n + 1)]).then_inc(w_ld[n % 2], 16)

            def load_z(b):
                if b == 0:
                    sp.wait_ge(ada_ready, 3)
                    sp.dma_start(wbuf[0][:, :, 0:N_MISC], win_v[:, :, C_WIN:C_WIN + N_MISC]).then_inc(w_ld[0], 16)
                    sp.dma_start(wbuf[0][:, :, N_MISC:N_MISC + 8], win_v[:, :, C_F:C_F + 8]).then_inc(w_ld[0], 16)
                    return
                if b == 1:
                    sp.wait_ge(ada_ready, 4)
                else:
                    sp.wait_ge(z_ready, T9 * (b - 1))
                c = ZC[ZB[b]]
                sp.dma_start(wbuf[b % 2][:, :, :], win_v[:, :, c:c + 512]).then_inc(w_ld[b % 2], 16)

            def load_ada(i):
                if i:
                    sp.wait_ge(ada_ready, ada1 + i)
                n = ada1 + i
                sp.dma_start(wbuf[2][:, :, :], wada_v[:, :, 512 * n:512 * (n + 1)]).then_inc(w_ld[2], 16)

            load_z(0)
            load_ada(0)
            for J in range(NJ + LAG):
                if J < NJ and jobs[J][1] == 0 and jobs[J][0] + 1 < len(ZB):
                    load_z(jobs[J][0] + 1)
                if J - 2 in ada_after and ada_after.index(J - 2) + 1 < len(ada_after):
                    load_ada(ada_after.index(J - 2) + 1)
                K = J - LAG
                if K < 0:
                    continue
                if z_stores(K):
                    if K in pool_jobs:
                        sp.wait_ge(pool_done, pool_count[K])
                    else:
                        sp.wait_ge(z_ev, K + 1)
                    for dst, src in z_stores(K):
                        sp.dma_start(dst, src).then_inc(z_st[K % 5], 16)
                if K in q_index:
                    i, t = q_index[K], jobs[K][1]
                    sp.wait_ge(tz_a, tz_order[tz_index[K]])
                    sp.dma_start(qt_d[i // NT, :, :, t * P:(t + 1) * P].rearrange("h d t -> d h t"),
                                 qst[i % 2][:, :, :]).then_inc(q_st[i % 2], 16)
                if K == csum_after + 3:
                    sp.wait_ge(g_done, 1)
                    sp.dma_start(flf_p.rearrange("a b (t p) h -> p (a b t) h", p=P), logf[:, 0:NT, :]).then_inc(misc_st, 16)
                    sp.dma_start(flf_s.rearrange("a b t h -> (a b t) h"), logf[0:NS, NT, :]).then_inc(misc_st, 16)
                    sp.dma_start(gs_d, gates[0:NS, NT, :]).then_inc(misc_st, 16)
                    sp.wait_ge(ct_copied, 1)
                    for t in range(NT):
                        sp.dma_start(kTf[HD:HD + 1, :, t * P:(t + 1) * P], nCT[t * NH:(t + 1) * NH, :]).then_inc(ct_moved, 16)
                if K == 20:
                    sp.dma_start(wins_v[:, 0:PAST - TQ, :], stw_rows[:, TQ:PAST, :]).then_inc(copy_st, 16)
            for i in range(5):
                last = max(J for J in range(NJ) if J % 5 == i)
                sp.wait_ge(z_st[i], stored(last))
            for i in range(2):
                sp.wait_ge(q_st[i], 16 * NT)
            sp.wait_ge(ct_moved, 16 * NT)
            sp.wait_ge(misc_st, 48)
            sp.wait_ge(copy_st, 16)

        @block.gpsimd
        def _(pool):
            ch = Chain(pool, pool_a)
            nc.gpsimd.memset(graw[:, :, :], 0.0).then_inc(misc_set, 1)
            pool.wait_ge(ln_t, 2 * T9)
            pool.wait_ge(sc_ready, 1)
            ch.link(nc.gpsimd.memset(Vf[:, :, :, HD:HD + 1], 1.0))
            ch.link(nc.gpsimd.memset(Vs[:, :, :, HD:HD + 1], 1.0))
            nc.gpsimd.memset(Vw[:, :, :, HD:HD + 1], 1.0).then_inc(kv_set, 1)
            pool.wait_ge(s_gvec, 96)
            ch.link(nc.gpsimd.tensor_scalar(gvec[:, 0, :], gvec[:, 0, :], SCALE, None, ALU.mult))
            ch.link(nc.gpsimd.tensor_scalar(gvec[:, 2, :], gvec[:, 2, :], SCALE, None, ALU.mult))
            for J in pool_jobs:
                b, t = jobs[J]
                name, z, r = ZB[b], zsb[J % 5], rows(t)
                if name == "vf":
                    pool.wait_ge(z_ev, J + 1)
                    nc.gpsimd.tensor_copy(Vf[:, t, :, 0:HD], z[:, :].rearrange("p (h d) -> p h d", d=HD)).then_inc(pool_done, 1)
                    continue
                pool.wait_ge(z_scaled, n_index[J] + 1)
                x = k_heads(name, z, r, HD)
                if name == "cs":
                    g = gvec[0:r, 3:5, :].unsqueeze(2).to_broadcast([r, 2, G, HD])
                else:
                    i = {"misc": 5, "kf": 1, "qf": 0, "qn": 2}[name]
                    g = gvec[0:r, i:i + 1, :].to_broadcast([r, G if name == "misc" else NH, HD])
                ins = nc.gpsimd.tensor_tensor(x, x, g, ALU.mult)
                if name in ("kf", "qf"):
                    ins.then_inc(pool_done, 1)
                    continue
                ch.link(ins)
                x = k_heads(name, z, r, 16)
                n = NH if name == "qn" else G
                if name == "cs":
                    a = rope[0][0:r, 0:4, :].rearrange("p (a h) d -> p a h d", a=2)
                    c = rope[1][0:r, 0:4, :].rearrange("p (a h) d -> p a h d", a=2)
                    lo, hi = c[:, :, :, 0:8], c[:, :, :, 8:16]
                    x_lo, x_hi = x[:, :, :, 0:8], x[:, :, :, 8:16]
                else:
                    a, c = rope[0][0:r, 0:n, :], rope[1][0:r, 0:n, :]
                    lo, hi = c[:, :, 0:8], c[:, :, 8:16]
                    x_lo, x_hi = x[:, :, 0:8], x[:, :, 8:16]

                def table(col, w):
                    v = cst[0:r, col + 16 * t:col + 16 * t + w].unsqueeze(1)
                    return v.unsqueeze(1).to_broadcast([r, 2, G, w]) if name == "cs" else v.to_broadcast([r, n, w])

                ch.link(nc.gpsimd.tensor_tensor(a, x, table(K_COS, 16), ALU.mult))
                ch.link(nc.gpsimd.tensor_tensor(lo, x_hi, table(K_SIN, 8), ALU.mult))
                ch.link(nc.gpsimd.tensor_tensor(hi, x_lo, table(K_SIN + 8, 8), ALU.mult))
                last = nc.gpsimd.tensor_tensor(x, a, c, ALU.add)
                if t < NT and name == "misc":
                    last = nc.gpsimd.tensor_copy(Vw[:, t, :, 0:HD], z[:, 128:256].rearrange("p (h d) -> p h d", d=HD))
                if t < NT and name == "cs":
                    last = nc.gpsimd.tensor_copy(Vs[:, t, :, 0:HD], z[:, 384:512].rearrange("p (h d) -> p h d", d=HD))
                last.then_inc(pool_done, 1)

        @block.scalar
        def _(act):
            act.wait_ge(c_neg, 1)
            nc.scalar.activation(c9e[:, :], c9e[:, :], ACT.Exp).then_inc(c_exp, 1)
            for g, (lo, hi) in enumerate(((0, 4), (4, 8), (8, 9))):
                act.wait_ge(s_x[g], 16)
                for t in range(lo, hi):
                    if t:
                        act.wait_ge(ln_sq, t)
                    nc.scalar.activation(junk[0:rows(t), :], xb[0:rows(t), t, :], ACT.Square,
                                         accum_out=ssum[0:rows(t), t:t + 1]).then_inc(ln_sq, 1)
                act.wait_ge(ln_var, g + 1)
                r = rows(lo)
                nc.scalar.activation(rstd[0:r, lo:hi], ssum[0:r, lo:hi], ACT.Sqrt).then_inc(ln_root, 1)
            for t in range(T9):
                act.wait_ge(ln_t, 2 * t + 1)
                r = rows(t)
                nc.scalar.activation(hT[:, 0:4, t * P:t * P + r],
                                     bk[2 * (t % 3)].rearrange("p (k n) -> p k n", k=4)[:, :, 0:r], ACT.Copy).then_inc(ln_ea, 1)
            act.wait_ge(mod_ready, 1)
            act.wait_ge(ln_ea, T9)
            for k in range(4):
                nc.scalar.activation(hT[:, k, 0:S], hT[:, k, 0:S], ACT.Identity, bias=modT[:, k, 0:1],
                                     scale=gain1[:, k, 0:1]).then_inc(mod_a, 1)

            def copy_t(K):
                b, t = jobs[K]
                i = tz_index[K]
                act.wait_ge(tz_ready, i + 1)
                src = bk[3 + i % 3].rearrange("p (j n) -> p j n", n=P)
                cols = slice(t * P, (t + 1) * P)
                if ZB[b] == "misc":
                    nc.scalar.activation(kTw[0:HD, 0, cols], src[0:HD, 0, :], ACT.Copy)
                    nc.scalar.activation(kTw[0:HD, 1, cols], src[HD:P, 0, :], ACT.Copy).then_inc(tz_a, 1)
                    return
                if ZB[b] == "kf":
                    dst = kTf[0:HD, :, cols].rearrange("p (j e) n -> p j e n", e=2)
                else:
                    q = q_index[K]
                    if q >= 2:
                        act.wait_ge(q_st[q % 2], 16 * (q // 2))
                    dst = qst[q % 2][:, :, :].rearrange("p (j e) n -> p j e n", e=2)
                nc.scalar.activation(dst[:, :, 0, :], src[0:HD, :, :], ACT.Copy)
                nc.scalar.activation(dst[:, :, 1, :], src[HD:P, :, :], ACT.Copy).then_inc(tz_a, 1)

            for J in range(NJ + LAG):
                if J < NJ:
                    b, t = jobs[J]
                    name, r, w = ZB[b], rows(t), ZW[ZB[b]]
                    act.wait_ge(z_ready, J + 1)
                    if J >= 5:
                        act.wait_ge(pool_done, pool_count[J - 5])
                        if J - 5 in tz_index:
                            act.wait_ge(tz_ready, tz_index[J - 5] + 1)
                        if stored(J - 5):
                            act.wait_ge(z_st[J % 5], stored(J - 5))
                    ins = nc.scalar.activation(zsb[J % 5][0:r, 0:w], bk[J % 3][0:r, 0:w], ACT.Copy)
                    if name != "vf":
                        before = sum(j <= J - 2 for j in normed)
                        if before:
                            act.wait_ge(z_var, before)
                        n = 128 if name == "misc" else 512
                        ins = nc.scalar.activation(sq[J % 2][0:r, 0:n], bk[J % 3][0:r, 0:n], ACT.Square)
                    ins.then_inc(z_ev, 1)
                    if name != "vf":
                        act.wait_ge(z_var, n_index[J] + 1)
                        h = hv[J % 3]
                        nc.scalar.activation(h[0:r, 1, :], h[0:r, 0, :], ACT.Sqrt).then_inc(z_root, 1)
                    if J == NT:
                        act.wait_ge(g_arg, 1)
                        nc.scalar.activation(gexp[:, :, :], gexp[:, :, :], ACT.Exp).then_inc(g_exp, 1)
                        act.wait_ge(g_one, 1)
                        nc.scalar.activation(lnv[:, :, :], gexp[:, :, 24:32], ACT.Ln).then_inc(g_ln, 1)
                K = J - LAG
                if K in tz_index and tz_eng[tz_index[K]] == "a":
                    copy_t(K)

        @block.vector
        def _(dve):
            ch = Chain(dve, dve_a)
            nc.vector.nop().then_inc(ada_ev, CREDIT)
            dve.wait_ge(s_c, 32)
            nc.vector.tensor_scalar(c9e[:, :], c9[:, :], -1.0, EXP_MAX, ALU.mult, ALU.min).then_inc(c_neg, 1)
            dve.wait_ge(c_exp, 1)
            ch.link(nc.vector.tensor_scalar(c9e[:, :], c9e[:, :], 1.0, None, ALU.add))
            ch.link(nc.vector.reciprocal(c9e[:, :], c9e[:, :]))
            nc.vector.tensor_tensor(c9e[:, :], c9[:, :], c9e[:, :], ALU.mult).then_inc(c_silu, 1)
            for g, (lo, hi) in enumerate(((0, 4), (4, 8), (8, 9))):
                r = rows(lo)
                dve.wait_ge(ln_sq, hi)
                nc.vector.tensor_scalar(ssum[0:r, lo:hi], ssum[0:r, lo:hi], 1.0 / D, EPS, ALU.mult, ALU.add).then_inc(ln_var, 1)
                dve.wait_ge(ln_root, g + 1)
                ch.link(nc.vector.reciprocal(rstd[0:r, lo:hi], rstd[0:r, lo:hi]))
                for t in range(lo, hi):
                    nc.vector.tensor_scalar(xb[0:r, t, :], xb[0:r, t, :], rstd[0:r, t:t + 1], None, ALU.mult).then_inc(xn_done, 1)
                if g == 0:
                    dve.wait_ge(t0_ready, 1)
                    nc.vector.tensor_copy(scT[:, :, :], bk[7][:, 0:72].rearrange("p (k n) -> p k n", k=KC))
                    nc.vector.tensor_copy(vecT[:, :], bk[7][:, 128:192])
                    nc.vector.tensor_copy(peT[:, :, :], bk[7][:, 256:384].rearrange("p (k n) -> p k n", k=2)).then_inc(sc_ready, 1)
            for t in range(T9):
                dve.wait_ge(ln_t, 2 * t + 2)
                r = rows(t)
                nc.vector.tensor_copy(hT[:, 4:8, t * P:t * P + r],
                                      bk[2 * (t % 3) + 1].rearrange("p (k n) -> p k n", k=4)[:, :, 0:r]).then_inc(ln_ed, 1)
            dve.wait_ge(sc_ready, 1)

            def store_ada(n, src):
                out, bias = modT[:, bass.ds(4 * n, 4), :], vecT[:, bass.ds(4 * n, 4)]
                nc.vector.tensor_tensor(out, src[:, 0:36].rearrange("p (k n) -> p k n", k=4),
                                        bias.unsqueeze(2).to_broadcast([P, 4, B + 1]), ALU.add).then_inc(ada_ev, 1)

            with dve.Fori(0, ada1 // 2) as it:
                for s in range(2):
                    dve.wait_ge(ada_ready, 2 * it + s + 1)
                    store_ada(2 * it + s, bk[6 + s])
            dve.wait_ge(ada_ev, CREDIT + ada1)
            nc.vector.scalar_tensor_tensor(gain1[:, :, :], modT[:, 8:16, :], 1.0,
                                           vecT[:, 48:56].unsqueeze(2).to_broadcast([P, KC, B + 1]),
                                           ALU.add, ALU.mult).then_inc(mod_ready, 1)
            dve.wait_ge(mod_ready, 1)
            dve.wait_ge(ln_ed, T9)
            for k in range(4, 8):
                nc.vector.tensor_scalar(hT[:, k, 0:S], hT[:, k, 0:S], gain1[:, k, 0:1], modT[:, k, 0:1],
                                        ALU.mult, ALU.add).then_inc(mod_d, 1)
            dve.wait_ge(ln_ea, T9)
            hs = hT[:, :, S:TOK].rearrange("p k (b t) -> p k b t", b=B)
            ch.link(nc.vector.tensor_tensor(hs, hs, gain1[:, :, 1:B + 1].unsqueeze(3).to_broadcast([P, KC, B, TQ]), ALU.mult))
            nc.vector.tensor_tensor(hs, hs, modT[:, 0:KC, 1:B + 1].unsqueeze(3).to_broadcast([P, KC, B, TQ]), ALU.add).then_inc(mod_d, 1)
            dve.wait_ge(misc_set, 1)
            dve.wait_ge(s_gvec, 96)

            def copy_t(K):
                t, i = jobs[K][1], tz_index[K]
                dve.wait_ge(tz_ready, i + 1)
                src = bk[3 + i % 3]
                for kv in range(2):
                    nc.vector.tensor_tensor(Xc[:, 2 * t:2 * t + 2, kv, :],
                                            src[:, P * kv:P * (kv + 1)].rearrange("p (n d) -> p n d", n=2),
                                            peT[:, kv:kv + 1, :].to_broadcast([P, 2, BLOCK]), ALU.add)
                nc.vector.tensor_copy(kTs[0:HD, 0, t * P:(t + 1) * P], src[0:HD, 256:384])
                nc.vector.tensor_copy(kTs[0:HD, 1, t * P:(t + 1) * P], src[HD:P, 256:384]).then_inc(tz_d, 1)

            for J in range(NJ + LAG):
                if J < NJ:
                    b, t = jobs[J]
                    name, z, r, h = ZB[b], zsb[J % 5], rows(t), hv[J % 3]
                    if name != "vf":
                        n = G if name == "misc" else NH
                        dve.wait_ge(z_ev, J + 1)
                        ch.link(nc.vector.tensor_reduce(h[0:r, 0, 0:n], sq[J % 2][0:r, 0:n * HD].rearrange("p (h d) -> p h d", d=HD),
                                                        AX.X, ALU.add))
                        if name == "misc":
                            ch.link(nc.vector.memset(h[0:r, 0, n:NH], 1.0))
                        nc.vector.tensor_scalar(h[0:r, 0, :], h[0:r, 0, :], 1.0 / HD, EPS, ALU.mult, ALU.add).then_inc(z_var, 1)
                        if name == "misc":
                            nc.vector.tensor_tensor(graw[0:r, t, :], z[0:r, 256:288], bias32[0:r, :], ALU.add)
                        dve.wait_ge(z_root, n_index[J] + 1)
                        ch.link(nc.vector.reciprocal(h[0:r, 2, :], h[0:r, 1, :]))
                        x = k_heads(name, z, r, HD)
                        if name == "cs":
                            s = h[0:r, 2, :].rearrange("p (a k h) -> p a k h", a=2, k=2)[:, :, 0, :].unsqueeze(3).to_broadcast([r, 2, G, HD])
                        else:
                            s = h[0:r, 2, 0:n].unsqueeze(2).to_broadcast([r, n, HD])
                        nc.vector.tensor_tensor(x, x, s, ALU.mult).then_inc(z_scaled, 1)
                    if J == NT:
                        dve.wait_ge(z_scaled, n_index[J] + 1)
                        ch.link(nc.vector.tensor_scalar(gexp[:, :, 0:24], graw[:, :, 0:24], -1.0, EXP_MAX, ALU.mult, ALU.min))
                        ch.link(nc.vector.tensor_scalar(gexp[:, :, 24:32], graw[:, :, 24:32], -1.0, None, ALU.mult))
                        nc.vector.tensor_tensor(gexp[:, :, 24:32], gexp[:, :, 24:32], graw[:, :, 24:32], ALU.min).then_inc(g_arg, 1)
                        dve.wait_ge(g_exp, 1)
                        nc.vector.tensor_scalar(gexp[:, :, :], gexp[:, :, :], 1.0, None, ALU.add).then_inc(g_one, 1)
                        dve.wait_ge(g_one, 1)
                        ch.link(nc.vector.reciprocal(gates[:, :, :], gexp[:, :, 0:24]))
                        ch.link(nc.vector.tensor_scalar(gates[:, 0, 0:NH], gates[:, 0, 0:NH], cst[:, K_ANY:K_ANY + 1], None, ALU.mult))
                        dve.wait_ge(g_ln, 1)
                        nc.vector.scalar_tensor_tensor(logf[:, :, :], graw[:, :, 24:32], 0.0, lnv[:, :, :],
                                                       ALU.min, ALU.subtract).then_inc(g_done, 1)
                    if J in ada_after:
                        i = ada_after.index(J)
                        dve.wait_ge(ada_ready, ada1 + i + 1)
                        store_ada(ada1 + i, bk[6])
                    if J == csum_after:
                        dve.wait_ge(c_ready, 1)
                        tot = bk[7][:, 64:128].rearrange("p (t h) -> p t h", h=NH)
                        ch.link(nc.vector.memset(cpre[:, 0, :], 0.0))
                        for t2 in range(1, NT):
                            ch.link(nc.vector.tensor_tensor(cpre[:, t2, :], cpre[:, t2 - 1, :], tot[:, t2 - 1, :], ALU.add))
                        nc.vector.scalar_tensor_tensor(csum[:, :, :], bk[7][:, 0:64].rearrange("p (t h) -> p t h", h=NH), -1.0,
                                                       cpre[:, :, :], ALU.mult, ALU.subtract).then_inc(c_neg2, 1)
                    if J == csum_after + 2:
                        dve.wait_ge(ct_ready, 1)
                        nc.vector.tensor_copy(nCT[:, :], bk[7][0:HD, 128:256]).then_inc(ct_copied, 1)
                K = J - LAG
                if K in tz_index and tz_eng[tz_index[K]] == "d":
                    copy_t(K)

        @block.tensor
        def _(pe):
            pe.wait_ge(s_const, 16)
            pe.wait_ge(s_vec, 48)
            pe.wait_ge(c_silu, 1)
            pe.wait_ge(s_pe, 32)
            for k in range(KC):
                nc.tensor.transpose(bk[7][:, 9 * k:9 * k + 9], c9e[:, k * P:(k + 1) * P], ident[0:B + 1, 0:B + 1])
            nc.tensor.transpose(bk[7][:, 128:192], vecn[:, :], ident[0:HD, 0:HD])
            for kv in range(2):
                last = nc.tensor.transpose(bk[7][:, 256 + 64 * kv:320 + 64 * kv],
                                           pen[:, kv, :, :].rearrange("p a d -> p (a d)"), ident[0:HD, 0:HD])
            last.then_inc(t0_ready, 1)
            for t in range(T9):
                r = rows(t)
                pe.wait_ge(xn_done, t + 1)
                if t >= 3:
                    pe.wait_ge(ln_ea, t - 2)
                    pe.wait_ge(ln_ed, t - 2)
                for k in range(KC):
                    dst = bk[2 * (t % 3) + k // 4][:, P * (k % 4):P * (k % 4) + r]
                    ins = nc.tensor.transpose(dst, xb[0:r, t, k * P:(k + 1) * P], ident[0:r, 0:r])
                    if k % 4 == 3:
                        ins.then_inc(ln_t, 1)
            pe.wait_ge(sc_ready, 1)

            def ada(buf, dst):
                for j in range(4):
                    for k in range(KC):
                        last = nc.tensor.matmul(dst[:, 9 * j:9 * j + 9], buf[:, k, j * P:(j + 1) * P], scT[:, k, :],
                                                start=(k == 0), stop=(k == KC - 1))
                last.then_inc(ada_ready, 1)

            with pe.Fori(0, ada1 // 2) as it:
                pe.wait_ge(ada_ev, 2 * it + CREDIT)
                for s in range(2):
                    pe.wait_ge(w_ld[s], 16 * it + 16)
                    ada(wbuf[s], bk[6 + s])
            pe.wait_ge(mod_a, 4)
            pe.wait_ge(mod_d, 5)
            for J in range(NJ + LAG):
                if J < NJ:
                    b, t = jobs[J]
                    r, w = rows(t), ZW[ZB[b]]
                    if t == 0:
                        pe.wait_ge(w_ld[b % 2], loaded(b % 2, 2 + b // 2))
                    if J >= 3:
                        pe.wait_ge(z_ev, J - 2)
                    for k in range(KC):
                        last = nc.tensor.matmul(bk[J % 3][0:r, 0:w], hT[:, k, t * P:t * P + r], wbuf[b % 2][:, k, 0:w],
                                                start=(k == 0), stop=(k == KC - 1))
                    last.then_inc(z_ready, 1)
                K = J - LAG
                if K in tz_index:
                    i = tz_index[K]
                    pe.wait_ge(pool_done, pool_count[K])
                    if i >= 3:
                        pe.wait_ge(tz_a if tz_eng[i - 3] == "a" else tz_d, tz_order[i - 3])
                    n = {"misc": 1, "cs": 3}.get(ZB[jobs[K][0]], 4)
                    for j in range(n):
                        last = nc.tensor.transpose(bk[3 + i % 3][:, j * P:(j + 1) * P], zsb[K % 5][:, j * P:(j + 1) * P], ident)
                    last.then_inc(tz_ready, 1)
                if J == csum_after:
                    pe.wait_ge(g_done, 1)
                    lf = logf[:, 0:NT, :].rearrange("p t h -> p (t h)")
                    nc.tensor.matmul(bk[7][:, 0:64], cst[:, K_U:K_U + P], lf, start=True, stop=True)
                    nc.tensor.matmul(bk[7][:, 64:128], cst[:, K_ONE:K_ONE + P], lf, start=True, stop=True).then_inc(c_ready, 1)
                if J == csum_after + 2:
                    pe.wait_ge(c_neg2, 1)
                    nc.tensor.transpose(bk[7][0:HD, 128:256], csum[:, :, :].rearrange("p t h -> p (t h)"), ident).then_inc(ct_ready, 1)
                if J in ada_after:
                    i = ada_after.index(J)
                    pe.wait_ge(w_ld[2], 16 * (i + 1))
                    pe.wait_ge(ada_ev, CREDIT + ada1 + i)
                    ada(wbuf[2], bk[6])

    cp_ld = [sem(f"cpage_loaded{i}") for i in range(2)]
    wc_ld = [sem(f"wcmp_loaded{i}") for i in range(2)]
    wc_set, cb_ready, xc_ev, wc_used, kvc_done, vt_ready, vc_done, vcp_set = (sem(n) for n in (
        "wcmp_cleared", "cpage_transposed", "cinput_stored", "wcmp_used", "kvc_copied",
        "vc_transposed", "vc_copied", "vcp_ones_set"))
    wcmp_v = w_cmp.rearrange("a k (p d) e -> (a k) d p e", d=HD)
    CW = 8
    NCW = BLOCK // CW

    with nc.Block() as block:

        @block.sync
        def _(sp):
            sp.wait_ge(s_pt, 16)
            sp.wait_ge(wc_set, 1)

            def load_w(c):
                for kv in range(2):
                    for i in range(2):
                        sp.dma_start(wbd[c % 2][HD * i:HD * (i + 1), kv, :, HD * i:HD * (i + 1)],
                                     wcmp_v[kv, :, CW * c:CW * (c + 1), :]).then_inc(wc_ld[c % 2], 16)

            def load_pages(b, s):
                for j in range(PAGES):
                    page = sp.value_load(ptab[0:1, bass.ds(b * PAGES + j, 1)], min_val=0, max_val=n_pool - 1)
                    sp.dma_start(cpage[s][:, j, :], cnsa_v[page, :, 0:256]).then_inc(cp_ld[s], 16)

            for s in range(2):
                load_pages(s, s)
            for c in range(2):
                load_w(c)
            with sp.Fori(0, B // 2 - 1) as it:
                for s in range(2):
                    sp.wait_ge(cb_ready, 2 * it + s + 1)
                    load_pages(2 * it + s + 2, s)
            for c in range(2, NCW):
                sp.wait_ge(wc_used, c - 1)
                load_w(c)

        @block.gpsimd
        def _(pool):
            nc.gpsimd.memset(kcP[HD:HD + 1, :, :], 0.0).then_inc(vcp_set, 1)
            pool.wait_ge(vcp_set, 1)
            nc.gpsimd.memset(vcP[:, :, :], 0.0).then_inc(vcp_set, 1)
            nc.gpsimd.memset(wbd[0][:, :, :, :], 0.0)
            nc.gpsimd.memset(wbd[1][:, :, :, :], 0.0).then_inc(wc_set, 1)

        @block.vector
        def _(dve):
            nc.vector.nop().then_inc(xc_ev, CREDIT)
            with dve.Fori(0, B // 2) as it:
                for s in range(2):
                    dve.wait_ge(cb_ready, 2 * it + s + 1)
                    for kv in range(2):
                        ins = nc.vector.tensor_tensor(
                            Xc[:, bass.ds(it * (2 * NBS) + (NBP + NBS * s), NBS), kv, :],
                            bk[2 * s + kv].rearrange("p (n d) -> p n d", d=BLOCK),
                            peT[:, kv:kv + 1, :].to_broadcast([P, NBS, BLOCK]), ALU.add)
                    ins.then_inc(xc_ev, 1)
            dve.wait_ge(vcp_set, 2)
            dve.wait_ge(vt_ready, 1)
            nc.vector.memset(vcP[0:NBP, :, HD:HD + 1], 1.0)
            nc.vector.tensor_copy(vcP[0:NBP, :, 0:HD], bk[6][0:NBP, 0:P].rearrange("p (g d) -> p g d", g=G))
            nc.vector.tensor_copy(vcS[:, 0:4, :], bk[7][0:NBS, :].rearrange("p (b d) -> p b d", b=4))
            nc.vector.tensor_copy(vcS[:, 4:8, :], bk[0][0:NBS, :].rearrange("p (b d) -> p b d", b=4)).then_inc(vc_done, 1)

        @block.scalar
        def _(act):
            act.wait_ge(wc_used, NCW)
            nc.scalar.activation(kvcT[:, 1, :], bk[5][:, 0:NBP + B * NBS], ACT.Copy).then_inc(kvc_done, 1)
            nc.scalar.activation(kcS[:, :], bk[4][:, NBP:NBP + B * NBS], ACT.Copy)
            nc.scalar.activation(kcP[0:HD, 0, :], bk[4][0:HD, 0:NBP], ACT.Copy)
            nc.scalar.activation(kcP[0:HD, 1, :], bk[4][HD:P, 0:NBP], ACT.Copy).then_inc(kvc_done, 1)

        @block.tensor
        def _(pe):
            with pe.Fori(0, B // 2) as it:
                pe.wait_ge(xc_ev, 2 * it + CREDIT)
                for s in range(2):
                    pe.wait_ge(cp_ld[s], it * (16 * PAGES) + 16 * PAGES)
                    for kv in range(2):
                        for j in range(PAGES):
                            last = nc.tensor.transpose(bk[2 * s + kv][:, j * P:(j + 1) * P], cpage[s][:, j, P * kv:P * (kv + 1)], ident)
                    last.then_inc(cb_ready, 1)
            pe.wait_ge(xc_ev, B + CREDIT)
            for c in range(NCW):
                pe.wait_ge(wc_ld[c % 2], 64 * (c // 2 + 1))
                for p in range(CW):
                    for kv in range(2):
                        last = nc.tensor.matmul(bk[4 + kv][:, 0:NBP + B * NBS], wbd[c % 2][:, kv, p, :], Xc[:, :, kv, CW * c + p],
                                                start=(c == 0 and p == 0), stop=(c == NCW - 1 and p == CW - 1))
                last.then_inc(wc_used, 1)
            pe.wait_ge(kvc_done, 1)
            nc.tensor.transpose(bk[6][0:NBP, 0:P], kvcT[:, 1, 0:NBP], ident)
            for b in range(B):
                last = nc.tensor.transpose((bk[7] if b < 4 else bk[0])[0:NBS, P * (b % 4):P * (b % 4 + 1)],
                                           kvcT[:, 1, NBP + NBS * b:NBP + NBS * (b + 1)], ident)
            last.then_inc(vt_ready, 1)

    q_one = sem("q_ones_set")

    def prompt_attention(tag, source, kinds):
        q_ld = [sem(f"{tag}_q_loaded{i}") for i in range(2)]
        scores_ready, max_ready, prob_ready, pt_ready, pt_act, pt_dve, o_ready, o_norm = (sem(f"{tag}_{n}") for n in (
            "scores_ready", "max_ready", "prob_ready", "pt_ready", "pt_copied_act", "pt_copied_dve", "o_ready", "o_stored"))
        dve_s = sem(f"{tag}_dve_step")
        fox = kinds == ("fox",)
        units = [(s, u) for s in range(2) for u in attention_units(kinds)]
        n = len(units)
        nk = [u[3] for _, u in units]
        halves = [(k + 3) // 4 for k in nk]
        h0 = [sum(halves[:i]) for i in range(n + 1)]
        d0 = [sum(h == 2 for h in halves[:i]) for i in range(n + 1)]
        owner = [(i, j) for i in range(n) for j in range(halves[i])]
        steps = sum((2 if u[0] == "win" and u[3] == 5 else 1) + (1 if fox else 2) for _, u in units)
        TURNS = NH // 2
        split_step, q_split = sem(f"{tag}_pool_step"), sem(f"{tag}_parts_ready")

        with nc.Block() as block:

            @block.sync
            def _(sp):
                for s in range(2):
                    sp.dma_start(qT[s][0:HD, :], qt_d[source, s, :, :]).then_inc(q_ld[s], 16)
                with sp.Fori(0, TURNS - 1) as it:
                    for s in range(2):
                        sp.wait_ge(scores_ready, it * n + (s + 1) * (n // 2))
                        sp.dma_start(qT[s][0:HD, :], qt_d[source, 2 * it + (s + 2), :, :]).then_inc(q_ld[s], 16)

            @block.gpsimd
            def _(pool):
                ch = Chain(pool, split_step)
                if fox:
                    nc.gpsimd.memset(probT[0][:, 0, :], 0.0)
                    nc.gpsimd.memset(probT[1][:, 0, :], 0.0).then_inc(q_one, 1)
                    pool.wait_ge(q_one, 1)
                    for i in range(2):
                        nc.gpsimd.memset(qT[i][HD:HD + 1, :], 1.0)
                        nc.gpsimd.memset(q3[i][HD:P, :].bitcast(F32), 1.0)
                        ch.link(nc.gpsimd.memset(k3[i][HD:P, :].bitcast(F32), 0.0))

                def split(hi, lo, x):
                    ch.link(nc.gpsimd.tensor_copy(hi, x))
                    return nc.gpsimd.tensor_tensor(lo, x, hi.bitcast(F32), ALU.subtract)

                for h in range(NH):
                    s = h % 2
                    if h >= 2:
                        pool.wait_ge(scores_ready, (h - 1) * (n // 2))
                    if fox:
                        k = kTf[:, h, :]
                        ch.link(nc.gpsimd.tensor_copy(k3[s][HD:HD + 1, :], k[HD:HD + 1, :]))
                        nc.gpsimd.tensor_tensor(k3[s][96:97, :], k[HD:HD + 1, :], k3[s][HD:HD + 1, :].bitcast(F32), ALU.subtract)
                        split(k2[s][0:HD, :], k2[s][HD:P, :], k[0:HD, :])
                        nc.gpsimd.tensor_copy(k3[s][0:HD, :], k2[s][0:HD, :].bitcast(F32))
                    pool.wait_ge(q_ld[s], 16 * (h // 2 + 1))
                    last = split(q2[s][0:HD, :], q3[s][0:HD, :], qT[s][0:HD, :])
                    if not fox:
                        ch.link(last)
                        nc.gpsimd.tensor_copy(q3[s][HD:P, :], q3[s][0:HD, :].bitcast(F32))
                    nc.gpsimd.tensor_copy(q2[s][HD:P, :], q2[s][0:HD, :].bitcast(F32)).then_inc(q_split, 1)

                if fox:
                    for g in range(G):
                        split(ks2[0:HD, g, :], ks2[HD:P, g, :], kTs[:, g, :])
                        split(kw2[0:HD, g, :], kw2[HD:P, g, :], kTw[:, g, :])

            @block.tensor
            def _(pe):
                with pe.Fori(0, TURNS) as it:

                    def scores(i):
                        s, (kind, t, lo, k) = units[i]
                        if i % (n // 2) == 0:
                            pe.wait_ge(q_split, it * 2 + (s + 1))
                        if i >= 2:
                            pe.wait_ge(prob_ready, it * n + (i - 1))
                        dst = banks(2 * (i % 2), 2)
                        q = slice(t * P, (t + 1) * P)
                        if kind == "cmp":
                            last = nc.tensor.matmul(dst[:, 0:NBP], qT[s][0:HD + 1, q], kcP[:, it // 2, :], start=True, stop=True)
                        for c in range(0, 0 if kind == "cmp" else k * P, 512):
                            w = min(512, k * P - c)
                            a, z = lo * P + c, lo * P + c + w
                            rhs = (k2[s][:, a:z] if kind == "fox" else ks2[:, it // 2, a:z] if kind == "slc" else kw2[:, it // 2, a:z])
                            rest = k3[s][:, a:z] if kind == "fox" else rhs
                            nc.tensor.matmul(dst[:, c:c + w], q2[s][:, q], rhs, start=True, stop=False)
                            last = nc.tensor.matmul(dst[:, c:c + w], q3[s][:, q], rest, start=False, stop=True)
                        last.then_inc(scores_ready, 1)

                    def transposes(i):
                        kind, _, _, k = units[i][1]
                        pe.wait_ge(prob_ready, it * n + (i + 1))
                        for hh in range(halves[i]):
                            g = h0[i] + hh
                            if g >= 2:
                                j, jj = owner[g - 2]
                                if jj == 0:
                                    pe.wait_ge(pt_act, it * n + (j + 1))
                                else:
                                    pe.wait_ge(pt_dve, it * d0[n] + d0[j + 1])
                            for j in range(4 * hh, min(k, 4 * hh + 4)):
                                w = NBP if kind == "cmp" else P
                                last = nc.tensor.transpose(bk[4 + g % 2][0:w, P * (j % 4):P * (j % 4 + 1)],
                                                           prob[i % 2][:, j * P:j * P + w], ident)
                            last.then_inc(pt_ready, 1)

                    def values(i):
                        s, (kind, t, lo, k) = units[i]
                        pe.wait_ge(pt_act, it * n + (i + 1))
                        if halves[i] == 2:
                            pe.wait_ge(pt_dve, it * d0[n] + d0[i + 1])
                        pe.wait_ge(o_norm, it * n + (max(i - 1, 0) + CREDIT))
                        dst = bk[6 + i % 2][:, 0:HD + 1]
                        for j in range(k):
                            v = (vcP[:, it // 2, :] if kind == "cmp" else Vf[:, lo + j, 2 * it + s, :] if kind == "fox" else
                                 Vs[:, lo + j, it // 2, :] if kind == "slc" else Vw[:, lo + j, it // 2, :])
                            last = nc.tensor.matmul(dst, probT[i % 2][:, j, :], v, start=(j == 0), stop=(j == k - 1))
                        last.then_inc(o_ready, 1)

                    scores(0)
                    for i in range(n):
                        if i + 1 < n:
                            scores(i + 1)
                        transposes(i)
                        if i:
                            values(i - 1)
                    values(n - 1)

            @block.scalar
            def _(act):
                if fox:
                    act.wait_ge(q_one, 1)
                with act.Fori(0, TURNS) as it:
                    for i, (s, (kind, t, lo, k)) in enumerate(units):
                        w = NBP if kind == "cmp" else k * P
                        act.wait_ge(max_ready, it * n + (i + 1))
                        nc.scalar.activation(prob[i % 2][:, 0:w], banks(2 * (i % 2), 2)[:, 0:w], ACT.Exp,
                                             bias=nmax[:, i % 2, 0:1]).then_inc(prob_ready, 1)
                        act.wait_ge(pt_ready, it * h0[n] + (h0[i] + 1))
                        m, r = min(k, 4), NBP if kind == "cmp" else P
                        nc.scalar.activation(probT[i % 2][0:r, 0:m, :],
                                             bk[4 + h0[i] % 2][0:r, 0:m * P].rearrange("p (j n) -> p j n", n=P),
                                             ACT.Copy).then_inc(pt_act, 1)

            @block.vector
            def _(dve):
                ch = Chain(dve, dve_s)
                nc.vector.nop().then_inc(o_norm, CREDIT)
                if fox:
                    dve.wait_ge(q_one, 1)
                with dve.Fori(0, TURNS) as it:
                    ch.loop(it, steps)

                    def maximum(i):
                        s, (kind, t, lo, k) = units[i]
                        src = banks(2 * (i % 2), 2)
                        dve.wait_ge(scores_ready, it * n + (i + 1))
                        if kind == "cmp":
                            w = NBP
                            ch.link(nc.vector.tensor_tensor(src[:, 0:w], src[:, 0:w], cst[:, K_CMP + NBP * t:K_CMP + NBP * (t + 1)], ALU.add))
                        else:
                            w = k * P
                            d = src[:, w - P:w]
                            ch.link(nc.vector.tensor_tensor(d, d, cst[:, K_CAUS:K_CAUS + P], ALU.add))
                            if kind == "win" and k == 5:
                                d = src[:, 0:P]
                                ch.link(nc.vector.tensor_tensor(d, d, cst[:, K_WIN:K_WIN + P], ALU.add))
                        nc.vector.tensor_reduce(nmax[:, i % 2, 0:1], src[:, 0:w], AX.X, ALU.max, negate=True).then_inc(max_ready, 1)

                    def second_half(i):
                        k = nk[i]
                        if halves[i] == 2:
                            dve.wait_ge(pt_ready, it * h0[n] + (h0[i] + 2))
                            nc.vector.tensor_copy(probT[i % 2][:, 4:k, :],
                                                  bk[4 + (h0[i] + 1) % 2][:, 0:(k - 4) * P].rearrange("p (j n) -> p j n", n=P)).then_inc(pt_dve, 1)

                    def output(i):
                        s, (kind, t, lo, k) = units[i]
                        dve.wait_ge(o_ready, it * n + (i + 1))
                        src, f = bk[6 + i % 2], gate_qk[:, i % 2, :]
                        ch.link(nc.vector.reciprocal(f[:, 0:1], src[:, HD:HD + 1]))
                        if kind == "fox":
                            nc.vector.tensor_scalar(mix[:, t, bass.ds(it * (2 * HD) + s * HD, HD)], src[:, 0:HD], f[:, 0:1], None, ALU.mult).then_inc(o_norm, 1)
                            return
                        br = {"cmp": 0, "slc": 1, "win": 2}[kind]
                        ch.link(nc.vector.tensor_tensor(f[:, 1:2], f[:, 0:1], gates[:, t, bass.ds(it * 2 + (br * NH + s), 1)], ALU.mult))
                        m = mix[:, t, bass.ds(it * (2 * HD) + (512 + s * HD), HD)]
                        if kind == "cmp":
                            nc.vector.tensor_scalar(m, src[:, 0:HD], f[:, 1:2], None, ALU.mult).then_inc(o_norm, 1)
                        else:
                            dve.wait_ge(o_norm, it * n + (i + CREDIT))
                            nc.vector.scalar_tensor_tensor(m, src[:, 0:HD], f[:, 1:2], m, ALU.mult, ALU.add).then_inc(o_norm, 1)

                    maximum(0)
                    for i in range(n):
                        if i + 1 < n:
                            maximum(i + 1)
                        second_half(i)
                        if i:
                            output(i - 1)
                    output(n - 1)
                    ch.end(TURNS)

    prompt_attention("fox", 0, ("fox",))
    prompt_attention("nsa", 1, ("cmp", "slc", "win"))

    in_ld = [sem(f"sample_loaded{i}") for i in range(2)]
    g_ld = sem("sample_gates_loaded")
    (e_set, lf_ready, p1_ready, q_bd, negc_done, kt_ready, kt_act, kt_dve, ks_ready, ks_done, sc_done, sc_act, m_ready,
     e_ready, p_ready, pt2_ready, pt2_act, pt2_dve, o2_ready, o2_done) = (sem(f"sample_{n}") for n in (
        "cleared", "logf_spread", "queries_transposed", "queries_placed", "bias_ready", "keys_transposed", "keys_act",
        "keys_dve", "new_keys_transposed", "new_keys_stored", "scores", "scores_act", "maxima", "exps", "probs",
        "probs_transposed", "probs_act", "probs_dve", "outputs", "outputs_copied"))
    os_st = [sem(f"sample_stored{i}") for i in range(2)]
    dve_e, pool_e = sem("dve_step_e"), sem("pool_step_e")
    nc.clear_and_free_semaphores(phase1_sems)
    N_LD = 20
    N_OS = 5
    TURNS2 = B // 2
    SAMPLE_STEPS = 2 * (3 + 2 + 3)

    with nc.Block() as block:

        @block.sync
        def _(sp):
            def load(b, s):
                q0 = b * TQ
                for j in range(PAGES):
                    page = sp.value_load(ptab[0:1, bass.ds(b * PAGES + j, 1)], min_val=0, max_val=n_pool - 1)
                    sp.dma_start(fpage[s][:, j, :], cfox_v[page, :, :]).then_inc(in_ld[s], 16)
                    sp.dma_start(npage[s][:, j, :], cnsa_v[page, :, 256:512]).then_inc(in_ld[s], 16)
                    sp.dma_start(lpage[s][:, j, :], clf_v[page, :, :]).then_inc(in_ld[s], 16)
                sp.dma_start(wpage[s][:, :, :], stw_v[b, :, :, :]).then_inc(in_ld[s], 16)
                sp.dma_start(fnew[s][:, :].rearrange("q (k x) -> q k x", k=2), fkvs_v[bass.ds(q0, TQ), :, :]).then_inc(in_ld[s], 16)
                sp.dma_start(nnew[s][:, :], nkvs_v[bass.ds(q0, TQ), 256:512]).then_inc(in_ld[s], 16)
                sp.dma_start(wnew[s][:, :], wins_v[b, PAST - TQ:PAST, :]).then_inc(in_ld[s], 16)
                sp.dma_start(lnew[s][:, :], flfs_b[b, :, :]).then_inc(in_ld[s], 16)
                sp.dma_start(qrow[s][:, 0:512], qs_d[bass.ds(q0, TQ), 0:512]).then_inc(in_ld[s], 16)
                for g in range(G):
                    sp.dma_start(qrow[s][:, 512:1024].rearrange("q (n g d) -> q n g d", g=G, d=HD)[:, :, g, :],
                                 qs_d[bass.ds(q0, TQ), 512 + 256 * g:768 + 256 * g].rearrange("q (n d) -> q n d", d=HD)).then_inc(in_ld[s], 16)

            def store(b, s):
                rows8 = bass.ds(b * TQ, TQ)
                sp.dma_start(mixs_d[rows8, 0:512], ofs[s][:, :]).then_inc(os_st[s], 16)
                for h in range(4):
                    dst = mixs_d[rows8, 512:1024].rearrange("q (g n d) -> q n g d", g=G, n=4)[:, h, :, :]
                    sp.dma_start(dst, ons[s][TQ * h:TQ * (h + 1), :, :]).then_inc(os_st[s], 16)

            for s in range(2):
                sp.nop().then_inc(os_st[s], CREDIT)
                load(s, s)
            with nc.allow_non_contiguous_dma(reason="gates of 64 tokens, once"):
                for h in range(NH):
                    for r in range(3):
                        sp.dma_start(gateS[h * TQ:(h + 1) * TQ, r, :],
                                     gs_d.rearrange("(b q) (r h) -> h r q b", q=TQ, h=NH)[h, r, :, :]).then_inc(g_ld, 16)
            with sp.Fori(0, TURNS2 - 1) as it:
                for s in range(2):
                    sp.wait_ge(o2_ready, 2 * it + (s + 1))
                    load(2 * it + (s + 2), s)
                for s in range(2):
                    sp.wait_ge(o2_done, 2 * it + (s + 1 + CREDIT))
                    store(2 * it + s, s)
            for s in range(2):
                sp.wait_ge(o2_done, B - 1 + s + CREDIT)
                store(B - 2 + s, s)
            for s in range(2):
                sp.wait_ge(os_st[s], 16 * N_OS * TURNS2 + CREDIT)

        @block.gpsimd
        def _(pool):
            ch = Chain(pool, pool_e)
            for s in range(2):
                ch.link(nc.gpsimd.memset(Qf[s][:, :], 0.0))
                ch.link(nc.gpsimd.memset(Qn[s][:, :], 0.0))
            nc.gpsimd.memset(ones512[:, :], 1.0).then_inc(e_set, 1)

        @block.tensor
        def _(pe):
            def pages(dst, src):
                for j in range(PAGES):
                    last = nc.tensor.transpose(dst[:, j * P:(j + 1) * P], src(j), ident)
                return last

            def flip(dst, src, eye, after_wait):
                if after_wait:
                    nc.tensor.matmul(dst, src, eye, start=True, stop=True)
                else:
                    nc.tensor.transpose(dst, src, eye)

            with pe.Fori(0, TURNS2) as it:
                for s in range(2):
                    b0, b1, b2, b3 = bk[4 * s:4 * s + 4]
                    pe.wait_ge(in_ld[s], it * (16 * N_LD) + 16 * N_LD)
                    pe.wait_ge(lf_ready, 2 * it + (s + 1))
                    pe.wait_ge(o2_done, 2 * it + CREDIT)
                    for j in range(8):
                        flip(b0[:, 8 * j:8 * j + 8], qrow[s][:, j * P:(j + 1) * P], ident[0:TQ, 0:TQ], j == 0)
                    for j in range(PAGES):
                        nc.tensor.transpose(b1[0:HD, j * P:(j + 1) * P], lf64[s][:, j, :, :].rearrange("p h q -> p (h q)"), ident)
                    nc.tensor.transpose(b0[0:HD, 64:72], lf64[s][0:TQ, PAGES, :, :].rearrange("p h q -> p (h q)"),
                                        ident[0:TQ, 0:TQ]).then_inc(p1_ready, 1)
                for s in range(2):
                    b0, b1, b2, b3 = bk[4 * s:4 * s + 4]
                    for k in range(6):
                        if k == 2:
                            pe.wait_ge(negc_done, 2 * it + (s + 1))
                        if k == 3:
                            pe.wait_ge(kt_act, it * 6 + (3 * s + 1))
                        if k == 4:
                            pe.wait_ge(kt_dve, it * 6 + (3 * s + 1))
                        if k == 5:
                            pe.wait_ge(kt_act, it * 6 + (3 * s + 2))
                        src = (lambda j: fpage[s][:, j, k * P:(k + 1) * P]) if k < 4 else \
                              (lambda j: (npage if k == 4 else wpage)[s][:, j, 0:P])
                        pages((b2, b3, b1)[k % 3], src).then_inc(kt_ready, 1)
                    for j in range(4):
                        nc.tensor.transpose(b0[:, 128 + 8 * j:136 + 8 * j], fnew[s][:, j * P:(j + 1) * P], ident[0:TQ, 0:TQ])
                    nc.tensor.transpose(b0[:, 160:168], nnew[s][:, 0:P], ident[0:TQ, 0:TQ])
                    nc.tensor.transpose(b0[:, 168:176], wnew[s][:, 0:P], ident[0:TQ, 0:TQ]).then_inc(ks_ready, 1)
                for s in range(2):
                    b0, b1, b2, b3 = bk[4 * s:4 * s + 4]
                    pe.wait_ge(q_bd, 2 * it + (s + 1))
                    pe.wait_ge(kt_act, it * 6 + (3 * s + 3))
                    pe.wait_ge(kt_dve, it * 6 + (3 * s + 3))
                    pe.wait_ge(ks_done, 2 * it + (s + 1))
                    for dst, cols in ((b1[0:HD, 0:PAST], slice(0, PAST)), (b0[0:HD, 192:200], slice(PAST, L))):
                        for j in range(4):
                            nc.tensor.matmul(dst, Qf[s][:, HD * j:HD * (j + 1)], KTf[s][:, j, cols], start=(j == 0), stop=(j == 3))
                    for i, dst in enumerate((b2, b3)):
                        nc.tensor.matmul(dst[0:HD, 0:PAST], Qn[s][:, :], KTn[s][:, i, 0:PAST], start=True, stop=True)
                        nc.tensor.matmul(b0[0:HD, 200 + 8 * i:208 + 8 * i], Qn[s][:, :], KTn[s][:, i, PAST:L], start=True, stop=True)
                    nc.tensor.matmul(b0[0:HD, 216:224], Qn[s][:, :], kcS[:, bass.ds(it * (2 * NBS) + NBS * s, NBS)],
                                     start=True, stop=True).then_inc(sc_done, 1)
                for s in range(2):
                    b0, b1, b2, b3 = bk[4 * s:4 * s + 4]
                    pe.wait_ge(p_ready, 2 * it + (s + 1))
                    for br, dst in enumerate((b1, b2, b3)):
                        for j in range(PAGES):
                            flip(dst[:, HD * j:HD * (j + 1)], sc[s][:, br, j * P:(j + 1) * P], ident[0:HD, 0:HD], br == 0 and j == 0)
                        nc.tensor.transpose(b0[0:TQ, 256 + HD * br:320 + HD * br], sc[s][:, br, PAST:L], ident[0:HD, 0:HD])
                    nc.tensor.transpose(b0[0:NBS, 448:512], scc[s][:, :], ident[0:HD, 0:HD]).then_inc(pt2_ready, 1)
                for s in range(2):
                    b0, b1, b2, b3 = bk[4 * s:4 * s + 4]
                    pe.wait_ge(pt2_act, 2 * it + (s + 1))
                    pe.wait_ge(pt2_dve, 2 * it + (s + 1))
                    for h in range(NH):
                        dst, a, v = b1[0:TQ, HD * h:HD * (h + 1)], slice(TQ * h, TQ * (h + 1)), slice(512 + HD * h, 576 + HD * h)
                        for j in range(PAGES):
                            nc.tensor.matmul(dst, PTb[s][:, 0, j, a], fpage[s][:, j, v], start=(j == 0), stop=False)
                        nc.tensor.matmul(dst, PTs[s][:, 0, a], fnew[s][:, v], start=False, stop=True)
                    for g in range(G):
                        dst, a, v = b2[0:32, HD * g:HD * (g + 1)], slice(32 * g, 32 * g + 32), slice(P + HD * g, P + HD * (g + 1))
                        nc.tensor.matmul(dst, PTs[s][:, 3, a], vcb[s][:, HD * g:HD * (g + 1)], start=True, stop=False)
                        for br, page, new in ((1, npage, nnew), (2, wpage, wnew)):
                            for j in range(PAGES):
                                nc.tensor.matmul(dst, PTb[s][:, br, j, a], page[s][:, j, v], start=False, stop=False)
                            last = nc.tensor.matmul(dst, PTs[s][:, br, a], new[s][:, v], start=False, stop=(br == 2))
                    last.then_inc(o2_ready, 1)

        @block.scalar
        def _(act):
            nc.scalar.nop().then_inc(o2_done, CREDIT)
            with act.Fori(0, TURNS2) as it:
                for s in range(2):
                    b0, b1, b2, b3 = bk[4 * s:4 * s + 4]
                    for k in (0, 2, 4):
                        act.wait_ge(kt_ready, it * 12 + (6 * s + k + 1))
                        dst = KTf[s][:, k, 0:PAST] if k < 4 else KTn[s][:, 0, 0:PAST]
                        nc.scalar.activation(dst, (b2, b3, b1)[k % 3], ACT.Copy).then_inc(kt_act, 1)
                    act.wait_ge(ks_ready, 2 * it + (s + 1))
                    nc.scalar.activation(KTf[s][:, :, PAST:L], b0[:, 128:160].rearrange("p (j n) -> p j n", j=4), ACT.Copy)
                    nc.scalar.activation(KTn[s][:, :, PAST:L], b0[:, 160:176].rearrange("p (j n) -> p j n", j=2), ACT.Copy).then_inc(ks_done, 1)
                for s in range(2):
                    b0, b1, b2, b3 = bk[4 * s:4 * s + 4]
                    act.wait_ge(sc_done, 2 * it + (s + 1))
                    nc.scalar.activation(sc[s][:, 1, 0:PAST], b2[0:HD, :], ACT.Copy)
                    nc.scalar.activation(sc[s][:, 2, 0:PAST], b3[0:HD, :], ACT.Copy).then_inc(sc_act, 1)
                for s in range(2):
                    act.wait_ge(m_ready, 2 * it + (s + 1))
                    for br in range(4):
                        x = sc[s][:, br, :] if br < 3 else scc[s][:, :]
                        ins = nc.scalar.activation(x, x, ACT.Exp, bias=srow[s][:, 0, br:br + 1], accum_out=srow[s][:, 1, br:br + 1])
                    ins.then_inc(e_ready, 1)
                for s in range(2):
                    b0, b1, b2, b3 = bk[4 * s:4 * s + 4]
                    act.wait_ge(pt2_ready, 2 * it + (s + 1))
                    nc.scalar.activation(PTb[s][:, 1, :, :], b2[:, 0:256].rearrange("p (j n) -> p j n", n=HD), ACT.Copy)
                    nc.scalar.activation(PTb[s][:, 2, :, :], b3[:, 0:256].rearrange("p (j n) -> p j n", n=HD), ACT.Copy).then_inc(pt2_act, 1)
                for s in range(2):
                    b0, b1, b2, b3 = bk[4 * s:4 * s + 4]
                    act.wait_ge(o2_ready, 2 * it + (s + 1))
                    act.wait_ge(os_st[s], it * (16 * N_OS) + CREDIT)
                    nc.scalar.activation(ofs[s][:, :], b1[0:TQ, :], ACT.Copy)
                    nc.scalar.activation(ons[s][:, :, :], b2[0:32, 0:P].rearrange("p (g d) -> p g d", g=G), ACT.Copy).then_inc(o2_done, 1)

        @block.vector
        def _(dve):
            ch = Chain(dve, dve_e)
            dve.wait_ge(e_set, 1)
            dve.wait_ge(g_ld, 16 * NH * 3)
            with dve.Fori(0, TURNS2) as it:
                ch.loop(it, SAMPLE_STEPS)
                for s in range(2):
                    dve.wait_ge(in_ld[s], it * (16 * N_LD) + 16 * N_LD)
                    nc.vector.tensor_copy(vcb[s][:, :], vcS[:, it * 2 + s, :])
                    nc.vector.tensor_copy(lf64[s][:, 0:PAGES, :, :].rearrange("p j h q -> p (j h) q"),
                                          lpage[s][:, :, :].rearrange("p j h -> p (j h)").unsqueeze(2).to_broadcast([P, PAGES * NH, TQ]))
                    nc.vector.tensor_copy(lf64[s][0:TQ, PAGES, :, :], lnew[s][:, :].unsqueeze(2).to_broadcast([TQ, NH, TQ])).then_inc(lf_ready, 1)
                for s in range(2):
                    b0, b1, b2, b3 = bk[4 * s:4 * s + 4]
                    dve.wait_ge(p1_ready, 2 * it + (s + 1))
                    q4 = Qf[s][:, :].rearrange("p (j c) -> p j c", c=80)
                    f4 = b0[:, 0:32].rearrange("p (j q) -> p j q", j=4)
                    nc.vector.tensor_copy(q4[0:HD, :, 0:8], f4[0:HD, :, :])
                    nc.vector.tensor_copy(q4[HD:P, :, 8:16], f4[HD:P, :, :])
                    nc.vector.tensor_copy(Qn[s][0:HD, 0:32], b0[0:HD, 32:64])
                    nc.vector.tensor_copy(Qn[s][HD:P, 32:64], b0[HD:P, 32:64]).then_inc(q_bd, 1)
                    ch.link(nc.vector.tensor_tensor_scan(negc[s][:, 0:PAST], ones512[:, :], b1[0:HD, :], 0.0, ALU.mult, ALU.add))
                    ch.link(nc.vector.tensor_tensor_scan(negc[s][:, PAST:L], ones512[:, 0:TQ], b0[0:HD, 64:72],
                                                         negc[s][:, PAST - 1:PAST], ALU.mult, ALU.add))
                    ch.link(nc.vector.tensor_scalar(negc[s][:, :], negc[s][:, :], -1.0, None, ALU.mult))
                    nc.vector.tensor_tensor(negc[s][:, PAST:L], negc[s][:, PAST:L], cst[0:HD, K_NEW:K_NEW + TQ], ALU.add).then_inc(negc_done, 1)
                for s in range(2):
                    b0, b1, b2, b3 = bk[4 * s:4 * s + 4]
                    for k in (1, 3, 5):
                        dve.wait_ge(kt_ready, it * 12 + (6 * s + k + 1))
                        dst = KTf[s][:, k, 0:PAST] if k < 4 else KTn[s][:, 1, 0:PAST]
                        nc.vector.tensor_copy(dst, (b2, b3, b1)[k % 3]).then_inc(kt_dve, 1)
                for s in range(2):
                    b0, b1, b2, b3 = bk[4 * s:4 * s + 4]
                    dve.wait_ge(sc_done, 2 * it + (s + 1))
                    dve.wait_ge(negc_done, 2 * it + (s + 1))
                    new = cst[0:HD, K_NEW:K_NEW + TQ].unsqueeze(1).to_broadcast([HD, 2, TQ])
                    nc.vector.tensor_tensor(sc[s][:, 0, 0:PAST], b1[0:HD, :], negc[s][:, 0:PAST], ALU.add)
                    nc.vector.tensor_tensor(sc[s][:, 0, PAST:L], b0[0:HD, 192:200], negc[s][:, PAST:L], ALU.add)
                    nc.vector.tensor_tensor(sc[s][:, 1:3, PAST:L], b0[0:HD, 200:216].rearrange("p (i n) -> p i n", i=2), new, ALU.add)
                    ch.link(nc.vector.tensor_copy(scc[s][:, :], b0[0:HD, 216:224]))
                    dve.wait_ge(sc_act, 2 * it + (s + 1))
                    ch.link(nc.vector.tensor_tensor(sc[s][:, 2, 0:TQ], sc[s][:, 2, 0:TQ], cst[0:HD, K_OLD:K_OLD + TQ], ALU.add))
                    nc.vector.tensor_reduce(srow[s][:, 0, 0:3], sc[s][:, :, :], AX.X, ALU.max, negate=True)
                    nc.vector.tensor_reduce(srow[s][:, 0, 3:4], scc[s][:, :], AX.X, ALU.max, negate=True).then_inc(m_ready, 1)
                for s in range(2):
                    dve.wait_ge(e_ready, 2 * it + (s + 1))
                    ch.link(nc.vector.reciprocal(srow[s][:, 2, :], srow[s][:, 1, :]))
                    w, g = srow[s][:, 2, :], gateS[:, :, bass.ds(it * 2 + s, 1)].rearrange("p r o -> p (r o)")
                    ch.link(nc.vector.tensor_tensor(w[:, 1:3], w[:, 1:3], g[:, 1:3], ALU.mult))
                    ch.link(nc.vector.tensor_tensor(w[:, 3:4], w[:, 3:4], g[:, 0:1], ALU.mult))
                    for br in range(4):
                        x = sc[s][:, br, :] if br < 3 else scc[s][:, :]
                        ins = nc.vector.tensor_scalar(x, x, w[:, br:br + 1], None, ALU.mult)
                    ins.then_inc(p_ready, 1)
                for s in range(2):
                    b0, b1, b2, b3 = bk[4 * s:4 * s + 4]
                    dve.wait_ge(pt2_ready, 2 * it + (s + 1))
                    nc.vector.tensor_copy(PTb[s][:, 0, :, :], b1[:, 0:256].rearrange("p (j n) -> p j n", n=HD))
                    nc.vector.tensor_copy(PTs[s][:, :, :], b0[0:TQ, 256:512].rearrange("p (j n) -> p j n", n=HD)).then_inc(pt2_dve, 1)
                ch.end(TURNS2)

    wo_ld, mx_ld, f_misc, gt_ready, gt_done, gb_ready, gb_done = (sem(n) for n in (
        "wout_loaded", "sample_mix_loaded", "gain2_ready", "gt1_transposed", "gt1_copied", "gt1_spread", "gt1b_ready"))
    x_ld = [sem(f"x_tile_loaded{i}") for i in range(2)]
    x1_st = [sem(f"x1_stored{i}") for i in range(2)]
    (mt_ready, mt_act, mt_dve, out_ready, x1_ready, sq2, var2, root2, rstd2, xn2, xt_ready, h2_act, h2_dve) = (sem(f"f_{n}") for n in (
        "mix_transposed", "mix_act", "mix_dve", "projected", "x1_ready", "squares", "variance", "root", "rstd", "xn_ready",
        "xn_transposed", "h_act", "h_dve"))
    h_hi, h_lo, h_pad = sem("h_hi"), sem("h_lo"), sem("h_pad_zero")
    dve_f = sem("dve_step_f")
    x1_tiles = [(x1_d[t * P:t * P + rows(t), :]) for t in range(T9)]

    with nc.Block() as block:

        @block.sync
        def _(sp):
            sp.dma_start(mix[0:NS, NT, :], mixs_d).then_inc(mx_ld, 16)
            for k in range(2):
                sp.dma_start(wo[:, 4 * k:4 * k + 4, :], wout_v[:, 4 * k:4 * k + 4, :]).then_inc(wo_ld, 16)
            for t in range(T9 + 1):
                if t < T9:
                    if t >= 2:
                        sp.wait_ge(x1_ready, t - 1)
                    src = xs_v if t == NT else xp_v[:, t, :]
                    sp.dma_start(xt[t % 2][0:rows(t), :], src).then_inc(x_ld[t % 2], 16)
                if t:
                    sp.wait_ge(x1_ready, t)
                    sp.dma_start(x1_tiles[t - 1], x1[(t - 1) % 2][0:rows(t - 1), :]).then_inc(x1_st[(t - 1) % 2], 16)
            sp.wait_ge(x1_st[0], 16 * 5)
            sp.wait_ge(x1_st[1], 16 * 4)

        @block.tensor
        def _(pe):
            for k in range(KC):
                last = nc.tensor.transpose(bk[k // 4][0:B + 1, P * (k % 4):P * (k % 4 + 1)], modT[:, 16 + k, :], ident)
            last.then_inc(gt_ready, 1)
            pe.wait_ge(gt_done, 1)
            for i, (col, r) in enumerate(((K_SELP, P), (K_SELS, NS))):
                for c in range(2):
                    last = nc.tensor.matmul(bk[2 + 2 * i + c][0:r, :], cst[0:B + 1, col:col + r], gt1n[:, 512 * c:512 * (c + 1)],
                                            start=True, stop=True)
            last.then_inc(gb_ready, 1)

            def mix_t(t):
                r = rows(t)
                if t:
                    pe.wait_ge(mt_act, t)
                    pe.wait_ge(mt_dve, t)
                if t == NT:
                    pe.wait_ge(mx_ld, 16)
                for k in range(KC):
                    last = nc.tensor.transpose(bk[k // 4][:, P * (k % 4):P * (k % 4) + r], mix[0:r, t, k * P:(k + 1) * P], ident[0:r, 0:r])
                last.then_inc(mt_ready, 1)

            def xn_t(t):
                r = rows(t)
                pe.wait_ge(xn2, t + 1)
                if t:
                    pe.wait_ge(h2_act, t)
                    pe.wait_ge(h2_dve, t)
                for k in range(KC):
                    last = nc.tensor.transpose(bk[6 + k // 4][:, P * (k % 4):P * (k % 4) + r], xn[t % 2][0:r, k * P:(k + 1) * P], ident[0:r, 0:r])
                last.then_inc(xt_ready, 1)

            mix_t(0)
            pe.wait_ge(gb_done, 1)
            pe.wait_ge(wo_ld, 32)
            for t in range(T9):
                r = rows(t)
                if t + 1 < T9:
                    mix_t(t + 1)
                else:
                    pe.wait_ge(mt_act, T9)
                    pe.wait_ge(mt_dve, T9)
                if t >= 2:
                    pe.wait_ge(x1_ready, t - 1)
                for c in range(2):
                    for k in range(KC):
                        last = nc.tensor.matmul(bk[2 + 2 * (t % 2) + c][0:r, :], mixT[t % 2][:, k, 0:r], wo[:, k, 512 * c:512 * (c + 1)],
                                                start=(k == 0), stop=(k == KC - 1))
                last.then_inc(out_ready, 1)
                if t:
                    xn_t(t - 1)
            xn_t(T9 - 1)

        @block.scalar
        def _(act):
            def mix_copy(t):
                r = rows(t)
                act.wait_ge(mt_ready, t + 1)
                nc.scalar.activation(mixT[t % 2][:, 0:4, 0:r], bk[0].rearrange("p (k n) -> p k n", k=4)[:, :, 0:r], ACT.Copy).then_inc(mt_act, 1)

            def h_copy(t):
                act.wait_ge(xt_ready, t + 1)
                act.wait_ge(f_misc, 1)
                if t >= 2:
                    act.wait_ge(h_lo, t - 1)
                if t == NT:
                    return
                for k in range(4):
                    last = nc.scalar.activation(h2s[t % 2][:, k, :], bk[6][:, P * k:P * (k + 1)], ACT.Identity,
                                                bias=modT[:, 24 + k, 0:1], scale=gain2[:, k, 0:1])
                last.then_inc(h2_act, 1)

            def h_split(t):
                act.wait_ge(h2_act, min(t + 1, NT))
                act.wait_ge(h2_dve, t + 1)
                nc.scalar.activation(h2hi[:, :, t * P:t * P + rows(t)], h2s[t % 2][:, :, 0:rows(t)], ACT.Copy).then_inc(h_hi, 1)

            mix_copy(0)
            for t in range(T9):
                r = rows(t)
                if t + 1 < T9:
                    mix_copy(t + 1)
                act.wait_ge(x1_ready, t + 1)
                if t:
                    act.wait_ge(sq2, t)
                nc.scalar.activation(junk2[0:r, :], x1[t % 2][0:r, :], ACT.Square, accum_out=ssum[0:r, t:t + 1]).then_inc(sq2, 1)
                act.wait_ge(var2, t + 1)
                nc.scalar.activation(rstd[0:r, t:t + 1], ssum[0:r, t:t + 1], ACT.Sqrt).then_inc(root2, 1)
                act.wait_ge(rstd2, t + 1)
                if t >= 2:
                    act.wait_ge(xt_ready, t - 1)
                nc.scalar.activation(xn[t % 2][0:r, :], x1[t % 2][0:r, :], ACT.Copy, scale=rstd[0:r, t:t + 1]).then_inc(xn2, 1)
                if t:
                    h_copy(t - 1)
                    h_split(t - 1)
            h_copy(NT)
            h_split(NT)

        @block.gpsimd
        def _(pool):
            for h in (h2hi, h2lo):
                nc.gpsimd.memset(h[:, :, TOK:TP].bitcast(F32), 0.0).then_inc(h_pad, 1)
            pool.wait_ge(h_pad, 2)

        @block.vector
        def _(dve):
            ch = Chain(dve, dve_f)
            nc.vector.scalar_tensor_tensor(gain2[:, :, :], modT[:, 32:40, :], 1.0,
                                           vecT[:, 56:64].unsqueeze(2).to_broadcast([P, KC, B + 1]), ALU.add, ALU.mult).then_inc(f_misc, 1)
            dve.wait_ge(gt_ready, 1)
            nc.vector.tensor_copy(gt1n[:, :], banks(0, 2)[0:B + 1, :]).then_inc(gt_done, 1)
            dve.wait_ge(gb_ready, 1)
            nc.vector.tensor_copy(gt1b[:, 0, :], banks(2, 2))
            ch.link(nc.vector.tensor_copy(gt1b[0:NS, 1, :], banks(4, 2)[0:NS, :]))
            nc.vector.nop().then_inc(gb_done, 1)

            def mix_copy(t):
                r = rows(t)
                dve.wait_ge(mt_ready, t + 1)
                nc.vector.tensor_copy(mixT[t % 2][:, 4:8, 0:r], bk[1].rearrange("p (k n) -> p k n", k=4)[:, :, 0:r]).then_inc(mt_dve, 1)

            def h_copy(t):
                dve.wait_ge(xt_ready, t + 1)
                dve.wait_ge(f_misc, 1)
                if t >= 2:
                    dve.wait_ge(h_lo, t - 1)
                if t < NT:
                    for k in range(4, 8):
                        last = nc.vector.tensor_scalar(h2s[t % 2][:, k, :], bk[7][:, P * (k - 4):P * (k - 3)],
                                                       gain2[:, k, 0:1], modT[:, 24 + k, 0:1], ALU.mult, ALU.add)
                    last.then_inc(h2_dve, 1)
                    return
                hs = h2s[NT % 2][:, :, 0:NS].rearrange("p k (b t) -> p k b t", b=B)
                src = banks(6, 2).rearrange("p (k n) -> p k n", n=P)[:, :, 0:NS].rearrange("p k (b t) -> p k b t", b=B)
                ch.link(nc.vector.tensor_tensor(hs, src, gain2[:, :, 1:B + 1].unsqueeze(3).to_broadcast([P, KC, B, TQ]), ALU.mult))
                nc.vector.tensor_tensor(hs, hs, modT[:, 24:32, 1:B + 1].unsqueeze(3).to_broadcast([P, KC, B, TQ]), ALU.add).then_inc(h2_dve, 1)

            def h_split(t):
                dve.wait_ge(h_hi, t + 1)
                tok = slice(t * P, t * P + rows(t))
                nc.vector.tensor_tensor(h2lo[:, :, tok], h2s[t % 2][:, :, 0:rows(t)], h2hi[:, :, tok].bitcast(F32), ALU.subtract).then_inc(h_lo, 1)

            mix_copy(0)
            for t in range(T9):
                r = rows(t)
                if t + 1 < T9:
                    mix_copy(t + 1)
                dve.wait_ge(out_ready, t + 1)
                dve.wait_ge(x_ld[t % 2], 16 * (t // 2 + 1))
                if t >= 2:
                    dve.wait_ge(x1_st[t % 2], 16 * (t // 2))
                    dve.wait_ge(xn2, t - 1)
                ch.link(nc.vector.tensor_tensor(x1[t % 2][0:r, :], banks(2 + 2 * (t % 2), 2)[0:r, :], gt1b[0:r, int(t == NT), :], ALU.mult))
                nc.vector.tensor_tensor(x1[t % 2][0:r, :], x1[t % 2][0:r, :], xt[t % 2][0:r, :], ALU.add).then_inc(x1_ready, 1)
                dve.wait_ge(sq2, t + 1)
                nc.vector.tensor_scalar(ssum[0:r, t:t + 1], ssum[0:r, t:t + 1], 1.0 / D, EPS, ALU.mult, ALU.add).then_inc(var2, 1)
                dve.wait_ge(root2, t + 1)
                nc.vector.reciprocal(rstd[0:r, t:t + 1], rstd[0:r, t:t + 1]).then_inc(rstd2, 1)
                if t:
                    h_copy(t - 1)
                    h_split(t - 1)
            h_copy(NT)
            h_split(NT)

    ROUNDS, LOADS, JOBS = FC // UC, 8, UC + KC
    BANKS_FREE, DOWN_FREE, U_FREE = JOBS, 3, 2
    GRP = 364
    w_ld = [sem(f"weights_loaded{i}") for i in range(2)]
    xo_ld = [sem(f"x1_reloaded{i}") for i in range(3)]
    yo_st = [sem(f"y_stored{i}") for i in range(3)]
    (w_hi, w_lo, up_ready, dn_ready, banks_read, u_relu, u_hi, u_lo, y_zero, y_gated, y_gated_s, yt_ready, yo_ready) = (sem(n) for n in (
        "weights_hi", "weights_lo", "up_ready", "down_ready", "banks_read", "u_relu", "u_hi", "u_lo", "y_zeroed", "y_gated", "y_gated_sample",
        "y_transposed", "y_added"))
    y_tiles = [ys_v if t == NT else yp_v[:, t, :] for t in range(T9)]

    def groups(ap):
        return ap.rearrange("p (g n) -> p g n", g=3)

    with nc.Block() as block:

        @block.sync
        def _(sp):
            def load(r, i):
                dst = wraw[i % 2]
                if i < UC:
                    sp.dma_start(dst.rearrange("p (k n) -> p k n", k=KC), wup_v[:, :, bass.ds(r * (UC * P) + P * i, P)]).then_inc(w_ld[i % 2], 16)
                else:
                    sp.dma_start(dst.rearrange("p (f n) -> p f n", f=UC),
                                 wdn_v[:, bass.ds(r * UC, UC), 2 * P * (i - UC):2 * P * (i - UC + 1)]).then_inc(w_ld[i % 2], 16)

            load(0, 0)
            load(0, 1)
            with sp.Fori(0, ROUNDS - 1) as r:
                for i in range(LOADS):
                    sp.wait_ge(w_lo, r * LOADS + (i + 1))
                    load(r + (i + 2) // LOADS, (i + 2) % LOADS)
            for i in range(LOADS - 2):
                sp.wait_ge(w_lo, (ROUNDS - 1) * LOADS + i + 1)
                load(ROUNDS - 1, i + 2)
            for t in range(T9 + 2):
                if t >= 2:
                    sp.wait_ge(yo_ready, t - 1)
                    sp.dma_start(y_tiles[t - 2], xo[(t - 2) % 3][0:rows(t - 2), :]).then_inc(yo_st[(t - 2) % 3], 16)
                if t < T9:
                    if t >= 3:
                        sp.wait_ge(yo_st[t % 3], 16 * (t // 3))
                    sp.dma_start(xo[t % 3][0:rows(t), :], x1_tiles[t]).then_inc(xo_ld[t % 3], 16)
            for i in range(3):
                sp.wait_ge(yo_st[i], 16 * 3)

        @block.tensor
        def _(pe):
            def product(ps, hi_w, lo_w, hi_x, lo_x, first, final):
                for n, (w, x) in enumerate(((hi_w, hi_x), (hi_w, lo_x), (lo_w, hi_x))):
                    for g in range(3):
                        last = nc.tensor.matmul(bk[ps + g][:, 0:GRP], w, x[:, GRP * g:GRP * (g + 1)],
                                                start=(first and n == 0), stop=(final and n == 2))
                return last

            def round_(r):
                for i in range(LOADS):
                    pe.wait_ge(w_lo, r * LOADS + (i + 1))
                    s = i % 2
                    for j in ([i] if i < UC else [2 * i - UC, 2 * i - UC + 1]):
                        pe.wait_ge(banks_read, r * JOBS + (j - 1 + BANKS_FREE))
                        for k in range(KC if i < UC else UC):
                            if i < UC:
                                w = slice(P * k, P * (k + 1))
                                x = h2hi[:, k, :], h2lo[:, k, :]
                            else:
                                if j == UC:
                                    pe.wait_ge(u_lo, r * UC + (k + 1 + U_FREE))
                                w = slice(2 * P * k + P * (j % 2), 2 * P * k + P * (j % 2 + 1))
                                x = u2hi[:, k, :], u2lo[:, k, :]
                            last = product(3 * (j % 2), whi[s][:, w], wlo[s][:, w], x[0], x[1], k == 0, k == (KC if i < UC else UC) - 1)
                        last.then_inc(up_ready if i < UC else dn_ready, 1)

            pe.wait_ge(h_pad, 2)
            with pe.Fori(0, ROUNDS - 1) as r:
                round_(r)
            round_(ROUNDS - 1)
            pe.wait_ge(y_gated, KC)
            pe.wait_ge(y_gated_s, 1)
            for t in range(T9):
                pe.wait_ge(banks_read, BANKS_FREE + ROUNDS * JOBS)
                if t >= 4:
                    pe.wait_ge(yo_ready, t - 3)
                for m in range(KC):
                    last = nc.tensor.transpose(bk[2 * (t % 4) + m // 4][0:rows(t), P * (m % 4):P * (m % 4 + 1)],
                                               yT[:, m, t * P:t * P + rows(t)], ident)
                last.then_inc(yt_ready, 1)

        @block.scalar
        def _(act):
            def weights(r, i):
                act.wait_ge(w_ld[i % 2], r * (16 * LOADS // 2) + 16 * (i // 2 + 1))
                if i in (0, 1):
                    act.wait_ge(dn_ready, r * KC + (2 * (i - 1) + DOWN_FREE))
                elif i - 2 < UC:
                    act.wait_ge(up_ready, r * UC + (i - 1))
                else:
                    act.wait_ge(dn_ready, r * KC + (2 * (i - 2 - UC + 1) + DOWN_FREE))
                nc.scalar.activation(whi[i % 2][:, :], wraw[i % 2][:, :], ACT.Copy).then_inc(w_hi, 1)

            def round_(r, final=False):
                for i in range(LOADS):
                    if not (final and i == LOADS - 1):
                        weights(r + (i + 1) // LOADS, (i + 1) % LOADS)
                    if i < UC:
                        act.wait_ge(up_ready, r * UC + (i + 1))
                        act.wait_ge(u_lo, r * UC + (i - 1 + U_FREE))
                        nc.scalar.activation(groups(us[i % 2][:, :]), bank[:, 3 * (i % 2):3 * (i % 2) + 3, 0:GRP], ACT.Relu).then_inc(u_relu, 1)
                        act.wait_ge(banks_read, r * JOBS + (i + 1 + BANKS_FREE))
                        nc.scalar.activation(u2hi[:, i, :], us[i % 2][:, :], ACT.Copy).then_inc(u_hi, 1)

            nc.scalar.nop().then_inc(dn_ready, DOWN_FREE)
            weights(0, 0)
            with act.Fori(0, ROUNDS - 1) as r:
                round_(r)
            round_(ROUNDS - 1, True)
            for m in range(KC):
                act.wait_ge(banks_read, BANKS_FREE + ROUNDS * JOBS - KC + m + 1)
                nc.scalar.activation(yT[:, m, 0:S], yT[:, m, 0:S], ACT.Copy, scale=modT[:, 40 + m, 0:1]).then_inc(y_gated, 1)

        @block.gpsimd
        def _(pool):
            nc.gpsimd.memset(yT[:, :, :], 0.0).then_inc(y_zero, 1)

        @block.vector
        def _(dve):
            def weights(r, i):
                dve.wait_ge(w_hi, r * LOADS + (i + 1))
                nc.vector.tensor_tensor(wlo[i % 2][:, :], wraw[i % 2][:, :], whi[i % 2][:, :].bitcast(F32), ALU.subtract).then_inc(w_lo, 1)

            def round_(r, final=False):
                for i in range(LOADS):
                    if not (final and i == LOADS - 1):
                        weights(r + (i + 1) // LOADS, (i + 1) % LOADS)
                    if i < UC:
                        dve.wait_ge(u_relu, r * UC + (i + 1))
                        u = us[i % 2][:, :]
                        nc.vector.tensor_tensor(u, u, u, ALU.mult).then_inc(banks_read, 1)
                        dve.wait_ge(u_hi, r * UC + (i + 1))
                        nc.vector.tensor_tensor(u2lo[:, i, :], us[i % 2][:, :], u2hi[:, i, :].bitcast(F32), ALU.subtract).then_inc(u_lo, 1)
                        continue
                    for m in (2 * (i - UC), 2 * (i - UC) + 1):
                        dve.wait_ge(dn_ready, r * KC + (m + 1 + DOWN_FREE))
                        dve.wait_ge(banks_read, r * JOBS + (m + 1 + UC - JOBS + BANKS_FREE))
                        y = groups(yT[:, m, :])
                        nc.vector.tensor_tensor(y, bank[:, 3 * (m % 2):3 * (m % 2) + 3, 0:GRP], y, ALU.add).then_inc(banks_read, 1)

            nc.vector.nop().then_inc(banks_read, BANKS_FREE)
            nc.vector.nop().then_inc(u_lo, U_FREE)
            dve.wait_ge(y_zero, 1)
            weights(0, 0)
            with dve.Fori(0, ROUNDS - 1) as r:
                round_(r)
            round_(ROUNDS - 1, True)
            dve.wait_ge(banks_read, BANKS_FREE + ROUNDS * JOBS)
            ysm = yT[:, :, S:TOK].rearrange("p m (b t) -> p m b t", b=B)
            nc.vector.tensor_tensor(ysm, ysm, modT[:, 40:48, 1:B + 1].unsqueeze(3).to_broadcast([P, KC, B, TQ]), ALU.mult).then_inc(y_gated_s, 1)
            for t in range(T9):
                dve.wait_ge(yt_ready, t + 1)
                dve.wait_ge(xo_ld[t % 3], 16 * (t // 3 + 1))
                nc.vector.tensor_tensor(xo[t % 3][0:rows(t), :], banks(2 * (t % 4), 2)[0:rows(t), :], xo[t % 3][0:rows(t), :], ALU.add).then_inc(yo_ready, 1)


_INS = ['x_prompt', 'x_sample', 'c_prompt', 'c_sample', 'cache_fox_kv', 'cache_fox_logf', 'cache_nsa_kv',
        'state_nsa_win', 'page_table', 'w_ada', 'b_ada', 'norm1_g', 'norm2_g', 'w_in', 'b_forget', 'b_gate',
        'g_q_fox', 'g_k_fox', 'g_q_nsa', 'g_k_nsa', 'pe_cmp', 'w_cmp', 'w_out', 'w_up', 'w_down']
_OUTS = [((1, S, D), 'float32'), ((B, TQ, D), 'float32'),
         ((1, 1, S, 2, NH, HD), 'float32'), ((1, B, TQ, 2, NH, HD), 'float32'),
         ((1, 1, S, NH), 'float32'), ((1, B, TQ, NH), 'float32'),
         ((1, 1, S, 4, G, HD), 'float32'), ((1, B, TQ, 4, G, HD), 'float32'),
         ((1, 1, 512, 2, G, HD), 'float32'), ((1, B, PAST, 2, G, HD), 'float32')]


def kernel(**inputs):
    import numpy as _np
    import concourse.bacc as _bacc
    from concourse import mybir as _mybir
    from concourse.bass_utils import run_bass_kernel_spmd as _run

    nc = _bacc.Bacc("TRN2", target_bir_lowering=False, num_devices=1)
    arrays, args = {}, []
    for name in _INS + ['constants']:
        a = constants() if name == 'constants' else _np.ascontiguousarray(inputs[name])
        arrays[f"in_{name}_dram"] = a
        args.append(nc.dram_tensor(f"in_{name}_dram", a.shape, _mybir.dt.from_np(a.dtype), kind="ExternalInput").ap())
    for i, (shape, dtype) in enumerate(_OUTS):
        dt = _mybir.dt.from_np(_np.dtype(dtype))
        args.append(nc.dram_tensor(f"out_{i}_dram", shape, dt, kind="ExternalOutput").ap())
    layer_kernel(nc, *args)
    r = _run(nc, [arrays], core_ids=[0])
    return tuple(r.results[0][f"out_{i}_dram"] for i in range(len(_OUTS)))
```

```python
import numpy as np

import concourse.bass as bass
from concourse import mybir

F32 = mybir.dt.float32
F32R = mybir.dt.float32r
I32 = mybir.dt.int32
ALU = mybir.AluOpType
ACT = mybir.ActivationFunctionType
AX = mybir.AxisListType

P = 128
D = 1024
KC = D // P
NT = 8
T9 = NT + 1
S = NT * P
B, TQ = 8, 8
NS = B * TQ
TOK = S + NS
HD = 64
NH = 8
G = 2
PAST = 512
PAGES = PAST // P
L = PAST + TQ
BLOCK = 64
NBP = S // BLOCK
NBS = PAST // BLOCK
DFF = 4096
FC = DFF // P
EPS = 1e-6
SCALE = HD ** -0.5
NEG = -1e30
CREDIT = 1
EXP_MAX = 88.0

C_QF, C_KF, C_VF, C_F, C_QN, C_KV = 0, 512, 1024, 1536, 1544, 2056
C_WIN = C_KV + 512
N_MISC = 256 + 24
ZB = ["misc", "kf", "vf", "qf", "qn", "cs"]
ZW = {"misc": N_MISC + 8, "kf": 512, "vf": 512, "qf": 512, "qn": 512, "cs": 512}
ZC = {"kf": C_KF, "vf": C_VF, "qf": C_QF, "qn": C_QN, "cs": C_KV}

K_ID, K_U, K_ONE, K_CAUS, K_WIN, K_CMP, K_ANY = 0, 128, 256, 384, 512, 640, 768
K_COS, K_SIN, K_SELP, K_SELS, K_NEW, K_OLD = 769, 913, 1057, 1185, 1249, 1257
K_SELH = 1265
K_HEAD = K_SELH + NH
K_N = K_HEAD + NH


def constants():
    c = np.zeros((P, K_N), np.float32)
    p = np.arange(P)[:, None]
    f = np.arange(P)[None, :]
    c[:, K_ID:K_ID + P] = p == f
    c[:, K_U:K_U + P] = p <= f
    c[:, K_ONE:K_ONE + P] = 1
    c[:, K_CAUS:K_CAUS + P] = np.where(f <= p, 0, NEG)
    c[:, K_WIN:K_WIN + P] = np.where(f > p, 0, NEG)
    for t in range(NT):
        blk = np.arange(NBP)[None, :]
        c[:, K_CMP + NBP * t:K_CMP + NBP * (t + 1)] = np.where((blk + 1) * BLOCK <= t * P + p + 1, 0, NEG)
    c[:, K_ANY] = (np.arange(P) + 1 >= BLOCK)
    half = 8
    inv = (np.float32(500000.0) ** (-np.arange(half, dtype=np.float32) / np.float32(half))).astype(np.float32)
    for t in range(T9):
        pos = t * P + np.arange(P) if t < NT else PAST + np.arange(P) % TQ
        ang = pos.astype(np.float32)[:, None] * inv[None, :]
        co, si = np.cos(ang), np.sin(ang)
        c[:, K_COS + 16 * t:K_COS + 16 * t + 16] = np.concatenate([co, co], 1)
        c[:, K_SIN + 16 * t:K_SIN + 16 * t + 16] = np.concatenate([-si, si], 1)
    c[0, K_SELP:K_SELP + P] = 1
    for b in range(B):
        c[b + 1, K_SELS + b * TQ:K_SELS + (b + 1) * TQ] = 1
    for h in range(NH):
        c[[h, 32 + h], K_SELH + h] = 1
        c[h * TQ:(h + 1) * TQ, K_HEAD + h] = 1
    q, k = (np.arange(HD) % TQ)[:, None], np.arange(TQ)[None, :]
    c[:HD, K_NEW:K_NEW + TQ] = np.where(k <= q, 0, NEG)
    c[:HD, K_OLD:K_OLD + TQ] = np.where(k > q, 0, NEG)
    return c


class Chain:

    def __init__(self, eng, sem):
        self.eng, self.sem = eng, sem
        self.base, self.k, self.reg, self.per = 0, 0, None, 0

    def loop(self, reg, per):
        self.base += self.k
        self.k, self.reg, self.per = 0, reg, per

    def end(self, times):
        assert self.k == self.per, ("steps in the loop", self.k, self.per)
        self.base, self.k, self.reg = self.base + times * self.per, 0, None

    def link(self, ins):
        self.k += 1
        ins.then_inc(self.sem, 1)
        n = self.base + self.k
        self.eng.wait_ge(self.sem, n if self.reg is None else self.reg * self.per + n)


def rows(t):
    return P if t < NT else NS


def attention_units(kinds):
    out = []
    for t in range(NT):
        for kind in kinds:
            if kind == "cmp":
                out.append((kind, t, 0, 1))
            elif kind == "win":
                lo = max(0, t - 4)
                out.append((kind, t, lo, t + 1 - lo))
            else:
                out.append((kind, t, 0, t + 1))
    return out


def layer_kernel(nc, x_prompt, x_sample, c_prompt, c_sample, cache_fox_kv, cache_fox_logf, cache_nsa_kv,
                 state_nsa_win, page_table, w_ada, b_ada, norm1_g, norm2_g, w_in, b_forget, b_gate,
                 g_q_fox, g_k_fox, g_q_nsa, g_k_nsa, pe_cmp, w_cmp, w_out, w_up, w_down, consts,
                 y_p, y_s, fkv_p, fkv_s, flf_p, flf_s, nkv_p, nkv_s, win_p, win_s):
    n_pool = cache_fox_kv.shape[1]
    xp_v = x_prompt.rearrange("a (t p) d -> p (a t) d", p=P)
    xs_v = x_sample.rearrange("b t d -> (b t) d")
    wada_v = w_ada.rearrange("a (k p) n -> p (a k) n", p=P)
    win_v = w_in.rearrange("a (k p) n -> p (a k) n", p=P)
    wout_v = w_out.rearrange("a (k p) n -> p (a k) n", p=P)
    wup_v = w_up.rearrange("a (k p) n -> p (a k) n", p=P)
    wdn_v = w_down.rearrange("a (f p) n -> p (a f) n", p=P)
    cfox_v = cache_fox_kv.rearrange("a n p k h d -> (a n) p (k h d)")
    clf_v = cache_fox_logf.rearrange("a n p h -> (a n) p h")
    cnsa_v = cache_nsa_kv.rearrange("a n p k g d -> (a n) p (k g d)")
    stw_v = state_nsa_win.rearrange("a b (j p) k g d -> (a b) p j (k g d)", p=P)
    stw_rows = state_nsa_win.rearrange("a b s k g d -> (a b) s (k g d)")
    fkvp_v = fkv_p.rearrange("a b (t p) k h d -> (a b t) p k (h d)", p=P)
    fkvs_v = fkv_s.rearrange("a b t k h d -> (a b t) k (h d)")
    nkvp_v = nkv_p.rearrange("a b (t p) k g d -> (a b t) p (k g d)", p=P)
    nkvs_v = nkv_s.rearrange("a b t k g d -> (a b t) (k g d)")
    winp_v = win_p.rearrange("a b (t p) k g d -> (a b t) p (k g d)", p=P)
    wins_v = win_s.rearrange("a b s k g d -> (a b) s (k g d)")
    flfs_b = flf_s.rearrange("a b t h -> (a b) t h")
    yp_v = y_p.rearrange("a (t p) d -> p (a t) d", p=P)
    ys_v = y_s.rearrange("b t d -> (b t) d")
    qt_d = nc.dram_tensor("qt_scratch", [2, NH, HD, S], F32, kind="Internal").ap()
    qs_d = nc.dram_tensor("qs_scratch", [NS, D], F32, kind="Internal").ap()
    gs_d = nc.dram_tensor("gs_scratch", [NS, 24], F32, kind="Internal").ap()
    mixs_d = nc.dram_tensor("mixs_scratch", [B, 2, HD, HD], F32, kind="Internal").ap()
    x1_d = nc.dram_tensor("x1_scratch", [TOK, D], F32, kind="Internal").ap()

    ARENA = 16640

    def at(name, shape, off, dt=F32):
        return nc.alloc_sbuf_tensor_at(name, shape, dt, offset=ARENA + off)

    small = [0]

    def keep(name, shape, dt=F32):
        n = 4
        for s in shape[1:]:
            n *= s
        off = small[0]
        small[0] += (n + 31) // 32 * 32
        return at(name, shape, off, dt)

    cst = keep("cst", [P, K_N])
    modT = keep("modT", [P, 6 * KC, B + 1])
    vecT = keep("vecT", [P, HD])
    gain1 = keep("gain1", [P, KC, B + 1])
    gain2 = keep("gain2", [P, KC, B + 1])
    gates = keep("gates", [P, T9, 24])
    logf = keep("logf", [P, T9, NH])
    ssum = keep("ssum", [P, 16])
    rstd = keep("rstd", [P, 16])
    gate_qk = keep("gate_qk", [P, 2, 4])
    nmax = keep("nmax", [P, 2, 4])
    scT = keep("scT", [P, KC, B + 1])
    ptab = keep("ptab", [1, B * PAGES], I32)
    kcS = keep("kcS", [P, B * NBS])
    kcP = keep("kcP", [P, G, NBP], F32R)
    vcP = keep("vcP", [P, G, HD + 1])
    gateS = keep("gateS", [HD, 3, B])
    SMALL = small[0]
    assert SMALL <= 14336, SMALL
    KV = 14336
    kTf = at("kTf", [P, NH, S], KV, F32R)
    Vf = at("Vf", [P, NT, NH, HD + 1], KV + 32768)
    kTs = at("kTs", [P, G, S], KV + 49408, F32R)
    kTw = at("kTw", [P, G, S], KV + 57600, F32R)
    Vs = at("Vs", [P, NT, G, HD + 1], KV + 65792)
    Vw = at("Vw", [P, NT, G, HD + 1], KV + 69952)
    XC = 88448
    Xc = at("Xc", [P, NBP + B * NBS, 2, BLOCK], XC)
    HT = 96640
    hT = at("hT", [P, KC, TOK], HT)
    WB = 131456
    wbuf = [at(f"wbuf{i}", [P, KC, 512], WB + 16384 * i) for i in range(3)]
    ST = WB + 3 * 16384
    zsb = [at(f"zsb{i}", [P, 512], ST + 2048 * i) for i in range(5)]
    sq = [at(f"sq{i}", [P, 512], ST + 10240 + 2048 * i) for i in range(2)]
    qst = [at(f"qst{i}", [HD, NH, P], ST + 14336 + 4096 * i) for i in range(2)]
    rope = [at(f"rope{i}", [P, NH, 16], ST + 22528 + 512 * i) for i in range(2)]
    EXTRA = ST + 23552
    gvec = at("gvec", [P, 6, HD], EXTRA)
    hv = [at(f"hv{i}", [P, 3, NH], EXTRA + 1536 + 96 * i) for i in range(3)]
    graw = at("graw", [P, T9, 32], EXTRA + 1824)
    gexp = at("gexp", [P, T9, 32], EXTRA + 2976)
    bias32 = at("bias32", [P, 32], EXTRA + 4128)
    peT = at("peT", [P, 2, BLOCK], EXTRA + 4256)
    csum = at("csum", [P, NT, NH], EXTRA + 4768)
    cpre = at("cpre", [P, NT, NH], EXTRA + 5024)
    nCT = at("nCT", [HD, P], EXTRA + 5280)
    lnv = at("lnv", [P, T9, NH], EXTRA + 5792)
    adan = [at("adan0", [B + 1, 512], EXTRA + 6080), at("adan1", [B + 1, 512], XC)]
    assert ARENA + EXTRA + 6080 + 2048 <= 229344
    xb = at("xb", [P, T9, D], KV)
    c9 = at("c9", [B + 1, D], KV + 36864)
    c9e = at("c9e", [B + 1, D], KV + 40960)
    vecn = at("vecn", [HD, P], KV + 45056)
    pen = at("pen", [BLOCK, 2, 2, HD], KV + 45568)
    junk = at("junk", [P, D], KV + 46592)
    cpage = [at(f"cpage{i}", [P, PAGES, 256], WB + 4096 * i) for i in range(2)]
    wbd = [at(f"wbd{i}", [P, 2, 8, P], WB + o) for i, o in enumerate((8192, 16384, 28672, 36864))]
    kvcN = at("kvcN", [NBP + B * NBS, 2, P], WB + 26624)
    kvcT = at("kvcT", [P, 2, NBP + B * NBS], WB + 24576)
    vcS = at("vcS", [NBS, B, P], XC + 25088)
    qT = [at(f"qT{i}", [P, S], XC + 4096 * i) for i in range(2)]
    prob = [at(f"prob{i}", [P, S], XC + 8192 + 4096 * i) for i in range(2)]
    probT = [at(f"probT{i}", [P, NT, P], XC + 16384 + 4096 * i) for i in range(2)]
    mix = at("mix", [P, T9, D], WB)
    q2 = [at(f"q2_{i}", [P, S], WB + 36864 + 4096 * i, F32R) for i in range(2)]
    q3 = [at(f"q3_{i}", [P, S], WB + 45056 + 4096 * i, F32R) for i in range(2)]
    b2 = at("b2", [P, S], WB + 53248, F32R)
    braw = at("braw", [NH, S], WB + 57344)
    eyer = at("eyer", [P, P], WB + 62464, F32R)
    maskr = at("maskr", [P, 3 * P], WB + 62976, F32R)
    pick = [at(f"pick{i}", [P, P], WB + 61440 + 512 * i, F32R) for i in range(2)]
    fpage = [at(f"fpage{i}", [P, PAGES, D], KV + 16384 * i) for i in range(2)]
    npage = [at(f"npage{i}", [P, PAGES, 256], KV + 32768 + 4096 * i) for i in range(2)]
    wpage = [at(f"wpage{i}", [P, PAGES, 256], KV + 40960 + 4096 * i) for i in range(2)]
    o = KV + 49152
    lpage, fnew, nnew, wnew, qrow, lnew, vcb = [], [], [], [], [], [], []
    for i in range(2):
        fnew.append(at(f"fnew{i}", [TQ, D], o)); o += 4096
        qrow.append(at(f"qrow{i}", [TQ, D], o)); o += 4096
        nnew.append(at(f"nnew{i}", [TQ, 256], o)); o += 1024
        wnew.append(at(f"wnew{i}", [TQ, 256], o)); o += 1024
        lpage.append(at(f"lpage{i}", [P, PAGES, NH], o)); o += 128
        lnew.append(at(f"lnew{i}", [TQ, NH], o)); o += 32
        vcb.append(at(f"vcb{i}", [NBS, P], o)); o += 512
    assert o <= KV + 74112
    KTf = [at(f"KTf{i}", [P, 4, L], XC + 8320 * i) for i in range(2)]
    KTn = [at(f"KTn{i}", [P, 2, L], XC + 16640 + 4160 * i) for i in range(2)]
    o = WB + 36864
    sc, scc, negc, lf64, Qf, Qn, PTb, PTs, odiag, os2, srow = ([] for _ in range(11))
    for i in range(2):
        sc.append(at(f"sc{i}", [HD, 3, L], o)); o += 6240
        scc.append(at(f"scc{i}", [HD, NBS], o)); o += 32
        negc.append(at(f"negc{i}", [HD, L], o)); o += 2080
        lf64.append(at(f"lf64{i}", [P, PAGES + 1, NH, TQ], o)); o += 1280
        Qf.append(at(f"Qf{i}", [P, 320], o)); o += 1280
        Qn.append(at(f"Qn{i}", [P, HD], o)); o += 256
        PTb.append(at(f"PTb{i}", [P, 3, PAGES, HD], o)); o += 3072
        PTs.append(at(f"PTs{i}", [TQ, 4, HD], o)); o += 1024
        odiag.append(at(f"odiag{i}", [HD, NH, HD], o)); o += 2048
        os2.append(at(f"os2_{i}", [HD, 2, HD], o)); o += 512
        srow.append(at(f"srow{i}", [HD, 4, 4], o)); o += 64
    ones512 = at("ones512", [HD, PAST], o); o += 2048
    assert ARENA + o <= 229344, o
    TP = 3 * 364
    h2hi = at("h2hi", [P, KC, TP], KV, F32R)
    h2lo = at("h2lo", [P, KC, TP], KV + 34944, F32R)
    wo = at("wo", [P, KC, D], KV + 69888)
    gt1b = at("gt1b", [P, 2, D], KV + 69888 + 32768)
    gt1n = at("gt1n", [B + 1, D], KV + 69888 + 40960)
    h2s = [at("h2s0", [P, KC, P], KV + 69888 + 40960)]
    assert KV + 69888 + 45056 <= WB
    o = WB + 36864
    mixT = [at(f"mixT{i}", [P, KC, P], o + 4096 * i) for i in range(2)]; o += 8192
    xt = [at(f"xt{i}", [P, D], o + 4096 * i) for i in range(2)]; o += 8192
    x1 = [at(f"x1{i}", [P, D], o + 4096 * i) for i in range(2)]; o += 8192
    xn = [at(f"xn{i}", [P, D], o + 4096 * i) for i in range(2)]; o += 8192
    junk2 = at("junk2", [P, D], o); o += 4096
    h2s.append(at("h2s1", [P, KC, P], o)); o += 4096
    assert ARENA + o <= 229344
    UC = 4
    o = KV + 69888
    u2hi = at("u2hi", [P, UC, TP], o, F32R); o += UC * TP * 4
    u2lo = at("u2lo", [P, UC, TP], o, F32R); o += UC * TP * 4
    xo = [at(f"xo{i}", [P, D], o + 4096 * i) for i in range(3)]; o += 12288
    assert o == WB
    wraw = [at(f"wraw{i}", [P, D], o + 4096 * i) for i in range(2)]; o += 8192
    whi = [at(f"whi{i}", [P, D], o + 4096 * i, F32R) for i in range(2)]; o += 8192
    wlo = [at(f"wlo{i}", [P, D], o + 4096 * i, F32R) for i in range(2)]; o += 8192
    yT = at("yT", [P, KC, TP], o); o += KC * TP * 4
    us = [at(f"us{i}", [P, TP], o + 4384 * i) for i in range(2)]; o += 8768
    assert ARENA + o <= 229344

    bank = nc.alloc_psum_tensor("bank", [P, 8, 512], F32)
    bk = [bank[:, i, :] for i in range(8)]

    def banks(i, n):
        return bank[:, i:i + n, :].rearrange("p a b -> p (a b)")

    sem = nc.alloc_semaphore

    ident = cst[:, K_ID:K_ID + P]

    s_const, s_c, s_vec, s_gvec, s_pe, s_pt = (sem(n) for n in (
        "const_loaded", "c_loaded", "vec_loaded", "gvec_loaded", "pe_loaded", "ptab_loaded"))
    s_x = [sem(f"x_loaded{i}") for i in range(3)]
    w_ld = [sem(f"w_loaded{i}") for i in range(3)]
    c_neg, c_exp, c_silu, t0_ready, sc_ready = (sem(n) for n in (
        "c_negated", "c_exp_done", "c_silu_done", "small_transposed", "small_copied"))
    ln_sq, ln_var, ln_root, xn_done, ln_t, ln_ea, ln_ed = (sem(n) for n in (
        "ln_squares", "ln_variance", "ln_root", "xn_ready", "ln_transposed", "ln_copied_act", "ln_copied_dve"))
    ada_ready, ada_ev, mod_ready, mod_a, mod_d = (sem(n) for n in (
        "ada_ready", "ada_stored", "gain_ready", "h_act", "h_dve"))
    z_ready, z_ev, z_var, z_root, z_scaled, pool_done, tz_ready, tz_a, tz_d = (sem(n) for n in (
        "z_ready", "z_copied", "z_variance", "z_root", "z_scaled", "z_normed", "z_transposed",
        "zt_copied_act", "zt_copied_dve"))
    z_st = [sem(f"z_stored{i}") for i in range(5)]
    q_st = [sem(f"qt_stored{i}") for i in range(2)]
    misc_set, kv_set, g_arg, g_exp, g_one, g_ln, g_done = (sem(n) for n in (
        "misc_cleared", "kv_ones_set", "gate_args", "gate_exps", "gate_ones", "gate_logs", "gates_done"))
    ada_cp, ada_t, c_ready, c_neg2, ct_ready, ct_copied, key_hi = (sem(n) for n in (
        "ada_copied", "ada_transposed", "csum_ready", "csum_negated", "csum_transposed", "csum_copied", "key_hi"))
    misc_st, copy_st = sem("logf_stored"), sem("window_copied")
    dve_a, pool_a = sem("dve_step_a"), sem("pool_step_a")
    phase1_sems = [s_const, s_c, s_vec, s_gvec, s_pe, *s_x, *w_ld, c_neg, c_exp, c_silu, t0_ready, sc_ready, ln_sq, ln_var,
                   ln_root, xn_done, ln_t, ln_ea, ln_ed, ada_ready, ada_ev, mod_ready, mod_a, mod_d, z_ready, z_ev, z_var,
                   z_root, z_scaled, pool_done, tz_ready, tz_a, tz_d, *z_st, *q_st, misc_set, kv_set, g_arg, g_exp, g_one,
                   g_ln, g_done, ada_cp, ada_t, c_ready, c_neg2, ct_ready, ct_copied, key_hi, misc_st, copy_st, dve_a, pool_a]

    cp_ld = [sem(f"cpage_loaded{i}") for i in range(2)]
    wc_ld = [sem(f"wcmp_loaded{i}") for i in range(4)]
    wc_set, cb_ready, xc_ev, wc_used, kvc_done, vt_ready, vc_done, vcp_set = (sem(n) for n in (
        "wcmp_cleared", "cpage_transposed", "cinput_stored", "wcmp_used", "kvc_copied",
        "vc_transposed", "vc_copied", "vcp_ones_set"))
    bias_ld, b_step = sem("bias_rows_loaded"), sem("bias_step")
    wcmp_v = w_cmp.rearrange("a k (p d) e -> (a k) d p e", d=HD)
    CW = 8
    NCW = BLOCK // CW

    def load_w(sp, c):
        for kv in range(2):
            for i in range(2):
                sp.dma_start(wbd[c % 4][HD * i:HD * (i + 1), kv, :, HD * i:HD * (i + 1)],
                             wcmp_v[kv, :, CW * c:CW * (c + 1), :]).then_inc(wc_ld[c % 4], 16)

    def load_pages(sp, b, s):
        for j in range(PAGES):
            page = sp.value_load(ptab[0:1, bass.ds(b * PAGES + j, 1)], min_val=0, max_val=n_pool - 1)
            sp.dma_start(cpage[s][:, j, :], cnsa_v[page, :, 0:256]).then_inc(cp_ld[s], 16)

    jobs = [(b, t) for b in range(len(ZB)) for t in range(T9)]
    NJ = len(jobs)
    LAG = 2
    tz_index, tz_eng = {}, []
    for J, (b, t) in enumerate(jobs):
        if t < NT and ZB[b] != "vf":
            tz_index[J] = len(tz_eng)
            tz_eng.append("a" if ZB[b] in ("qf", "qn") else "d")
    tz_order = [tz_eng[:i + 1].count(e) for i, e in enumerate(tz_eng)]
    k_order = {J: i for i, J in enumerate(J for J in tz_index if ZB[jobs[J][0]] in ("misc", "kf"))}
    q_index = {J: i for i, J in enumerate(J for J in tz_index if ZB[jobs[J][0]] in ("qf", "qn"))}
    normed = [J for J, (b, t) in enumerate(jobs) if ZB[b] != "vf"]
    n_index = {J: i for i, J in enumerate(normed)}
    pool_jobs = [J for J, (b, t) in enumerate(jobs) if not (ZB[b] == "vf" and t == NT)]
    pool_count = [sum(j <= J for j in pool_jobs) for J in range(NJ)]
    ada1 = 4
    ada_after = [4, 13, 22, 26, 31, 35, 40, 49]
    csum_after = 12
    loads01 = {0: [1, 1, 2, 1, 1], 1: [1, 1, 1, 1, 1]}

    def loaded(buf, item):
        return 16 * sum(loads01[buf][:item + 1])

    def z_stores(J):
        b, t = jobs[J]
        name, z, r = ZB[b], zsb[J % 5], rows(t)
        if name == "misc":
            if t == NT:
                return [(wins_v[q, PAST - TQ:PAST, :], z[q * TQ:(q + 1) * TQ, 0:256]) for q in range(B)]
            return [(winp_v[t - 4, :, :], z[:, 0:256])] if t >= 4 else []
        if name in ("kf", "vf"):
            i = int(name == "vf")
            return [(fkvs_v[:, i, :] if t == NT else fkvp_v[t, :, i, :], z[0:r, :])]
        if name in ("qf", "qn"):
            i = int(name == "qn")
            return [(qs_d[:, 512 * i:512 * (i + 1)], z[0:NS, :])] if t == NT else []
        return [(nkvs_v if t == NT else nkvp_v[t, :, :], z[0:r, :])]

    def stored(J):
        return 16 * sum(len(z_stores(j)) for j in range(J + 1) if j % 5 == J % 5)

    def keys_of(K, e, row, src):
        b, t = jobs[K]
        cols = slice(t * P, (t + 1) * P)
        if ZB[b] == "kf":
            return kTf[row:row + HD, :, cols].rearrange("p (j e) n -> p j e n", e=2)[:, :, e, :], src[HD * e:HD * (e + 1), :, :]
        dst, j = (kTw, 0) if ZB[b] == "misc" else (kTs, 2)
        return dst[row:row + HD, e, cols], src[HD * e:HD * (e + 1), j, :]

    def k_heads(name, z, r, w):
        if name == "cs":
            return z[0:r, :].rearrange("p (a k h d) -> p a k h d", a=2, k=2, h=G)[:, :, 0, :, 0:w]
        n = G if name == "misc" else NH
        return z[0:r, 0:n * HD].rearrange("p (h d) -> p h d", d=HD)[:, :, 0:w]

    with nc.Block() as block:

        @block.sync
        def _(sp):
            sp.dma_start(c9[0:1, :], c_prompt).then_inc(s_c, 16)
            sp.dma_start(c9[1:B + 1, :], c_sample).then_inc(s_c, 16)
            sp.dma_start(vecn[0:48, :], b_ada.rearrange("a (n p) -> (a n) p", p=P)).then_inc(s_vec, 16)
            sp.dma_start(vecn[48:56, :], norm1_g.rearrange("a (n p) -> (a n) p", p=P)).then_inc(s_vec, 16)
            sp.dma_start(vecn[56:64, :], norm2_g.rearrange("a (n p) -> (a n) p", p=P)).then_inc(s_vec, 16)
            sp.dma_start(cst[:, :], consts).then_inc(s_const, 16)
            sp.dma_start(xb[:, 0:4, :], xp_v[:, 0:4, :]).then_inc(s_x[0], 16)
            sp.dma_start(wbuf[0][:, :, :], wada_v[:, :, 0:512]).then_inc(w_ld[0], 16)
            sp.dma_start(xb[:, 4:8, :], xp_v[:, 4:8, :]).then_inc(s_x[1], 16)
            sp.dma_start(xb[0:NS, NT, :], xs_v).then_inc(s_x[2], 16)
            for i in range(2):
                sp.dma_start(pen[:, :, i, :], pe_cmp.rearrange("a k p d -> p (a k) d")).then_inc(s_pe, 16)
            sp.dma_start(wbuf[1][:, :, :], wada_v[:, :, 512:1024]).then_inc(w_ld[1], 16)
            for i, g in enumerate((g_q_fox, g_k_fox, g_q_nsa)):
                sp.dma_start(gvec[:, i, :], g[0, :].partition_broadcast(P)).then_inc(s_gvec, 16)
            sp.dma_start(gvec[:, 3:6, :], g_k_nsa[0, :, :].partition_broadcast(P)).then_inc(s_gvec, 16)
            sp.dma_start(bias32[:, 0:24], b_gate[0, :].partition_broadcast(P)).then_inc(s_gvec, 16)
            sp.dma_start(bias32[:, 24:32], b_forget[0, :].partition_broadcast(P)).then_inc(s_gvec, 16)
            sp.dma_start(ptab[:, :], page_table.rearrange("b (o j) -> o (b j)", o=1)).then_inc(s_pt, 16)
            for n in (2, 3):
                sp.wait_ge(ada_ready, n - 1)
                sp.dma_start(wbuf[n % 2][:, :, :], wada_v[:, :, 512 * n:512 * (n + 1)]).then_inc(w_ld[n % 2], 16)

            def load_z(b):
                if b == 0:
                    sp.wait_ge(ada_ready, 3)
                    sp.dma_start(wbuf[0][:, :, 0:N_MISC], win_v[:, :, C_WIN:C_WIN + N_MISC]).then_inc(w_ld[0], 16)
                    sp.dma_start(wbuf[0][:, :, N_MISC:N_MISC + 8], win_v[:, :, C_F:C_F + 8]).then_inc(w_ld[0], 16)
                    return
                if b == 1:
                    sp.wait_ge(ada_ready, 4)
                else:
                    sp.wait_ge(z_ready, T9 * (b - 1))
                c = ZC[ZB[b]]
                sp.dma_start(wbuf[b % 2][:, :, :], win_v[:, :, c:c + 512]).then_inc(w_ld[b % 2], 16)

            def load_ada(i):
                if i:
                    sp.wait_ge(ada_ready, ada1 + i)
                n = ada1 + i
                sp.dma_start(wbuf[2][:, :, :], wada_v[:, :, 512 * n:512 * (n + 1)]).then_inc(w_ld[2], 16)

            load_z(0)
            load_ada(0)
            for J in range(NJ + LAG):
                if J < NJ and jobs[J][1] == 0 and jobs[J][0] + 1 < len(ZB):
                    load_z(jobs[J][0] + 1)
                if J - 2 in ada_after and ada_after.index(J - 2) + 1 < len(ada_after):
                    load_ada(ada_after.index(J - 2) + 1)
                K = J - LAG
                if K < 0:
                    continue
                if z_stores(K):
                    if K in pool_jobs:
                        sp.wait_ge(pool_done, pool_count[K])
                    else:
                        sp.wait_ge(z_ev, K + 1)
                    for dst, src in z_stores(K):
                        sp.dma_start(dst, src).then_inc(z_st[K % 5], 16)
                if K in q_index:
                    i, t = q_index[K], jobs[K][1]
                    sp.wait_ge(tz_a, tz_order[tz_index[K]])
                    sp.dma_start(qt_d[i // NT, :, :, t * P:(t + 1) * P].rearrange("h d t -> d h t"),
                                 qst[i % 2][:, :, :]).then_inc(q_st[i % 2], 16)
                if K == csum_after + 3:
                    sp.wait_ge(g_done, 1)
                    sp.dma_start(flf_p.rearrange("a b (t p) h -> p (a b t) h", p=P), logf[:, 0:NT, :]).then_inc(misc_st, 16)
                    sp.dma_start(flf_s.rearrange("a b t h -> (a b t) h"), logf[0:NS, NT, :]).then_inc(misc_st, 16)
                    sp.dma_start(gs_d, gates[0:NS, NT, :]).then_inc(misc_st, 16)
                if K == 5 * T9:
                    sp.wait_ge(z_ready, 5 * T9)
                    sp.wait_ge(s_pt, 16)
                    for s in range(2):
                        load_pages(sp, s, s)
                    sp.wait_ge(wc_set, 1)
                    load_w(sp, 0)
                if K == 20:
                    sp.dma_start(wins_v[:, 0:PAST - TQ, :], stw_rows[:, TQ:PAST, :]).then_inc(copy_st, 16)
            for i in range(5):
                last = max(J for J in range(NJ) if J % 5 == i)
                sp.wait_ge(z_st[i], stored(last))
            for i in range(2):
                sp.wait_ge(q_st[i], 16 * NT)
            sp.wait_ge(misc_st, 48)
            sp.wait_ge(copy_st, 16)

        @block.gpsimd
        def _(pool):
            ch = Chain(pool, pool_a)
            nc.gpsimd.memset(graw[:, :, :], 0.0).then_inc(misc_set, 1)
            pool.wait_ge(ln_t, 2 * T9)
            pool.wait_ge(sc_ready, 1)
            ch.link(nc.gpsimd.memset(Vf[:, :, :, HD:HD + 1], 1.0))
            ch.link(nc.gpsimd.memset(Vs[:, :, :, HD:HD + 1], 1.0))
            nc.gpsimd.memset(Vw[:, :, :, HD:HD + 1], 1.0).then_inc(kv_set, 1)
            pool.wait_ge(s_gvec, 96)
            ch.link(nc.gpsimd.tensor_scalar(gvec[:, 0, :], gvec[:, 0, :], SCALE, None, ALU.mult))
            ch.link(nc.gpsimd.tensor_scalar(gvec[:, 2, :], gvec[:, 2, :], SCALE, None, ALU.mult))
            for J in pool_jobs:
                if J == 5 * T9:
                    pool.wait_ge(z_ready, 5 * T9)
                    nc.gpsimd.memset(wbd[0][:, :, :, :], 0.0).then_inc(wc_set, 1)
                b, t = jobs[J]
                name, z, r = ZB[b], zsb[J % 5], rows(t)
                if name == "vf":
                    pool.wait_ge(z_ev, J + 1)
                    nc.gpsimd.tensor_copy(Vf[:, t, :, 0:HD], z[:, :].rearrange("p (h d) -> p h d", d=HD)).then_inc(pool_done, 1)
                    continue
                pool.wait_ge(z_scaled, n_index[J] + 1)
                x = k_heads(name, z, r, HD)
                if name == "cs":
                    g = gvec[0:r, 3:5, :].unsqueeze(2).to_broadcast([r, 2, G, HD])
                else:
                    i = {"misc": 5, "kf": 1, "qf": 0, "qn": 2}[name]
                    g = gvec[0:r, i:i + 1, :].to_broadcast([r, G if name == "misc" else NH, HD])
                ins = nc.gpsimd.tensor_tensor(x, x, g, ALU.mult)
                if name in ("kf", "qf"):
                    ins.then_inc(pool_done, 1)
                    continue
                ch.link(ins)
                x = k_heads(name, z, r, 16)
                n = NH if name == "qn" else G
                if name == "cs":
                    a = rope[0][0:r, 0:4, :].rearrange("p (a h) d -> p a h d", a=2)
                    c = rope[1][0:r, 0:4, :].rearrange("p (a h) d -> p a h d", a=2)
                    lo, hi = c[:, :, :, 0:8], c[:, :, :, 8:16]
                    x_lo, x_hi = x[:, :, :, 0:8], x[:, :, :, 8:16]
                else:
                    a, c = rope[0][0:r, 0:n, :], rope[1][0:r, 0:n, :]
                    lo, hi = c[:, :, 0:8], c[:, :, 8:16]
                    x_lo, x_hi = x[:, :, 0:8], x[:, :, 8:16]

                def table(col, w):
                    v = cst[0:r, col + 16 * t:col + 16 * t + w].unsqueeze(1)
                    return v.unsqueeze(1).to_broadcast([r, 2, G, w]) if name == "cs" else v.to_broadcast([r, n, w])

                ch.link(nc.gpsimd.tensor_tensor(a, x, table(K_COS, 16), ALU.mult))
                ch.link(nc.gpsimd.tensor_tensor(lo, x_hi, table(K_SIN, 8), ALU.mult))
                ch.link(nc.gpsimd.tensor_tensor(hi, x_lo, table(K_SIN + 8, 8), ALU.mult))
                last = nc.gpsimd.tensor_tensor(x, a, c, ALU.add)
                if t < NT and name == "misc":
                    last = nc.gpsimd.tensor_copy(Vw[:, t, :, 0:HD], z[:, 128:256].rearrange("p (h d) -> p h d", d=HD))
                if t < NT and name == "cs":
                    last = nc.gpsimd.tensor_copy(Vs[:, t, :, 0:HD], z[:, 384:512].rearrange("p (h d) -> p h d", d=HD))
                last.then_inc(pool_done, 1)

        @block.scalar
        def _(act):
            act.wait_ge(c_neg, 1)
            nc.scalar.activation(c9e[:, :], c9e[:, :], ACT.Exp).then_inc(c_exp, 1)
            for g, (lo, hi) in enumerate(((0, 4), (4, 8), (8, 9))):
                act.wait_ge(s_x[g], 16)
                for t in range(lo, hi):
                    if t:
                        act.wait_ge(ln_sq, t)
                    nc.scalar.activation(junk[0:rows(t), :], xb[0:rows(t), t, :], ACT.Square,
                                         accum_out=ssum[0:rows(t), t:t + 1]).then_inc(ln_sq, 1)
                act.wait_ge(ln_var, g + 1)
                r = rows(lo)
                nc.scalar.activation(rstd[0:r, lo:hi], ssum[0:r, lo:hi], ACT.Sqrt).then_inc(ln_root, 1)
            for t in range(T9):
                act.wait_ge(ln_t, 2 * t + 1)
                r = rows(t)
                nc.scalar.activation(hT[:, 0:4, t * P:t * P + r],
                                     bk[2 * (t % 3)].rearrange("p (k n) -> p k n", k=4)[:, :, 0:r], ACT.Copy).then_inc(ln_ea, 1)
            act.wait_ge(mod_ready, 1)
            act.wait_ge(ln_ea, T9)
            for k in range(4):
                nc.scalar.activation(hT[:, k, 0:S], hT[:, k, 0:S], ACT.Identity, bias=modT[:, k, 0:1],
                                     scale=gain1[:, k, 0:1]).then_inc(mod_a, 1)

            def copy_t(K):
                b, t = jobs[K]
                i = tz_index[K]
                act.wait_ge(tz_ready, i + 1)
                src = bk[3 + i % 3].rearrange("p (j n) -> p j n", n=P)
                if K in k_order:
                    for e in range(2):
                        dst, x = keys_of(K, e, HD * e, src)
                        last = nc.scalar.activation(dst, x, ACT.Copy)
                    last.then_inc(key_hi, 1)
                    return
                q = q_index[K]
                if q >= 2:
                    act.wait_ge(q_st[q % 2], 16 * (q // 2))
                dst = qst[q % 2][:, :, :].rearrange("p (j e) n -> p j e n", e=2)
                nc.scalar.activation(dst[:, :, 0, :], src[0:HD, :, :], ACT.Copy)
                nc.scalar.activation(dst[:, :, 1, :], src[HD:P, :, :], ACT.Copy).then_inc(tz_a, 1)

            for J in range(NJ + LAG):
                if J < NJ:
                    b, t = jobs[J]
                    name, r, w = ZB[b], rows(t), ZW[ZB[b]]
                    act.wait_ge(z_ready, J + 1)
                    if J >= 5:
                        act.wait_ge(pool_done, pool_count[J - 5])
                        if J - 5 in tz_index:
                            act.wait_ge(tz_ready, tz_index[J - 5] + 1)
                        if stored(J - 5):
                            act.wait_ge(z_st[J % 5], stored(J - 5))
                    ins = nc.scalar.activation(zsb[J % 5][0:r, 0:w], bk[J % 3][0:r, 0:w], ACT.Copy)
                    if name != "vf":
                        before = sum(j <= J - 2 for j in normed)
                        if before:
                            act.wait_ge(z_var, before)
                        n = 128 if name == "misc" else 512
                        ins = nc.scalar.activation(sq[J % 2][0:r, 0:n], bk[J % 3][0:r, 0:n], ACT.Square)
                    ins.then_inc(z_ev, 1)
                    if name != "vf":
                        act.wait_ge(z_var, n_index[J] + 1)
                        h = hv[J % 3]
                        nc.scalar.activation(h[0:r, 1, :], h[0:r, 0, :], ACT.Sqrt).then_inc(z_root, 1)
                    if J == NT:
                        act.wait_ge(g_arg, 1)
                        nc.scalar.activation(gexp[:, :, :], gexp[:, :, :], ACT.Exp).then_inc(g_exp, 1)
                        act.wait_ge(g_one, 1)
                        nc.scalar.activation(lnv[:, :, :], gexp[:, :, 24:32], ACT.Ln).then_inc(g_ln, 1)
                K = J - LAG
                if K in q_index or K in k_order:
                    copy_t(K)

        @block.vector
        def _(dve):
            ch = Chain(dve, dve_a)
            nc.vector.nop().then_inc(ada_ev, CREDIT)
            dve.wait_ge(s_c, 32)
            nc.vector.tensor_scalar(c9e[:, :], c9[:, :], -1.0, EXP_MAX, ALU.mult, ALU.min).then_inc(c_neg, 1)
            dve.wait_ge(c_exp, 1)
            ch.link(nc.vector.tensor_scalar(c9e[:, :], c9e[:, :], 1.0, None, ALU.add))
            ch.link(nc.vector.reciprocal(c9e[:, :], c9e[:, :]))
            nc.vector.tensor_tensor(c9e[:, :], c9[:, :], c9e[:, :], ALU.mult).then_inc(c_silu, 1)
            for g, (lo, hi) in enumerate(((0, 4), (4, 8), (8, 9))):
                r = rows(lo)
                dve.wait_ge(ln_sq, hi)
                nc.vector.tensor_scalar(ssum[0:r, lo:hi], ssum[0:r, lo:hi], 1.0 / D, EPS, ALU.mult, ALU.add).then_inc(ln_var, 1)
                dve.wait_ge(ln_root, g + 1)
                ch.link(nc.vector.reciprocal(rstd[0:r, lo:hi], rstd[0:r, lo:hi]))
                for t in range(lo, hi):
                    nc.vector.tensor_scalar(xb[0:r, t, :], xb[0:r, t, :], rstd[0:r, t:t + 1], None, ALU.mult).then_inc(xn_done, 1)
                if g == 0:
                    dve.wait_ge(t0_ready, 1)
                    nc.vector.tensor_copy(scT[:, :, :], bk[7][:, 0:72].rearrange("p (k n) -> p k n", k=KC))
                    nc.vector.tensor_copy(vecT[:, :], bk[7][:, 128:192])
                    nc.vector.tensor_copy(peT[:, :, :], bk[7][:, 256:384].rearrange("p (k n) -> p k n", k=2)).then_inc(sc_ready, 1)
            for t in range(T9):
                dve.wait_ge(ln_t, 2 * t + 2)
                r = rows(t)
                nc.vector.tensor_copy(hT[:, 4:8, t * P:t * P + r],
                                      bk[2 * (t % 3) + 1].rearrange("p (k n) -> p k n", k=4)[:, :, 0:r]).then_inc(ln_ed, 1)
            dve.wait_ge(sc_ready, 1)

            def store_ada(n, src):
                out, bias = modT[:, bass.ds(4 * n, 4), :], vecT[:, bass.ds(4 * n, 4)]
                nc.vector.tensor_tensor(out, src[:, 0:36].rearrange("p (k n) -> p k n", k=4),
                                        bias.unsqueeze(2).to_broadcast([P, 4, B + 1]), ALU.add).then_inc(ada_ev, 1)

            with dve.Fori(0, ada1 // 2) as it:
                for s in range(2):
                    dve.wait_ge(ada_ready, 2 * it + s + 1)
                    nc.vector.tensor_copy(adan[s][:, :], bk[6 + s][0:B + 1, :]).then_inc(ada_cp, 1)
                for s in range(2):
                    dve.wait_ge(ada_t, 2 * it + s + 1)
                    store_ada(2 * it + s, bk[6 + s])
            dve.wait_ge(ada_ev, CREDIT + ada1)
            nc.vector.scalar_tensor_tensor(gain1[:, :, :], modT[:, 8:16, :], 1.0,
                                           vecT[:, 48:56].unsqueeze(2).to_broadcast([P, KC, B + 1]),
                                           ALU.add, ALU.mult).then_inc(mod_ready, 1)
            dve.wait_ge(mod_ready, 1)
            dve.wait_ge(ln_ed, T9)
            for k in range(4, 8):
                nc.vector.tensor_scalar(hT[:, k, 0:S], hT[:, k, 0:S], gain1[:, k, 0:1], modT[:, k, 0:1],
                                        ALU.mult, ALU.add).then_inc(mod_d, 1)
            dve.wait_ge(ln_ea, T9)
            hs = hT[:, :, S:TOK].rearrange("p k (b t) -> p k b t", b=B)
            ch.link(nc.vector.tensor_tensor(hs, hs, gain1[:, :, 1:B + 1].unsqueeze(3).to_broadcast([P, KC, B, TQ]), ALU.mult))
            nc.vector.tensor_tensor(hs, hs, modT[:, 0:KC, 1:B + 1].unsqueeze(3).to_broadcast([P, KC, B, TQ]), ALU.add).then_inc(mod_d, 1)
            dve.wait_ge(misc_set, 1)
            dve.wait_ge(s_gvec, 96)

            def copy_t(K):
                t, i = jobs[K][1], tz_index[K]
                if K in k_order:
                    dve.wait_ge(key_hi, k_order[K] + 1)
                else:
                    dve.wait_ge(tz_ready, i + 1)
                tile = bk[3 + i % 3]
                src = tile.rearrange("p (j n) -> p j n", n=P)
                if K not in k_order:
                    for kv in range(2):
                        nc.vector.tensor_tensor(Xc[:, 2 * t:2 * t + 2, kv, :],
                                                tile[:, P * kv:P * (kv + 1)].rearrange("p (n d) -> p n d", n=2),
                                                peT[:, kv:kv + 1, :].to_broadcast([P, 2, BLOCK]), ALU.add)
                    for e in range(2):
                        hi, x = keys_of(K, e, HD * e, src)
                        ins = nc.vector.tensor_copy(hi, x)
                    ch.link(ins)
                for e in range(2):
                    hi, x = keys_of(K, e, HD * e, src)
                    lo, _ = keys_of(K, e, HD * (1 - e), src)
                    ins = nc.vector.tensor_tensor(lo, x, hi.bitcast(F32), ALU.subtract)
                ins.then_inc(tz_d, 1)

            for J in range(NJ + LAG):
                if J < NJ:
                    b, t = jobs[J]
                    name, z, r, h = ZB[b], zsb[J % 5], rows(t), hv[J % 3]
                    if name != "vf":
                        n = G if name == "misc" else NH
                        dve.wait_ge(z_ev, J + 1)
                        ch.link(nc.vector.tensor_reduce(h[0:r, 0, 0:n], sq[J % 2][0:r, 0:n * HD].rearrange("p (h d) -> p h d", d=HD),
                                                        AX.X, ALU.add))
                        if name == "misc":
                            ch.link(nc.vector.memset(h[0:r, 0, n:NH], 1.0))
                        nc.vector.tensor_scalar(h[0:r, 0, :], h[0:r, 0, :], 1.0 / HD, EPS, ALU.mult, ALU.add).then_inc(z_var, 1)
                        if name == "misc":
                            nc.vector.tensor_tensor(graw[0:r, t, :], z[0:r, 256:288], bias32[0:r, :], ALU.add)
                        dve.wait_ge(z_root, n_index[J] + 1)
                        ch.link(nc.vector.reciprocal(h[0:r, 2, :], h[0:r, 1, :]))
                        x = k_heads(name, z, r, HD)
                        if name == "cs":
                            s = h[0:r, 2, :].rearrange("p (a k h) -> p a k h", a=2, k=2)[:, :, 0, :].unsqueeze(3).to_broadcast([r, 2, G, HD])
                        else:
                            s = h[0:r, 2, 0:n].unsqueeze(2).to_broadcast([r, n, HD])
                        nc.vector.tensor_tensor(x, x, s, ALU.mult).then_inc(z_scaled, 1)
                    if J == NT:
                        dve.wait_ge(z_scaled, n_index[J] + 1)
                        ch.link(nc.vector.tensor_scalar(gexp[:, :, 0:24], graw[:, :, 0:24], -1.0, EXP_MAX, ALU.mult, ALU.min))
                        ch.link(nc.vector.tensor_scalar(gexp[:, :, 24:32], graw[:, :, 24:32], -1.0, None, ALU.mult))
                        nc.vector.tensor_tensor(gexp[:, :, 24:32], gexp[:, :, 24:32], graw[:, :, 24:32], ALU.min).then_inc(g_arg, 1)
                        dve.wait_ge(g_exp, 1)
                        nc.vector.tensor_scalar(gexp[:, :, :], gexp[:, :, :], 1.0, None, ALU.add).then_inc(g_one, 1)
                        dve.wait_ge(g_one, 1)
                        ch.link(nc.vector.reciprocal(gates[:, :, :], gexp[:, :, 0:24]))
                        ch.link(nc.vector.tensor_scalar(gates[:, 0, 0:NH], gates[:, 0, 0:NH], cst[:, K_ANY:K_ANY + 1], None, ALU.mult))
                        dve.wait_ge(g_ln, 1)
                        nc.vector.scalar_tensor_tensor(logf[:, :, :], graw[:, :, 24:32], 0.0, lnv[:, :, :],
                                                       ALU.min, ALU.subtract).then_inc(g_done, 1)
                    if J in ada_after:
                        i = ada_after.index(J)
                        dve.wait_ge(ada_ready, ada1 + i + 1)
                        nc.vector.tensor_copy(adan[0][:, :], bk[6][0:B + 1, :]).then_inc(ada_cp, 1)
                    if J - 1 in ada_after:
                        i = ada_after.index(J - 1)
                        dve.wait_ge(ada_t, ada1 + i + 1)
                        store_ada(ada1 + i, bk[6])
                    if J == csum_after:
                        dve.wait_ge(c_ready, 1)
                        tot = bk[7][:, 64:128].rearrange("p (t h) -> p t h", h=NH)
                        ch.link(nc.vector.memset(cpre[:, 0, :], 0.0))
                        for t2 in range(1, NT):
                            ch.link(nc.vector.tensor_tensor(cpre[:, t2, :], cpre[:, t2 - 1, :], tot[:, t2 - 1, :], ALU.add))
                        nc.vector.scalar_tensor_tensor(csum[:, :, :], bk[7][:, 0:64].rearrange("p (t h) -> p t h", h=NH), -1.0,
                                                       cpre[:, :, :], ALU.mult, ALU.subtract).then_inc(c_neg2, 1)
                    if J == csum_after + 2:
                        dve.wait_ge(ct_ready, 1)
                        nc.vector.tensor_copy(nCT[:, :], bk[7][0:HD, 128:256]).then_inc(ct_copied, 1)
                K = J - LAG
                if K in tz_index and tz_eng[tz_index[K]] == "d":
                    copy_t(K)

        @block.tensor
        def _(pe):
            pe.wait_ge(s_const, 16)
            pe.wait_ge(s_vec, 48)
            pe.wait_ge(c_silu, 1)
            pe.wait_ge(s_pe, 32)
            for k in range(KC):
                nc.tensor.transpose(bk[7][:, 9 * k:9 * k + 9], c9e[:, k * P:(k + 1) * P], ident[0:B + 1, 0:B + 1])
            nc.tensor.transpose(bk[7][:, 128:192], vecn[:, :], ident[0:HD, 0:HD])
            for kv in range(2):
                last = nc.tensor.transpose(bk[7][:, 256 + 64 * kv:320 + 64 * kv],
                                           pen[:, kv, :, :].rearrange("p a d -> p (a d)"), ident[0:HD, 0:HD])
            last.then_inc(t0_ready, 1)
            for t in range(T9):
                r = rows(t)
                pe.wait_ge(xn_done, t + 1)
                if t >= 3:
                    pe.wait_ge(ln_ea, t - 2)
                    pe.wait_ge(ln_ed, t - 2)
                for k in range(KC):
                    dst = bk[2 * (t % 3) + k // 4][:, P * (k % 4):P * (k % 4) + r]
                    ins = nc.tensor.transpose(dst, xb[0:r, t, k * P:(k + 1) * P], ident[0:r, 0:r])
                    if k % 4 == 3:
                        ins.then_inc(ln_t, 1)
            pe.wait_ge(sc_ready, 1)

            def ada(buf, dst):
                for k in range(KC):
                    last = nc.tensor.matmul(dst[0:B + 1, :], scT[:, k, :], buf[:, k, :], start=(k == 0), stop=(k == KC - 1))
                last.then_inc(ada_ready, 1)

            def ada_flip(src, dst, after_register_wait):
                for j in range(4):
                    out, x, eye = dst[:, 9 * j:9 * j + 9], src[:, j * P:(j + 1) * P], ident[0:B + 1, 0:B + 1]
                    if j == 0 and after_register_wait:
                        nc.tensor.matmul(out, x, eye, start=True, stop=True)
                    else:
                        last = nc.tensor.transpose(out, x, eye)
                last.then_inc(ada_t, 1)

            with pe.Fori(0, ada1 // 2) as it:
                pe.wait_ge(ada_ev, 2 * it + CREDIT)
                for s in range(2):
                    pe.wait_ge(w_ld[s], 16 * it + 16)
                    ada(wbuf[s], bk[6 + s])
                for s in range(2):
                    pe.wait_ge(ada_cp, 2 * it + (s + 1))
                    ada_flip(adan[s], bk[6 + s], True)
            pe.wait_ge(mod_a, 4)
            pe.wait_ge(mod_d, 5)
            for J in range(NJ + LAG):
                if J < NJ:
                    b, t = jobs[J]
                    r, w = rows(t), ZW[ZB[b]]
                    if t == 0:
                        pe.wait_ge(w_ld[b % 2], loaded(b % 2, 2 + b // 2))
                    if J >= 3:
                        pe.wait_ge(z_ev, J - 2)
                    for k in range(KC):
                        last = nc.tensor.matmul(bk[J % 3][0:r, 0:w], hT[:, k, t * P:t * P + r], wbuf[b % 2][:, k, 0:w],
                                                start=(k == 0), stop=(k == KC - 1))
                    last.then_inc(z_ready, 1)
                K = J - LAG
                if K in tz_index:
                    i = tz_index[K]
                    pe.wait_ge(pool_done, pool_count[K])
                    if i >= 3:
                        pe.wait_ge(tz_a if tz_eng[i - 3] == "a" else tz_d, tz_order[i - 3])
                    n = {"misc": 1, "cs": 3}.get(ZB[jobs[K][0]], 4)
                    for j in range(n):
                        last = nc.tensor.transpose(bk[3 + i % 3][:, j * P:(j + 1) * P], zsb[K % 5][:, j * P:(j + 1) * P], ident)
                    last.then_inc(tz_ready, 1)
                if J == csum_after:
                    pe.wait_ge(g_done, 1)
                    lf = logf[:, 0:NT, :].rearrange("p t h -> p (t h)")
                    nc.tensor.matmul(bk[7][:, 0:64], cst[:, K_U:K_U + P], lf, start=True, stop=True)
                    nc.tensor.matmul(bk[7][:, 64:128], cst[:, K_ONE:K_ONE + P], lf, start=True, stop=True).then_inc(c_ready, 1)
                if J == csum_after + 2:
                    pe.wait_ge(c_neg2, 1)
                    nc.tensor.transpose(bk[7][0:HD, 128:256], csum[:, :, :].rearrange("p t h -> p (t h)"), ident).then_inc(ct_ready, 1)
                if J in ada_after:
                    i = ada_after.index(J)
                    pe.wait_ge(w_ld[2], 16 * (i + 1))
                    pe.wait_ge(ada_ev, CREDIT + ada1 + i)
                    ada(wbuf[2], bk[6])
                if J - 1 in ada_after:
                    pe.wait_ge(ada_cp, ada1 + ada_after.index(J - 1) + 1)
                    ada_flip(adan[0], bk[6], False)

    cn_copied, cn_flipped = sem("compressed_copied"), sem("compressed_flipped")

    with nc.Block() as block:

        @block.sync
        def _(sp):
            with sp.Fori(0, B // 2 - 1) as it:
                for s in range(2):
                    sp.wait_ge(cb_ready, 2 * it + s + 1)
                    load_pages(sp, 2 * it + s + 2, s)
            for c in range(1, 4):
                sp.wait_ge(wc_set, c + 1)
                load_w(sp, c)
            for t in range(NT):
                sp.dma_start(braw[:, t * P:(t + 1) * P], nCT[t * NH:(t + 1) * NH, :]).then_inc(bias_ld, 16)
            for c in range(4, NCW):
                sp.wait_ge(wc_used, c - 3)
                load_w(sp, c)

        @block.gpsimd
        def _(pool):
            for i in range(1, 4):
                nc.gpsimd.memset(wbd[i][:, :, :, :], 0.0).then_inc(wc_set, 1)
            nc.gpsimd.memset(vcP[:, :, :], 0.0).then_inc(vcp_set, 1)
            ch = Chain(pool, b_step)
            ch.link(nc.gpsimd.memset(b2[:, :].bitcast(F32), 0.0))
            nc.gpsimd.tensor_copy(eyer[:, :], ident)
            nc.gpsimd.tensor_copy(maskr[:, :], cst[:, K_CAUS:K_CAUS + 3 * P])
            pool.wait_ge(bias_ld, 16 * NT)
            ch.link(nc.gpsimd.tensor_copy(b2[0:NH, :], braw[:, :]))
            ch.link(nc.gpsimd.tensor_tensor(b2[32:32 + NH, :], braw[:, :], b2[0:NH, :].bitcast(F32), ALU.subtract))

        @block.vector
        def _(dve):
            nc.vector.nop().then_inc(xc_ev, CREDIT)
            with dve.Fori(0, B // 2) as it:
                for s in range(2):
                    dve.wait_ge(cb_ready, 2 * it + s + 1)
                    for kv in range(2):
                        ins = nc.vector.tensor_tensor(
                            Xc[:, bass.ds(it * (2 * NBS) + (NBP + NBS * s), NBS), kv, :],
                            bk[2 * s + kv].rearrange("p (n d) -> p n d", d=BLOCK),
                            peT[:, kv:kv + 1, :].to_broadcast([P, NBS, BLOCK]), ALU.add)
                    ins.then_inc(xc_ev, 1)
            dve.wait_ge(kvc_done, 2)
            for g in range(G):
                nc.vector.tensor_tensor(kcP[HD * (1 - g):HD * (2 - g), g, :], bk[2][HD * g:HD * (g + 1), 0:NBP],
                                        kcP[HD * g:HD * (g + 1), g, :].bitcast(F32), ALU.subtract)
            dve.wait_ge(vcp_set, 1)
            dve.wait_ge(vt_ready, 1)
            nc.vector.memset(vcP[0:NBP, :, HD:HD + 1], 1.0)
            nc.vector.tensor_copy(vcP[0:NBP, :, 0:HD], bk[6][0:NBP, 0:P].rearrange("p (g d) -> p g d", g=G))
            nc.vector.tensor_copy(vcS[:, 0:4, :], bk[7][0:NBS, :].rearrange("p (b d) -> p b d", b=4))
            nc.vector.tensor_copy(vcS[:, 4:8, :], bk[0][0:NBS, :].rearrange("p (b d) -> p b d", b=4)).then_inc(vc_done, 1)

        @block.scalar
        def _(act):
            act.wait_ge(wc_used, NCW)
            nc.scalar.activation(kvcN[:, :, :], bank[0:NBP + B * NBS, 4:6, 0:P], ACT.Copy).then_inc(cn_copied, 1)
            act.wait_ge(cn_flipped, 1)
            nc.scalar.activation(kvcT[:, 1, :], bk[3][:, 0:NBP + B * NBS], ACT.Copy).then_inc(kvc_done, 1)
            nc.scalar.activation(kcS[:, :], bk[2][:, NBP:NBP + B * NBS], ACT.Copy)
            nc.scalar.activation(kcP[0:HD, 0, :], bk[2][0:HD, 0:NBP], ACT.Copy)
            nc.scalar.activation(kcP[HD:P, 1, :], bk[2][HD:P, 0:NBP], ACT.Copy).then_inc(kvc_done, 1)

        @block.tensor
        def _(pe):
            with pe.Fori(0, B // 2) as it:
                pe.wait_ge(xc_ev, 2 * it + CREDIT)
                for s in range(2):
                    pe.wait_ge(cp_ld[s], it * (16 * PAGES) + 16 * PAGES)
                    for kv in range(2):
                        for j in range(PAGES):
                            last = nc.tensor.transpose(bk[2 * s + kv][:, j * P:(j + 1) * P], cpage[s][:, j, P * kv:P * (kv + 1)], ident)
                    last.then_inc(cb_ready, 1)
            pe.wait_ge(xc_ev, B + CREDIT)
            for c in range(NCW):
                pe.wait_ge(wc_ld[c % 4], 64 * (c // 4 + 1))
                for p in range(CW):
                    for kv in range(2):
                        last = nc.tensor.matmul(bk[4 + kv][0:NBP + B * NBS, 0:P], Xc[:, :, kv, CW * c + p], wbd[c % 4][:, kv, p, :],
                                                start=(c == 0 and p == 0), stop=(c == NCW - 1 and p == CW - 1))
                last.then_inc(wc_used, 1)
            pe.wait_ge(cn_copied, 1)
            for kv in range(2):
                last = nc.tensor.transpose(bk[2 + kv][:, 0:NBP + B * NBS], kvcN[:, kv, :], ident[0:NBP + B * NBS, 0:NBP + B * NBS])
            last.then_inc(cn_flipped, 1)
            pe.wait_ge(kvc_done, 1)
            nc.tensor.transpose(bk[6][0:NBP, 0:P], kvcT[:, 1, 0:NBP], ident)
            for b in range(B):
                last = nc.tensor.transpose((bk[7] if b < 4 else bk[0])[0:NBS, P * (b % 4):P * (b % 4 + 1)],
                                           kvcT[:, 1, NBP + NBS * b:NBP + NBS * (b + 1)], ident)
            last.then_inc(vt_ready, 1)

    probt_clear = sem("probt_cleared")

    def prompt_attention(tag, source, kinds):
        q_ld = [sem(f"{tag}_q_loaded{i}") for i in range(2)]
        scores_ready, max_ready, prob_ready, pt_ready, pt_act, pt_dve, o_ready, o_norm = (sem(f"{tag}_{n}") for n in (
            "scores_ready", "max_ready", "prob_ready", "pt_ready", "pt_copied_act", "pt_copied_dve", "o_ready", "o_stored"))
        dve_s = sem(f"{tag}_dve_step")
        fox = kinds == ("fox",)
        units = [(s, u) for s in range(2) for u in attention_units(kinds)]
        n = len(units)
        nk = [u[3] for _, u in units]
        halves = [(k + 3) // 4 for k in nk]
        h0 = [sum(halves[:i]) for i in range(n + 1)]
        d0 = [sum(h == 2 for h in halves[:i]) for i in range(n + 1)]
        owner = [(i, j) for i in range(n) for j in range(halves[i])]
        steps = n * (1 if fox else 2)
        TURNS = NH // 2
        split_step, q_split = sem(f"{tag}_pool_step"), sem(f"{tag}_parts_ready")
        first_hi, first_lo = sem(f"{tag}_first_hi"), sem(f"{tag}_first_lo")

        with nc.Block() as block:

            @block.sync
            def _(sp):
                def load(h, s):
                    for i in range(2):
                        sp.dma_start(qT[s][HD * i:HD * (i + 1), :], qt_d[source, h, :, :]).then_inc(q_ld[s], 16)

                for s in range(2):
                    load(s, s)
                with sp.Fori(0, TURNS - 1) as it:
                    for s in range(2):
                        sp.wait_ge(q_split, it * 2 + (s + 1))
                        load(2 * it + (s + 2), s)
                if not fox:
                    with nc.allow_non_contiguous_dma(reason="gates of 64 tokens, once"):
                        for h in range(NH):
                            for r in range(3):
                                sp.dma_start(gateS[h * TQ:(h + 1) * TQ, r, :],
                                             gs_d.rearrange("(b q) (r h) -> h r q b", q=TQ, h=NH)[h, r, :, :]).then_inc(g_ld, 16)
                if not fox:
                    for part, done in enumerate((in_ld, v_ld)):
                        for s in range(2):
                            load_pages_of(sp, s, s, part, done[s])

            @block.gpsimd
            def _(pool):
                ch = Chain(pool, split_step)
                if fox:
                    nc.gpsimd.memset(probT[0][:, 0, :], 0.0)
                    nc.gpsimd.memset(probT[1][:, 0, :], 0.0).then_inc(probt_clear, 1)
                    pool.wait_ge(probt_clear, 1)

                if fox:
                    ch.link(nc.gpsimd.tensor_copy(pick[0][:, :], cst[:, K_SELH:K_SELH + 1].to_broadcast([P, P])))
                pool.wait_ge(first_lo, 1)
                nc.gpsimd.nop().then_inc(q_split, 1)
                for h in range(1, NH):
                    s = h % 2
                    pool.wait_ge(q_ld[s], 32 * (h // 2 + 1))
                    if h >= 2:
                        pool.wait_ge(scores_ready, (h - 1) * (n // 2))
                    if fox:
                        nc.gpsimd.tensor_copy(pick[s][:, :], cst[:, K_SELH + h:K_SELH + h + 1].to_broadcast([P, P]))
                    ch.link(nc.gpsimd.tensor_copy(q2[s][:, :], qT[s][:, :]))
                    nc.gpsimd.tensor_tensor(q3[s][:, :], qT[s][:, :], q2[s][:, :].bitcast(F32), ALU.subtract).then_inc(q_split, 1)

            @block.tensor
            def _(pe):
                with pe.Fori(0, TURNS) as it:

                    def scores(i):
                        s, (kind, t, lo, k) = units[i]
                        if i % (n // 2) == 0:
                            pe.wait_ge(q_split, it * 2 + (s + 1))
                        if i >= 2:
                            pe.wait_ge(prob_ready, it * n + (i - 1))
                        dst = banks(2 * (i % 2), 2)
                        q = slice(t * P, (t + 1) * P)
                        width = NBP if kind == "cmp" else k * P
                        for c in range(0, width, 512):
                            w = min(512, width - c)
                            a, z = lo * P + c, lo * P + c + w
                            rhs = (kcP[:, it // 2, :] if kind == "cmp" else kTf[:, 2 * it + s, a:z] if kind == "fox" else
                                   kTs[:, it // 2, a:z] if kind == "slc" else kTw[:, it // 2, a:z])
                            nc.tensor.matmul(dst[:, c:c + w], q2[s][:, q], rhs, start=True, stop=False)
                            if kind == "win" and k == 5 and c == 0:
                                nc.tensor.matmul(dst[:, 0:P], eyer[:, :], maskr[:, P:2 * P], start=False, stop=False)
                            if c + w == width:
                                m = slice(2 * P + NBP * t, 2 * P + NBP * (t + 1)) if kind == "cmp" else slice(0, P)
                                nc.tensor.matmul(dst[:, width - (m.stop - m.start):width], eyer[:, :], maskr[:, m], start=False, stop=False)
                            if fox:
                                nc.tensor.matmul(dst[:, c:c + w], pick[s][:, :], b2[:, a:z], start=False, stop=False)
                            last = nc.tensor.matmul(dst[:, c:c + w], q3[s][:, q], rhs, start=False, stop=True)
                        last.then_inc(scores_ready, 1)

                    def transposes(i):
                        kind, _, _, k = units[i][1]
                        pe.wait_ge(prob_ready, it * n + (i + 1))
                        for hh in range(halves[i]):
                            g = h0[i] + hh
                            if g >= 2:
                                j, jj = owner[g - 2]
                                if jj == 0:
                                    pe.wait_ge(pt_act, it * n + (j + 1))
                                else:
                                    pe.wait_ge(pt_dve, it * d0[n] + d0[j + 1])
                            for j in range(4 * hh, min(k, 4 * hh + 4)):
                                w = NBP if kind == "cmp" else P
                                last = nc.tensor.transpose(bk[4 + g % 2][0:w, P * (j % 4):P * (j % 4 + 1)],
                                                           prob[i % 2][:, j * P:j * P + w], ident)
                            last.then_inc(pt_ready, 1)

                    def values(i):
                        s, (kind, t, lo, k) = units[i]
                        pe.wait_ge(pt_act, it * n + (i + 1))
                        if halves[i] == 2:
                            pe.wait_ge(pt_dve, it * d0[n] + d0[i + 1])
                        pe.wait_ge(o_norm, it * n + (max(i - 1, 0) + CREDIT))
                        dst = bk[6 + i % 2][:, 0:HD + 1]
                        for j in range(k):
                            v = (vcP[:, it // 2, :] if kind == "cmp" else Vf[:, lo + j, 2 * it + s, :] if kind == "fox" else
                                 Vs[:, lo + j, it // 2, :] if kind == "slc" else Vw[:, lo + j, it // 2, :])
                            last = nc.tensor.matmul(dst, probT[i % 2][:, j, :], v, start=(j == 0), stop=(j == k - 1))
                        last.then_inc(o_ready, 1)

                    scores(0)
                    for i in range(n):
                        if i + 1 < n:
                            scores(i + 1)
                        transposes(i)
                        if i:
                            values(i - 1)
                    values(n - 1)

            @block.scalar
            def _(act):
                act.wait_ge(q_ld[0], 32)
                nc.scalar.activation(q2[0][:, :], qT[0][:, :], ACT.Copy).then_inc(first_hi, 1)
                if fox:
                    act.wait_ge(probt_clear, 1)
                with act.Fori(0, TURNS) as it:

                    def exps(i):
                        s, (kind, t, lo, k) = units[i]
                        w = NBP if kind == "cmp" else k * P
                        act.wait_ge(max_ready, it * n + (i + 1))
                        nc.scalar.activation(prob[i % 2][:, 0:w], banks(2 * (i % 2), 2)[:, 0:w], ACT.Exp,
                                             bias=nmax[:, i % 2, 0:1]).then_inc(prob_ready, 1)

                    exps(0)
                    for i, (s, (kind, t, lo, k)) in enumerate(units):
                        if i + 1 < n:
                            exps(i + 1)
                        act.wait_ge(pt_ready, it * h0[n] + (h0[i] + 1))
                        m, r = min(k, 4), NBP if kind == "cmp" else P
                        nc.scalar.activation(probT[i % 2][0:r, 0:m, :],
                                             bk[4 + h0[i] % 2][0:r, 0:m * P].rearrange("p (j n) -> p j n", n=P),
                                             ACT.Copy).then_inc(pt_act, 1)

            @block.vector
            def _(dve):
                ch = Chain(dve, dve_s)
                nc.vector.nop().then_inc(o_norm, CREDIT)
                dve.wait_ge(first_hi, 1)
                nc.vector.tensor_tensor(q3[0][:, :], qT[0][:, :], q2[0][:, :].bitcast(F32), ALU.subtract).then_inc(first_lo, 1)
                if fox:
                    dve.wait_ge(probt_clear, 1)
                with dve.Fori(0, TURNS) as it:
                    ch.loop(it, steps)

                    def maximum(i):
                        s, (kind, t, lo, k) = units[i]
                        src = banks(2 * (i % 2), 2)
                        dve.wait_ge(scores_ready, it * n + (i + 1))
                        w = NBP if kind == "cmp" else k * P
                        nc.vector.tensor_reduce(nmax[:, i % 2, 0:1], src[:, 0:w], AX.X, ALU.max, negate=True).then_inc(max_ready, 1)

                    def second_half(i):
                        k = nk[i]
                        if halves[i] == 2:
                            dve.wait_ge(pt_ready, it * h0[n] + (h0[i] + 2))
                            nc.vector.tensor_copy(probT[i % 2][:, 4:k, :],
                                                  bk[4 + (h0[i] + 1) % 2][:, 0:(k - 4) * P].rearrange("p (j n) -> p j n", n=P)).then_inc(pt_dve, 1)

                    def output(i):
                        s, (kind, t, lo, k) = units[i]
                        dve.wait_ge(o_ready, it * n + (i + 1))
                        src, f = bk[6 + i % 2], gate_qk[:, i % 2, :]
                        ch.link(nc.vector.reciprocal(f[:, 0:1], src[:, HD:HD + 1]))
                        if kind == "fox":
                            nc.vector.tensor_scalar(mix[:, t, bass.ds(it * (2 * HD) + s * HD, HD)], src[:, 0:HD], f[:, 0:1], None, ALU.mult).then_inc(o_norm, 1)
                            return
                        br = {"cmp": 0, "slc": 1, "win": 2}[kind]
                        ch.link(nc.vector.tensor_tensor(f[:, 1:2], f[:, 0:1], gates[:, t, bass.ds(it * 2 + (br * NH + s), 1)], ALU.mult))
                        m = mix[:, t, bass.ds(it * (2 * HD) + (512 + s * HD), HD)]
                        if kind == "cmp":
                            nc.vector.tensor_scalar(m, src[:, 0:HD], f[:, 1:2], None, ALU.mult).then_inc(o_norm, 1)
                        else:
                            dve.wait_ge(o_norm, it * n + (i + CREDIT))
                            nc.vector.scalar_tensor_tensor(m, src[:, 0:HD], f[:, 1:2], m, ALU.mult, ALU.add).then_inc(o_norm, 1)

                    maximum(0)
                    for i in range(n):
                        if i + 1 < n:
                            maximum(i + 1)
                        second_half(i)
                        if i:
                            output(i - 1)
                    output(n - 1)
                    ch.end(TURNS)

    in_ld = [sem(f"sample_loaded{i}") for i in range(2)]
    g_ld = sem("sample_gates_loaded")
    v_ld = [sem(f"sample_values_loaded{i}") for i in range(2)]

    def load_pages_of(sp, b, s, part, done):
        for j in range(PAGES):
            page = sp.value_load(ptab[0:1, bass.ds(b * PAGES + j, 1)], min_val=0, max_val=n_pool - 1)
            f, x = slice(512 * part, 512 * (part + 1)), slice(P * part, P * (part + 1))
            sp.dma_start(fpage[s][:, j, f], cfox_v[page, :, f]).then_inc(done, 16)
            sp.dma_start(npage[s][:, j, x], cnsa_v[page, :, 256 + P * part:256 + P * (part + 1)]).then_inc(done, 16)
        sp.dma_start(wpage[s][:, :, x], stw_v[b, :, :, x]).then_inc(done, 16)

    prompt_attention("fox", 0, ("fox",))
    prompt_attention("nsa", 1, ("cmp", "slc", "win"))

    (e_set, lf_ready, p1_ready, q_bd, negc_done, kt_ready, kt_act, kt_dve, ks_ready, ks_done, sc_done, sc_act, m_ready,
     e_ready, p_ready, pt2_ready, pt2_act, pt2_dve, o2_ready, o2_done, o2_fox) = (sem(f"sample_{n}") for n in (
        "cleared", "logf_spread", "queries_transposed", "queries_placed", "bias_ready", "keys_transposed", "keys_act",
        "keys_dve", "new_keys_transposed", "new_keys_stored", "scores", "scores_act", "maxima", "exps", "probs",
        "probs_transposed", "probs_act", "probs_dve", "outputs", "outputs_copied", "outputs_fox"))
    os_st = [sem(f"sample_stored{i}") for i in range(2)]
    dve_e, pool_e = sem("dve_step_e"), sem("pool_step_e")
    nc.clear_and_free_semaphores(phase1_sems)
    N_LD, N_VLD = 9 + PAGES + 4 + 3, 9 + 3
    N_OS = 1
    TURNS2 = B // 2
    SAMPLE_STEPS = 2 * (3 + 2 + 3 + 1)

    with nc.Block() as block:

        @block.sync
        def _(sp):
            def load_keys(b, s, first=False):
                q0 = b * TQ
                load_new(q0, b, s, 0, in_ld[s])
                if not first:
                    load_pages_of(sp, b, s, 0, in_ld[s])
                for j in range(PAGES):
                    page = sp.value_load(ptab[0:1, bass.ds(b * PAGES + j, 1)], min_val=0, max_val=n_pool - 1)
                    sp.dma_start(lpage[s][:, j, :], clf_v[page, :, :]).then_inc(in_ld[s], 16)
                sp.dma_start(lnew[s][:, :], flfs_b[b, :, :]).then_inc(in_ld[s], 16)
                sp.dma_start(qrow[s][:, 0:512], qs_d[bass.ds(q0, TQ), 0:512]).then_inc(in_ld[s], 16)
                for g in range(G):
                    sp.dma_start(qrow[s][:, 512:1024].rearrange("q (n g d) -> q n g d", g=G, d=HD)[:, :, g, :],
                                 qs_d[bass.ds(q0, TQ), 512 + 256 * g:768 + 256 * g].rearrange("q (n d) -> q n d", d=HD)).then_inc(in_ld[s], 16)

            def load_values(b, s, first=False):
                load_new(b * TQ, b, s, 1, v_ld[s])
                if not first:
                    load_pages_of(sp, b, s, 1, v_ld[s])

            def load_new(q0, b, s, part, done):
                f, x = slice(512 * part, 512 * (part + 1)), slice(P * part, P * (part + 1))
                sp.dma_start(fnew[s][:, f], fkvs_v[bass.ds(q0, TQ), part, :]).then_inc(done, 16)
                sp.dma_start(nnew[s][:, x], nkvs_v[bass.ds(q0, TQ), 256 + P * part:256 + P * (part + 1)]).then_inc(done, 16)
                sp.dma_start(wnew[s][:, x], wins_v[b, PAST - TQ:PAST, x]).then_inc(done, 16)

            def store(b, s):
                sp.dma_start(mixs_d[b, :, :, :].rearrange("r p d -> p r d"), os2[s][:, :, :]).then_inc(os_st[s], 16)

            for s in range(2):
                sp.nop().then_inc(os_st[s], CREDIT)
                load_keys(s, s, first=True)
            for s in range(2):
                load_values(s, s, first=True)
            with sp.Fori(0, TURNS2 - 1) as it:
                for s in range(2):
                    sp.wait_ge(ks_ready, 2 * it + (s + 1))
                    load_keys(2 * it + (s + 2), s)
                for s in range(2):
                    sp.wait_ge(o2_ready, 2 * it + (s + 1))
                    load_values(2 * it + (s + 2), s)
                for s in range(2):
                    sp.wait_ge(o2_done, 2 * it + (s + 1 + CREDIT))
                    sp.wait_ge(o2_fox, 2 * it + (s + 1 + CREDIT))
                    store(2 * it + s, s)
            for s in range(2):
                sp.wait_ge(o2_done, B - 1 + s + CREDIT)
                sp.wait_ge(o2_fox, B - 1 + s + CREDIT)
                store(B - 2 + s, s)
            for s in range(2):
                sp.wait_ge(os_st[s], 16 * N_OS * TURNS2 + CREDIT)

        @block.gpsimd
        def _(pool):
            ch = Chain(pool, pool_e)
            for s in range(2):
                ch.link(nc.gpsimd.memset(Qf[s][:, :], 0.0))
                ch.link(nc.gpsimd.memset(Qn[s][:, :], 0.0))
            nc.gpsimd.memset(ones512[:, :], 1.0).then_inc(e_set, 1)

        @block.tensor
        def _(pe):
            def pages(dst, src):
                for j in range(PAGES):
                    last = nc.tensor.transpose(dst[:, j * P:(j + 1) * P], src(j), ident)
                return last

            def flip(dst, src, eye, after_wait):
                if after_wait:
                    nc.tensor.matmul(dst, src, eye, start=True, stop=True)
                else:
                    nc.tensor.transpose(dst, src, eye)

            with pe.Fori(0, TURNS2) as it:
                for s in range(2):
                    b0, b1, b2, b3 = bk[4 * s:4 * s + 4]
                    pe.wait_ge(in_ld[s], it * (16 * N_LD) + 16 * N_LD)
                    pe.wait_ge(lf_ready, 2 * it + (s + 1))
                    pe.wait_ge(o2_done, 2 * it + CREDIT)
                    pe.wait_ge(o2_fox, 2 * it + CREDIT)
                    for j in range(8):
                        flip(b0[:, 8 * j:8 * j + 8], qrow[s][:, j * P:(j + 1) * P], ident[0:TQ, 0:TQ], j == 0)
                    for j in range(PAGES):
                        nc.tensor.transpose(b1[0:HD, j * P:(j + 1) * P], lf64[s][:, j, :, :].rearrange("p h q -> p (h q)"), ident)
                    nc.tensor.transpose(b0[0:HD, 64:72], lf64[s][0:TQ, PAGES, :, :].rearrange("p h q -> p (h q)"),
                                        ident[0:TQ, 0:TQ]).then_inc(p1_ready, 1)
                for s in range(2):
                    b0, b1, b2, b3 = bk[4 * s:4 * s + 4]
                    for k in range(6):
                        if k == 2:
                            pe.wait_ge(negc_done, 2 * it + (s + 1))
                        if k == 3:
                            pe.wait_ge(kt_act, it * 6 + (3 * s + 1))
                        if k == 4:
                            pe.wait_ge(kt_dve, it * 6 + (3 * s + 1))
                        if k == 5:
                            pe.wait_ge(kt_act, it * 6 + (3 * s + 2))
                        src = (lambda j: fpage[s][:, j, k * P:(k + 1) * P]) if k < 4 else \
                              (lambda j: (npage if k == 4 else wpage)[s][:, j, 0:P])
                        pages((b2, b3, b1)[k % 3], src).then_inc(kt_ready, 1)
                    for j in range(4):
                        nc.tensor.transpose(b0[:, 128 + 8 * j:136 + 8 * j], fnew[s][:, j * P:(j + 1) * P], ident[0:TQ, 0:TQ])
                    nc.tensor.transpose(b0[:, 160:168], nnew[s][:, 0:P], ident[0:TQ, 0:TQ])
                    nc.tensor.transpose(b0[:, 168:176], wnew[s][:, 0:P], ident[0:TQ, 0:TQ]).then_inc(ks_ready, 1)
                for s in range(2):
                    b0, b1, b2, b3 = bk[4 * s:4 * s + 4]
                    pe.wait_ge(q_bd, 2 * it + (s + 1))
                    pe.wait_ge(kt_act, it * 6 + (3 * s + 3))
                    pe.wait_ge(kt_dve, it * 6 + (3 * s + 3))
                    pe.wait_ge(ks_done, 2 * it + (s + 1))
                    for dst, cols in ((b1[0:HD, 0:PAST], slice(0, PAST)), (b0[0:HD, 192:200], slice(PAST, L))):
                        for j in range(4):
                            nc.tensor.matmul(dst, Qf[s][:, HD * j:HD * (j + 1)], KTf[s][:, j, cols], start=(j == 0), stop=(j == 3))
                    for i, dst in enumerate((b2, b3)):
                        nc.tensor.matmul(dst[0:HD, 0:PAST], Qn[s][:, :], KTn[s][:, i, 0:PAST], start=True, stop=True)
                        nc.tensor.matmul(b0[0:HD, 200 + 8 * i:208 + 8 * i], Qn[s][:, :], KTn[s][:, i, PAST:L], start=True, stop=True)
                    nc.tensor.matmul(b0[0:HD, 216:224], Qn[s][:, :], kcS[:, bass.ds(it * (2 * NBS) + NBS * s, NBS)],
                                     start=True, stop=True).then_inc(sc_done, 1)
                for s in range(2):
                    b0, b1, b2, b3 = bk[4 * s:4 * s + 4]
                    pe.wait_ge(p_ready, 2 * it + (s + 1))
                    for br, dst in enumerate((b1, b2, b3)):
                        for j in range(PAGES):
                            flip(dst[:, HD * j:HD * (j + 1)], sc[s][:, br, j * P:(j + 1) * P], ident[0:HD, 0:HD], br == 0 and j == 0)
                        nc.tensor.transpose(b0[0:TQ, 256 + HD * br:320 + HD * br], sc[s][:, br, PAST:L], ident[0:HD, 0:HD])
                    nc.tensor.transpose(b0[0:NBS, 448:512], scc[s][:, :], ident[0:HD, 0:HD]).then_inc(pt2_ready, 1)
                for s in range(2):
                    b0, b1, b2, b3 = bk[4 * s:4 * s + 4]
                    pe.wait_ge(v_ld[s], it * (16 * N_VLD) + 16 * N_VLD)
                    pe.wait_ge(pt2_act, 2 * it + (s + 1))
                    pe.wait_ge(pt2_dve, 2 * it + (s + 1))
                    for j in range(PAGES):
                        nc.tensor.matmul(b1[0:HD, :], PTb[s][:, 0, j, :], fpage[s][:, j, 512:1024], start=(j == 0), stop=False)
                    nc.tensor.matmul(b1[0:HD, :], PTs[s][:, 0, :], fnew[s][:, 512:1024], start=False, stop=True)
                    dst = b2[0:HD, 0:P]
                    nc.tensor.matmul(dst, PTs[s][:, 3, :], vcb[s][:, :], start=True, stop=False)
                    for br, page, new in ((1, npage, nnew), (2, wpage, wnew)):
                        for j in range(PAGES):
                            nc.tensor.matmul(dst, PTb[s][:, br, j, :], page[s][:, j, P:2 * P], start=False, stop=False)
                        last = nc.tensor.matmul(dst, PTs[s][:, br, :], new[s][:, P:2 * P], start=False, stop=(br == 2))
                    last.then_inc(o2_ready, 1)

        @block.scalar
        def _(act):
            nc.scalar.nop().then_inc(o2_done, CREDIT)
            with act.Fori(0, TURNS2) as it:
                for s in range(2):
                    b0, b1, b2, b3 = bk[4 * s:4 * s + 4]
                    for k in (0, 2, 4):
                        act.wait_ge(kt_ready, it * 12 + (6 * s + k + 1))
                        dst = KTf[s][:, k, 0:PAST] if k < 4 else KTn[s][:, 0, 0:PAST]
                        nc.scalar.activation(dst, (b2, b3, b1)[k % 3], ACT.Copy).then_inc(kt_act, 1)
                    act.wait_ge(ks_ready, 2 * it + (s + 1))
                    nc.scalar.activation(KTf[s][:, :, PAST:L], b0[:, 128:160].rearrange("p (j n) -> p j n", j=4), ACT.Copy)
                    nc.scalar.activation(KTn[s][:, :, PAST:L], b0[:, 160:176].rearrange("p (j n) -> p j n", j=2), ACT.Copy).then_inc(ks_done, 1)
                for s in range(2):
                    b0, b1, b2, b3 = bk[4 * s:4 * s + 4]
                    act.wait_ge(sc_done, 2 * it + (s + 1))
                    nc.scalar.activation(sc[s][:, 1, 0:PAST], b2[0:HD, :], ACT.Copy)
                    nc.scalar.activation(sc[s][:, 2, 0:PAST], b3[0:HD, :], ACT.Copy).then_inc(sc_act, 1)
                for s in range(2):
                    act.wait_ge(m_ready, 2 * it + (s + 1))
                    for br in range(4):
                        x = sc[s][:, br, :] if br < 3 else scc[s][:, :]
                        ins = nc.scalar.activation(x, x, ACT.Exp, bias=srow[s][:, 0, br:br + 1], accum_out=srow[s][:, 1, br:br + 1])
                    ins.then_inc(e_ready, 1)
                for s in range(2):
                    b0, b1, b2, b3 = bk[4 * s:4 * s + 4]
                    act.wait_ge(pt2_ready, 2 * it + (s + 1))
                    nc.scalar.activation(PTb[s][:, 1, :, :], b2[:, 0:256].rearrange("p (j n) -> p j n", n=HD), ACT.Copy)
                    nc.scalar.activation(PTb[s][:, 2, :, :], b3[:, 0:256].rearrange("p (j n) -> p j n", n=HD), ACT.Copy).then_inc(pt2_act, 1)
                for s in range(2):
                    b0, b1, b2, b3 = bk[4 * s:4 * s + 4]
                    act.wait_ge(o2_ready, 2 * it + (s + 1))
                    act.wait_ge(os_st[s], it * (16 * N_OS) + CREDIT)
                    nc.scalar.activation(os2[s][0:32, 1, :], b2[0:32, 0:HD], ACT.Copy)
                    nc.scalar.activation(os2[s][32:HD, 1, :], b2[32:HD, HD:P], ACT.Copy).then_inc(o2_done, 1)

        @block.vector
        def _(dve):
            ch = Chain(dve, dve_e)
            dve.wait_ge(e_set, 1)
            dve.wait_ge(g_ld, 16 * NH * 3)
            nc.vector.nop().then_inc(o2_fox, CREDIT)
            with dve.Fori(0, TURNS2) as it:
                ch.loop(it, SAMPLE_STEPS)
                for s in range(2):
                    dve.wait_ge(in_ld[s], it * (16 * N_LD) + 16 * N_LD)
                    nc.vector.tensor_copy(vcb[s][:, :], vcS[:, it * 2 + s, :])
                    nc.vector.tensor_copy(lf64[s][:, 0:PAGES, :, :].rearrange("p j h q -> p (j h) q"),
                                          lpage[s][:, :, :].rearrange("p j h -> p (j h)").unsqueeze(2).to_broadcast([P, PAGES * NH, TQ]))
                    nc.vector.tensor_copy(lf64[s][0:TQ, PAGES, :, :], lnew[s][:, :].unsqueeze(2).to_broadcast([TQ, NH, TQ])).then_inc(lf_ready, 1)
                for s in range(2):
                    b0, b1, b2, b3 = bk[4 * s:4 * s + 4]
                    dve.wait_ge(p1_ready, 2 * it + (s + 1))
                    q4 = Qf[s][:, :].rearrange("p (j c) -> p j c", c=80)
                    f4 = b0[:, 0:32].rearrange("p (j q) -> p j q", j=4)
                    nc.vector.tensor_copy(q4[0:HD, :, 0:8], f4[0:HD, :, :])
                    nc.vector.tensor_copy(q4[HD:P, :, 8:16], f4[HD:P, :, :])
                    nc.vector.tensor_copy(Qn[s][0:HD, 0:32], b0[0:HD, 32:64])
                    nc.vector.tensor_copy(Qn[s][HD:P, 32:64], b0[HD:P, 32:64]).then_inc(q_bd, 1)
                    ch.link(nc.vector.tensor_tensor_scan(negc[s][:, 0:PAST], ones512[:, :], b1[0:HD, :], 0.0, ALU.mult, ALU.add))
                    ch.link(nc.vector.tensor_tensor_scan(negc[s][:, PAST:L], ones512[:, 0:TQ], b0[0:HD, 64:72],
                                                         negc[s][:, PAST - 1:PAST], ALU.mult, ALU.add))
                    ch.link(nc.vector.tensor_scalar(negc[s][:, :], negc[s][:, :], -1.0, None, ALU.mult))
                    nc.vector.tensor_tensor(negc[s][:, PAST:L], negc[s][:, PAST:L], cst[0:HD, K_NEW:K_NEW + TQ], ALU.add).then_inc(negc_done, 1)
                for s in range(2):
                    b0, b1, b2, b3 = bk[4 * s:4 * s + 4]
                    for k in (1, 3, 5):
                        dve.wait_ge(kt_ready, it * 12 + (6 * s + k + 1))
                        dst = KTf[s][:, k, 0:PAST] if k < 4 else KTn[s][:, 1, 0:PAST]
                        nc.vector.tensor_copy(dst, (b2, b3, b1)[k % 3]).then_inc(kt_dve, 1)
                for s in range(2):
                    b0, b1, b2, b3 = bk[4 * s:4 * s + 4]
                    dve.wait_ge(sc_done, 2 * it + (s + 1))
                    dve.wait_ge(negc_done, 2 * it + (s + 1))
                    new = cst[0:HD, K_NEW:K_NEW + TQ].unsqueeze(1).to_broadcast([HD, 2, TQ])
                    nc.vector.tensor_tensor(sc[s][:, 0, 0:PAST], b1[0:HD, :], negc[s][:, 0:PAST], ALU.add)
                    nc.vector.tensor_tensor(sc[s][:, 0, PAST:L], b0[0:HD, 192:200], negc[s][:, PAST:L], ALU.add)
                    nc.vector.tensor_tensor(sc[s][:, 1:3, PAST:L], b0[0:HD, 200:216].rearrange("p (i n) -> p i n", i=2), new, ALU.add)
                    ch.link(nc.vector.tensor_copy(scc[s][:, :], b0[0:HD, 216:224]))
                    dve.wait_ge(sc_act, 2 * it + (s + 1))
                    ch.link(nc.vector.tensor_tensor(sc[s][:, 2, 0:TQ], sc[s][:, 2, 0:TQ], cst[0:HD, K_OLD:K_OLD + TQ], ALU.add))
                    nc.vector.tensor_reduce(srow[s][:, 0, 0:3], sc[s][:, :, :], AX.X, ALU.max, negate=True)
                    nc.vector.tensor_reduce(srow[s][:, 0, 3:4], scc[s][:, :], AX.X, ALU.max, negate=True).then_inc(m_ready, 1)
                for s in range(2):
                    dve.wait_ge(e_ready, 2 * it + (s + 1))
                    ch.link(nc.vector.reciprocal(srow[s][:, 2, :], srow[s][:, 1, :]))
                    w, g = srow[s][:, 2, :], gateS[:, :, bass.ds(it * 2 + s, 1)].rearrange("p r o -> p (r o)")
                    ch.link(nc.vector.tensor_tensor(w[:, 1:3], w[:, 1:3], g[:, 1:3], ALU.mult))
                    ch.link(nc.vector.tensor_tensor(w[:, 3:4], w[:, 3:4], g[:, 0:1], ALU.mult))
                    for br in range(4):
                        x = sc[s][:, br, :] if br < 3 else scc[s][:, :]
                        ins = nc.vector.tensor_scalar(x, x, w[:, br:br + 1], None, ALU.mult)
                    ins.then_inc(p_ready, 1)
                for s in range(2):
                    b0, b1, b2, b3 = bk[4 * s:4 * s + 4]
                    dve.wait_ge(pt2_ready, 2 * it + (s + 1))
                    nc.vector.tensor_copy(PTb[s][:, 0, :, :], b1[:, 0:256].rearrange("p (j n) -> p j n", n=HD))
                    nc.vector.tensor_copy(PTs[s][:, :, :], b0[0:TQ, 256:512].rearrange("p (j n) -> p j n", n=HD)).then_inc(pt2_dve, 1)
                for s in range(2):
                    b1 = bk[4 * s + 1]
                    dve.wait_ge(o2_ready, 2 * it + (s + 1))
                    dve.wait_ge(os_st[s], it * (16 * N_OS) + CREDIT)
                    one = cst[0:HD, K_HEAD:K_HEAD + NH].unsqueeze(2).to_broadcast([HD, NH, HD])
                    ch.link(nc.vector.tensor_tensor(odiag[s][:, :, :], b1[0:HD, :].rearrange("p (h d) -> p h d", h=NH), one, ALU.mult))
                    nc.vector.tensor_reduce(os2[s][:, 0, :], odiag[s][:, :, :].rearrange("p h d -> p d h"), AX.X, ALU.add).then_inc(o2_fox, 1)
                ch.end(TURNS2)

    w_ld = [sem(f"weights_loaded{i}") for i in range(2)]
    wo_ld, mx_ld, f_misc, gt_ready, gt_done, gb_ready, gb_done = (sem(n) for n in (
        "wout_loaded", "sample_mix_loaded", "gain2_ready", "gt1_transposed", "gt1_copied", "gt1_spread", "gt1b_ready"))
    x_ld = [sem(f"x_tile_loaded{i}") for i in range(2)]
    x1_st = [sem(f"x1_stored{i}") for i in range(2)]
    (mt_ready, mt_act, mt_dve, out_ready, x1_ready, sq2, var2, root2, rstd2, xn2, xt_ready, h2_act, h2_dve) = (sem(f"f_{n}") for n in (
        "mix_transposed", "mix_act", "mix_dve", "projected", "x1_ready", "squares", "variance", "root", "rstd", "xn_ready",
        "xn_transposed", "h_act", "h_dve"))
    h_hi, h_lo, h_pad = sem("h_hi"), sem("h_lo"), sem("h_pad_zero")
    dve_f = sem("dve_step_f")
    def load_weights(sp, r, i):
        dst = wraw[i % 2]
        if i < UC:
            sp.dma_start(dst.rearrange("p (k n) -> p k n", k=KC), wup_v[:, :, bass.ds(r * (UC * P) + P * i, P)]).then_inc(w_ld[i % 2], 16)
        else:
            sp.dma_start(dst.rearrange("p (f n) -> p f n", f=UC),
                         wdn_v[:, bass.ds(r * UC, UC), 2 * P * (i - UC):2 * P * (i - UC + 1)]).then_inc(w_ld[i % 2], 16)

    x1_tiles = [(x1_d[t * P:t * P + rows(t), :]) for t in range(T9)]

    with nc.Block() as block:

        @block.sync
        def _(sp):
            for k in range(2):
                sp.dma_start(wo[:, 4 * k:4 * k + 4, :], wout_v[:, 4 * k:4 * k + 4, :]).then_inc(wo_ld, 16)
            for b in range(B):
                sp.dma_start(mix[b * TQ:(b + 1) * TQ, NT, :].rearrange("q (r d) -> q r d", d=HD),
                             mixs_d[b, :, :, :].rearrange("r (h q) d -> q (r h) d", q=TQ)).then_inc(mx_ld, 16)
            for t in range(T9 + 1):
                if t < T9:
                    if t >= 2:
                        sp.wait_ge(x1_ready, t - 1)
                    src = xs_v if t == NT else xp_v[:, t, :]
                    sp.dma_start(xt[t % 2][0:rows(t), :], src).then_inc(x_ld[t % 2], 16)
                if t == 6:
                    sp.wait_ge(mt_ready, 2)
                    for i in range(2):
                        load_weights(sp, 0, i)
                if t:
                    sp.wait_ge(x1_ready, t)
                    sp.dma_start(x1_tiles[t - 1], x1[(t - 1) % 2][0:rows(t - 1), :]).then_inc(x1_st[(t - 1) % 2], 16)
            sp.wait_ge(x1_st[0], 16 * 5)
            sp.wait_ge(x1_st[1], 16 * 4)

        @block.tensor
        def _(pe):
            for k in range(KC):
                last = nc.tensor.transpose(bk[k // 4][0:B + 1, P * (k % 4):P * (k % 4 + 1)], modT[:, 16 + k, :], ident)
            last.then_inc(gt_ready, 1)
            pe.wait_ge(gt_done, 1)
            for i, (col, r) in enumerate(((K_SELP, P), (K_SELS, NS))):
                for c in range(2):
                    last = nc.tensor.matmul(bk[2 + 2 * i + c][0:r, :], cst[0:B + 1, col:col + r], gt1n[:, 512 * c:512 * (c + 1)],
                                            start=True, stop=True)
            last.then_inc(gb_ready, 1)

            def mix_t(t):
                r = rows(t)
                if t:
                    pe.wait_ge(mt_act, t)
                    pe.wait_ge(mt_dve, t)
                if t == NT:
                    pe.wait_ge(mx_ld, 16 * B)
                for k in range(KC):
                    last = nc.tensor.transpose(bk[k // 4][:, P * (k % 4):P * (k % 4) + r], mix[0:r, t, k * P:(k + 1) * P], ident[0:r, 0:r])
                last.then_inc(mt_ready, 1)

            def xn_t(t):
                r = rows(t)
                pe.wait_ge(xn2, t + 1)
                if t:
                    pe.wait_ge(h2_act, t)
                    pe.wait_ge(h2_dve, t)
                for k in range(KC):
                    last = nc.tensor.transpose(bk[6 + k // 4][:, P * (k % 4):P * (k % 4) + r], xn[t % 2][0:r, k * P:(k + 1) * P], ident[0:r, 0:r])
                last.then_inc(xt_ready, 1)

            mix_t(0)
            pe.wait_ge(gb_done, 1)
            pe.wait_ge(wo_ld, 32)
            for t in range(T9):
                r = rows(t)
                if t + 1 < T9:
                    mix_t(t + 1)
                else:
                    pe.wait_ge(mt_act, T9)
                    pe.wait_ge(mt_dve, T9)
                if t >= 2:
                    pe.wait_ge(x1_ready, t - 1)
                for c in range(2):
                    for k in range(KC):
                        last = nc.tensor.matmul(bk[2 + 2 * (t % 2) + c][0:r, :], mixT[t % 2][:, k, 0:r], wo[:, k, 512 * c:512 * (c + 1)],
                                                start=(k == 0), stop=(k == KC - 1))
                last.then_inc(out_ready, 1)
                if t:
                    xn_t(t - 1)
            xn_t(T9 - 1)

        @block.scalar
        def _(act):
            def mix_copy(t):
                r = rows(t)
                act.wait_ge(mt_ready, t + 1)
                nc.scalar.activation(mixT[t % 2][:, 0:4, 0:r], bk[0].rearrange("p (k n) -> p k n", k=4)[:, :, 0:r], ACT.Copy).then_inc(mt_act, 1)

            def h_copy(t):
                act.wait_ge(xt_ready, t + 1)
                act.wait_ge(f_misc, 1)
                if t >= 2:
                    act.wait_ge(h_lo, t - 1)
                if t == NT:
                    return
                for k in range(4):
                    last = nc.scalar.activation(h2s[t % 2][:, k, :], bk[6][:, P * k:P * (k + 1)], ACT.Identity,
                                                bias=modT[:, 24 + k, 0:1], scale=gain2[:, k, 0:1])
                last.then_inc(h2_act, 1)

            def h_split(t):
                act.wait_ge(h2_act, min(t + 1, NT))
                act.wait_ge(h2_dve, t + 1)
                nc.scalar.activation(h2hi[:, :, t * P:t * P + rows(t)], h2s[t % 2][:, :, 0:rows(t)], ACT.Copy).then_inc(h_hi, 1)

            mix_copy(0)
            for t in range(T9):
                r = rows(t)
                if t + 1 < T9:
                    mix_copy(t + 1)
                act.wait_ge(x1_ready, t + 1)
                if t:
                    act.wait_ge(sq2, t)
                nc.scalar.activation(junk2[0:r, :], x1[t % 2][0:r, :], ACT.Square, accum_out=ssum[0:r, t:t + 1]).then_inc(sq2, 1)
                act.wait_ge(var2, t + 1)
                nc.scalar.activation(rstd[0:r, t:t + 1], ssum[0:r, t:t + 1], ACT.Sqrt).then_inc(root2, 1)
                act.wait_ge(rstd2, t + 1)
                if t >= 2:
                    act.wait_ge(xt_ready, t - 1)
                nc.scalar.activation(xn[t % 2][0:r, :], x1[t % 2][0:r, :], ACT.Copy, scale=rstd[0:r, t:t + 1]).then_inc(xn2, 1)
                if t:
                    h_copy(t - 1)
                    h_split(t - 1)
            h_copy(NT)
            h_split(NT)

        @block.gpsimd
        def _(pool):
            for h in (h2hi, h2lo):
                nc.gpsimd.memset(h[:, :, TOK:TP].bitcast(F32), 0.0).then_inc(h_pad, 1)
            pool.wait_ge(h_pad, 2)

        @block.vector
        def _(dve):
            ch = Chain(dve, dve_f)
            nc.vector.scalar_tensor_tensor(gain2[:, :, :], modT[:, 32:40, :], 1.0,
                                           vecT[:, 56:64].unsqueeze(2).to_broadcast([P, KC, B + 1]), ALU.add, ALU.mult).then_inc(f_misc, 1)
            dve.wait_ge(gt_ready, 1)
            nc.vector.tensor_copy(gt1n[:, :], banks(0, 2)[0:B + 1, :]).then_inc(gt_done, 1)
            dve.wait_ge(gb_ready, 1)
            nc.vector.tensor_copy(gt1b[:, 0, :], banks(2, 2))
            ch.link(nc.vector.tensor_copy(gt1b[0:NS, 1, :], banks(4, 2)[0:NS, :]))
            nc.vector.nop().then_inc(gb_done, 1)

            def mix_copy(t):
                r = rows(t)
                dve.wait_ge(mt_ready, t + 1)
                nc.vector.tensor_copy(mixT[t % 2][:, 4:8, 0:r], bk[1].rearrange("p (k n) -> p k n", k=4)[:, :, 0:r]).then_inc(mt_dve, 1)

            def h_copy(t):
                dve.wait_ge(xt_ready, t + 1)
                dve.wait_ge(f_misc, 1)
                if t >= 2:
                    dve.wait_ge(h_lo, t - 1)
                if t < NT:
                    for k in range(4, 8):
                        last = nc.vector.tensor_scalar(h2s[t % 2][:, k, :], bk[7][:, P * (k - 4):P * (k - 3)],
                                                       gain2[:, k, 0:1], modT[:, 24 + k, 0:1], ALU.mult, ALU.add)
                    last.then_inc(h2_dve, 1)
                    return
                hs = h2s[NT % 2][:, :, 0:NS].rearrange("p k (b t) -> p k b t", b=B)
                src = banks(6, 2).rearrange("p (k n) -> p k n", n=P)[:, :, 0:NS].rearrange("p k (b t) -> p k b t", b=B)
                ch.link(nc.vector.tensor_tensor(hs, src, gain2[:, :, 1:B + 1].unsqueeze(3).to_broadcast([P, KC, B, TQ]), ALU.mult))
                nc.vector.tensor_tensor(hs, hs, modT[:, 24:32, 1:B + 1].unsqueeze(3).to_broadcast([P, KC, B, TQ]), ALU.add).then_inc(h2_dve, 1)

            def h_split(t):
                dve.wait_ge(h_hi, t + 1)
                tok = slice(t * P, t * P + rows(t))
                nc.vector.tensor_tensor(h2lo[:, :, tok], h2s[t % 2][:, :, 0:rows(t)], h2hi[:, :, tok].bitcast(F32), ALU.subtract).then_inc(h_lo, 1)

            mix_copy(0)
            for t in range(T9):
                r = rows(t)
                if t + 1 < T9:
                    mix_copy(t + 1)
                dve.wait_ge(out_ready, t + 1)
                dve.wait_ge(x_ld[t % 2], 16 * (t // 2 + 1))
                if t >= 2:
                    dve.wait_ge(x1_st[t % 2], 16 * (t // 2))
                    dve.wait_ge(xn2, t - 1)
                ch.link(nc.vector.tensor_tensor(x1[t % 2][0:r, :], banks(2 + 2 * (t % 2), 2)[0:r, :], gt1b[0:r, int(t == NT), :], ALU.mult))
                nc.vector.tensor_tensor(x1[t % 2][0:r, :], x1[t % 2][0:r, :], xt[t % 2][0:r, :], ALU.add).then_inc(x1_ready, 1)
                dve.wait_ge(sq2, t + 1)
                nc.vector.tensor_scalar(ssum[0:r, t:t + 1], ssum[0:r, t:t + 1], 1.0 / D, EPS, ALU.mult, ALU.add).then_inc(var2, 1)
                dve.wait_ge(root2, t + 1)
                nc.vector.reciprocal(rstd[0:r, t:t + 1], rstd[0:r, t:t + 1]).then_inc(rstd2, 1)
                if t:
                    h_copy(t - 1)
                    h_split(t - 1)
            h_copy(NT)
            h_split(NT)

    ROUNDS, LOADS, JOBS = FC // UC, 8, UC + KC
    BANKS_FREE, DOWN_FREE, U_FREE = JOBS, 3, 2
    GRP = 364
    xo_ld = [sem(f"x1_reloaded{i}") for i in range(3)]
    yo_st = [sem(f"y_stored{i}") for i in range(3)]
    (w_hi, w_lo, up_ready, dn_ready, banks_read, u_relu, u_hi, u_lo, y_zero, y_gated, y_gated_s, yt_ready, yo_ready) = (sem(n) for n in (
        "weights_hi", "weights_lo", "up_ready", "down_ready", "banks_read", "u_relu", "u_hi", "u_lo", "y_zeroed", "y_gated", "y_gated_sample",
        "y_transposed", "y_added"))
    y_tiles = [ys_v if t == NT else yp_v[:, t, :] for t in range(T9)]

    def groups(ap):
        return ap.rearrange("p (g n) -> p g n", g=3)

    with nc.Block() as block:

        @block.sync
        def _(sp):
            with sp.Fori(0, ROUNDS - 1) as r:
                for i in range(LOADS):
                    sp.wait_ge(w_lo, r * LOADS + (i + 1))
                    load_weights(sp, r + (i + 2) // LOADS, (i + 2) % LOADS)
            for i in range(LOADS - 2):
                sp.wait_ge(w_lo, (ROUNDS - 1) * LOADS + i + 1)
                load_weights(sp, ROUNDS - 1, i + 2)
            for t in range(T9 + 2):
                if t >= 2:
                    sp.wait_ge(yo_ready, t - 1)
                    sp.dma_start(y_tiles[t - 2], xo[(t - 2) % 3][0:rows(t - 2), :]).then_inc(yo_st[(t - 2) % 3], 16)
                if t < T9:
                    if t >= 3:
                        sp.wait_ge(yo_st[t % 3], 16 * (t // 3))
                    sp.dma_start(xo[t % 3][0:rows(t), :], x1_tiles[t]).then_inc(xo_ld[t % 3], 16)
            for i in range(3):
                sp.wait_ge(yo_st[i], 16 * 3)

        @block.tensor
        def _(pe):
            def product(ps, hi_w, lo_w, hi_x, lo_x, first, final):
                for n, (w, x) in enumerate(((hi_w, hi_x), (hi_w, lo_x), (lo_w, hi_x))):
                    for g in range(3):
                        last = nc.tensor.matmul(bk[ps + g][:, 0:GRP], w, x[:, GRP * g:GRP * (g + 1)],
                                                start=(first and n == 0), stop=(final and n == 2))
                return last

            def round_(r):
                for i in range(LOADS):
                    pe.wait_ge(w_lo, r * LOADS + (i + 1))
                    s = i % 2
                    for j in ([i] if i < UC else [2 * i - UC, 2 * i - UC + 1]):
                        pe.wait_ge(banks_read, r * JOBS + (j - 1 + BANKS_FREE))
                        for k in range(KC if i < UC else UC):
                            if i < UC:
                                w = slice(P * k, P * (k + 1))
                                x = h2hi[:, k, :], h2lo[:, k, :]
                            else:
                                if j == UC:
                                    pe.wait_ge(u_lo, r * UC + (k + 1 + U_FREE))
                                w = slice(2 * P * k + P * (j % 2), 2 * P * k + P * (j % 2 + 1))
                                x = u2hi[:, k, :], u2lo[:, k, :]
                            last = product(3 * (j % 2), whi[s][:, w], wlo[s][:, w], x[0], x[1], k == 0, k == (KC if i < UC else UC) - 1)
                        last.then_inc(up_ready if i < UC else dn_ready, 1)

            pe.wait_ge(h_pad, 2)
            with pe.Fori(0, ROUNDS - 1) as r:
                round_(r)
            round_(ROUNDS - 1)
            pe.wait_ge(y_gated, KC)
            pe.wait_ge(y_gated_s, 1)
            for t in range(T9):
                pe.wait_ge(banks_read, BANKS_FREE + ROUNDS * JOBS)
                if t >= 4:
                    pe.wait_ge(yo_ready, t - 3)
                for m in range(KC):
                    last = nc.tensor.transpose(bk[2 * (t % 4) + m // 4][0:rows(t), P * (m % 4):P * (m % 4 + 1)],
                                               yT[:, m, t * P:t * P + rows(t)], ident)
                last.then_inc(yt_ready, 1)

        @block.scalar
        def _(act):
            def weights(r, i):
                act.wait_ge(w_ld[i % 2], r * (16 * LOADS // 2) + 16 * (i // 2 + 1))
                if i in (0, 1):
                    act.wait_ge(dn_ready, r * KC + (2 * (i - 1) + DOWN_FREE))
                elif i - 2 < UC:
                    act.wait_ge(up_ready, r * UC + (i - 1))
                else:
                    act.wait_ge(dn_ready, r * KC + (2 * (i - 2 - UC + 1) + DOWN_FREE))
                nc.scalar.activation(whi[i % 2][:, :], wraw[i % 2][:, :], ACT.Copy).then_inc(w_hi, 1)

            def round_(r, final=False):
                for i in range(LOADS):
                    if not (final and i == LOADS - 1):
                        weights(r + (i + 1) // LOADS, (i + 1) % LOADS)
                    if i < UC:
                        act.wait_ge(up_ready, r * UC + (i + 1))
                        act.wait_ge(u_lo, r * UC + (i - 1 + U_FREE))
                        nc.scalar.activation(groups(us[i % 2][:, :]), bank[:, 3 * (i % 2):3 * (i % 2) + 3, 0:GRP], ACT.Relu).then_inc(u_relu, 1)
                        act.wait_ge(banks_read, r * JOBS + (i + 1 + BANKS_FREE))
                        nc.scalar.activation(u2hi[:, i, :], us[i % 2][:, :], ACT.Copy).then_inc(u_hi, 1)

            nc.scalar.nop().then_inc(dn_ready, DOWN_FREE)
            weights(0, 0)
            with act.Fori(0, ROUNDS - 1) as r:
                round_(r)
            round_(ROUNDS - 1, True)
            for m in range(KC):
                act.wait_ge(banks_read, BANKS_FREE + ROUNDS * JOBS - KC + m + 1)
                nc.scalar.activation(yT[:, m, 0:S], yT[:, m, 0:S], ACT.Copy, scale=modT[:, 40 + m, 0:1]).then_inc(y_gated, 1)

        @block.gpsimd
        def _(pool):
            nc.gpsimd.memset(yT[:, :, :], 0.0).then_inc(y_zero, 1)

        @block.vector
        def _(dve):
            def weights(r, i):
                dve.wait_ge(w_hi, r * LOADS + (i + 1))
                nc.vector.tensor_tensor(wlo[i % 2][:, :], wraw[i % 2][:, :], whi[i % 2][:, :].bitcast(F32), ALU.subtract).then_inc(w_lo, 1)

            def round_(r, final=False):
                for i in range(LOADS):
                    if not (final and i == LOADS - 1):
                        weights(r + (i + 1) // LOADS, (i + 1) % LOADS)
                    if i < UC:
                        dve.wait_ge(u_relu, r * UC + (i + 1))
                        u = us[i % 2][:, :]
                        nc.vector.tensor_tensor(u, u, u, ALU.mult).then_inc(banks_read, 1)
                        dve.wait_ge(u_hi, r * UC + (i + 1))
                        nc.vector.tensor_tensor(u2lo[:, i, :], us[i % 2][:, :], u2hi[:, i, :].bitcast(F32), ALU.subtract).then_inc(u_lo, 1)
                        continue
                    dve.wait_ge(y_zero, 1)
                    for m in (2 * (i - UC), 2 * (i - UC) + 1):
                        dve.wait_ge(dn_ready, r * KC + (m + 1 + DOWN_FREE))
                        dve.wait_ge(banks_read, r * JOBS + (m + 1 + UC - JOBS + BANKS_FREE))
                        y = groups(yT[:, m, :])
                        nc.vector.tensor_tensor(y, bank[:, 3 * (m % 2):3 * (m % 2) + 3, 0:GRP], y, ALU.add).then_inc(banks_read, 1)

            nc.vector.nop().then_inc(banks_read, BANKS_FREE)
            nc.vector.nop().then_inc(u_lo, U_FREE)
            weights(0, 0)
            with dve.Fori(0, ROUNDS - 1) as r:
                round_(r)
            round_(ROUNDS - 1, True)
            dve.wait_ge(banks_read, BANKS_FREE + ROUNDS * JOBS)
            ysm = yT[:, :, S:TOK].rearrange("p m (b t) -> p m b t", b=B)
            nc.vector.tensor_tensor(ysm, ysm, modT[:, 40:48, 1:B + 1].unsqueeze(3).to_broadcast([P, KC, B, TQ]), ALU.mult).then_inc(y_gated_s, 1)
            for t in range(T9):
                dve.wait_ge(yt_ready, t + 1)
                dve.wait_ge(xo_ld[t % 3], 16 * (t // 3 + 1))
                nc.vector.tensor_tensor(xo[t % 3][0:rows(t), :], banks(2 * (t % 4), 2)[0:rows(t), :], xo[t % 3][0:rows(t), :], ALU.add).then_inc(yo_ready, 1)


_INS = ['x_prompt', 'x_sample', 'c_prompt', 'c_sample', 'cache_fox_kv', 'cache_fox_logf', 'cache_nsa_kv',
        'state_nsa_win', 'page_table', 'w_ada', 'b_ada', 'norm1_g', 'norm2_g', 'w_in', 'b_forget', 'b_gate',
        'g_q_fox', 'g_k_fox', 'g_q_nsa', 'g_k_nsa', 'pe_cmp', 'w_cmp', 'w_out', 'w_up', 'w_down']
_OUTS = [((1, S, D), 'float32'), ((B, TQ, D), 'float32'),
         ((1, 1, S, 2, NH, HD), 'float32'), ((1, B, TQ, 2, NH, HD), 'float32'),
         ((1, 1, S, NH), 'float32'), ((1, B, TQ, NH), 'float32'),
         ((1, 1, S, 4, G, HD), 'float32'), ((1, B, TQ, 4, G, HD), 'float32'),
         ((1, 1, 512, 2, G, HD), 'float32'), ((1, B, PAST, 2, G, HD), 'float32')]


def kernel(**inputs):
    import numpy as _np
    import concourse.bacc as _bacc
    from concourse import mybir as _mybir
    from concourse.bass_utils import run_bass_kernel_spmd as _run

    nc = _bacc.Bacc("TRN2", target_bir_lowering=False, num_devices=1)
    arrays, args = {}, []
    for name in _INS + ['constants']:
        a = constants() if name == 'constants' else _np.ascontiguousarray(inputs[name])
        arrays[f"in_{name}_dram"] = a
        args.append(nc.dram_tensor(f"in_{name}_dram", a.shape, _mybir.dt.from_np(a.dtype), kind="ExternalInput").ap())
    for i, (shape, dtype) in enumerate(_OUTS):
        dt = _mybir.dt.from_np(_np.dtype(dtype))
        args.append(nc.dram_tensor(f"out_{i}_dram", shape, dt, kind="ExternalOutput").ap())
    layer_kernel(nc, *args)
    r = _run(nc, [arrays], core_ids=[0])
    return tuple(r.results[0][f"out_{i}_dram"] for i in range(len(_OUTS)))
```
